# Optimizing a Trainium2 kernel written in Bass

```python
import math
import jax, jax.numpy as jnp
from jax import lax
import numpy as np
import jax
import jax.numpy as jnp

D_MODEL = 1024
BATCH = 1
SEQ = 256
DEPTH = 1

MEM_LEN = 256
MEM_HEADS = 4
MEM_HEAD_DIM = D_MODEL // MEM_HEADS
A_HEADS = 8
A_HEAD_DIM = 64
A_WIDTH = A_HEADS * A_HEAD_DIM
MOBA_BLOCK = 256
MOBA_TOPK = 3
B_HEADS = 4
B_QK_DIM = 64
B_V_DIM = 2 * B_QK_DIM
B_QK_WIDTH = B_HEADS * 2 * B_QK_DIM
B_WIDTH = B_HEADS * B_V_DIM
MIX_WIDTH = A_WIDTH + B_WIDTH
IN_WIDTH = 3 * A_WIDTH + 2 * B_QK_WIDTH + B_WIDTH
IN_SPLITS = [A_WIDTH, 2 * A_WIDTH, 3 * A_WIDTH, 3 * A_WIDTH + B_QK_WIDTH, 3 * A_WIDTH + 2 * B_QK_WIDTH]
N_ATT_HEADS = A_HEADS + B_HEADS
REL_BUCKETS = 32
REL_MAX_DIST = 128
D_FF = -(-8 * D_MODEL // (3 * 256)) * 256
Q_BLOCK = 128
EPS = 1e-6
NEG_INF = -1e30


def rms_norm(x, g):
    xf = x.astype(jnp.float32)
    y = xf * lax.rsqrt(jnp.mean(xf * xf, axis=-1, keepdims=True) + EPS)
    return (y * g.astype(jnp.float32)).astype(x.dtype)

def rel_bucket(dist):
    n = jnp.maximum(dist, 0)
    max_exact = REL_BUCKETS // 2
    log_ratio = jnp.log(jnp.maximum(n, max_exact).astype(jnp.float32) / max_exact) / math.log(REL_MAX_DIST / max_exact)
    large = max_exact + (log_ratio * (REL_BUCKETS - max_exact)).astype(jnp.int32)
    large = jnp.minimum(large, REL_BUCKETS - 1)
    return jnp.where(n < max_exact, n, large)

def moba_attention(q, k, v, table_a):
    B_, S, H, dh = q.shape
    nb = -(-S // MOBA_BLOCK)
    pad = nb * MOBA_BLOCK - S
    topk = min(MOBA_TOPK, nb)
    n_chunks = S // Q_BLOCK
    scale = dh ** -0.5
    bias_ht = table_a.T.astype(jnp.float32)
    h_i = jnp.arange(H)[:, None, None]
    blk_ids = jnp.arange(nb)
    key_off = jnp.arange(MOBA_BLOCK)

    def per_batch(args):
        q1, k1, v1 = args
        kp = jnp.pad(k1, ((0, pad), (0, 0), (0, 0))).reshape(nb, MOBA_BLOCK, H, dh).transpose(2, 0, 1, 3)
        vp = jnp.pad(v1, ((0, pad), (0, 0), (0, 0))).reshape(nb, MOBA_BLOCK, H, dh).transpose(2, 0, 1, 3)
        kmean = jnp.mean(kp.astype(jnp.float32), axis=2)
        qc = q1.reshape(n_chunks, Q_BLOCK, H, dh).transpose(0, 2, 1, 3)

        def per_chunk(args2):
            qblk, c = args2
            t = c * Q_BLOCK + jnp.arange(Q_BLOCK)
            own = t // MOBA_BLOCK
            gate = jnp.einsum('hqd,hnd->hqn', qblk.astype(jnp.float32), kmean)
            gate = jnp.where(blk_ids[None, None, :] < own[None, :, None], gate, NEG_INF)
            _, sel = lax.top_k(gate, topk)
            idx = jnp.concatenate([sel, jnp.broadcast_to(own[None, :, None], (H, Q_BLOCK, 1))], axis=-1)
            k_sel = kp[h_i, idx]
            v_sel = vp[h_i, idx]
            logits = jnp.einsum('hqd,hqtld->hqtl', qblk, k_sel, preferred_element_type=jnp.float32) * scale
            kpos = idx[..., None] * MOBA_BLOCK + key_off
            dist = t[None, :, None, None] - kpos
            logits = logits + bias_ht[h_i[..., None], rel_bucket(dist)]
            slot_ok = jnp.concatenate([jnp.arange(topk)[None, :] < own[:, None],
                                       jnp.ones((Q_BLOCK, 1), dtype=bool)], axis=1)
            mask = slot_ok[None, :, :, None] & (dist >= 0)
            logits = jnp.where(mask, logits, NEG_INF)
            p = jax.nn.softmax(logits.reshape(H, Q_BLOCK, -1), axis=-1).reshape(logits.shape)
            out = jnp.einsum('hqtl,hqtld->hqd', p.astype(v_sel.dtype), v_sel, preferred_element_type=jnp.float32)
            return out.astype(q.dtype)

        outs = lax.map(per_chunk, (qc, jnp.arange(n_chunks)))
        return outs.transpose(0, 2, 1, 3).reshape(S, H, dh)

    return lax.map(per_batch, (q, k, v))

def diff_attention(q, k, v, table_b, lam, subln_g, lambda_init):
    B_, S, H, _, dq = q.shape
    n_chunks = S // Q_BLOCK
    scale = dq ** -0.5
    kt = k.transpose(0, 2, 3, 1, 4)
    vt = v.transpose(0, 2, 1, 3)
    qc = q.reshape(B_, n_chunks, Q_BLOCK, H, 2, dq).transpose(1, 0, 3, 4, 2, 5)
    bias_ht = table_b.T.astype(jnp.float32)
    s_pos = jnp.arange(S)

    def per_chunk(args):
        qblk, c = args
        t = c * Q_BLOCK + jnp.arange(Q_BLOCK)
        dist = t[:, None] - s_pos[None, :]
        bias = bias_ht[:, rel_bucket(dist)]
        logits = jnp.einsum('bhmqd,bhmsd->bhmqs', qblk, kt, preferred_element_type=jnp.float32) * scale
        logits = jnp.where(dist >= 0, logits + bias[None, :, None], NEG_INF)
        p = jax.nn.softmax(logits, axis=-1)
        attn = p[:, :, 0] - lam * p[:, :, 1]
        return jnp.einsum('bhqs,bhsd->bhqd', attn.astype(v.dtype), vt, preferred_element_type=jnp.float32)

    outs = lax.map(per_chunk, (qc, jnp.arange(n_chunks)))
    o = outs.transpose(1, 0, 3, 2, 4).reshape(B_, S, H, -1)
    o = rms_norm(o, subln_g) * (1.0 - lambda_init)
    return o.astype(v.dtype)

def memory_cross_attention(x, mem, norm_g, mem_g, wq, wk, wv, wo):
    B_, S, _ = x.shape
    M = mem.shape[1]
    h = rms_norm(x, norm_g)
    m = rms_norm(mem, mem_g)
    q = (h @ wq).reshape(B_, S, MEM_HEADS, MEM_HEAD_DIM)
    k = (m @ wk).reshape(B_, M, MEM_HEADS, MEM_HEAD_DIM)
    v = (m @ wv).reshape(B_, M, MEM_HEADS, MEM_HEAD_DIM)
    logits = jnp.einsum('bshd,bmhd->bhsm', q, k, preferred_element_type=jnp.float32) * (MEM_HEAD_DIM ** -0.5)
    p = jax.nn.softmax(logits, axis=-1)
    o = jnp.einsum('bhsm,bmhd->bshd', p.astype(v.dtype), v, preferred_element_type=jnp.float32).astype(x.dtype)
    return o.reshape(B_, S, MEM_HEADS * MEM_HEAD_DIM) @ wo

def swiglu(x, norm_g, w_gate, w_up, w_down):
    h = rms_norm(x, norm_g)
    return (jax.nn.silu(h @ w_gate) * (h @ w_up)) @ w_down

def first_inputs(seed: int = 0) -> dict:
    key = jax.random.key(seed)
    ks = jax.random.split(key, 24)
    f32 = jnp.float32

    def w(k, shape, fan_in):
        return jax.random.normal(k, shape, f32) * (fan_in ** -0.5)

    def gain(k, shape):
        return 1.0 + 0.02 * jax.random.normal(k, shape, f32)

    return {
        "x": jax.random.normal(ks[0], (BATCH, SEQ, D_MODEL), f32),
        "mem": jax.random.normal(ks[1], (BATCH, MEM_LEN, D_MODEL), f32),
        "mix_norm_g": gain(ks[2], (DEPTH, D_MODEL)),
        "w_in": w(ks[3], (DEPTH, D_MODEL, IN_WIDTH), D_MODEL),
        "moba_out_g": gain(ks[4], (DEPTH, A_WIDTH)),
        "diff_lambda": 0.1 * jax.random.normal(ks[5], (DEPTH, 4, B_QK_DIM), f32),
        "diff_subln_g": gain(ks[6], (DEPTH, B_V_DIM)),
        "w_out": w(ks[7], (DEPTH, MIX_WIDTH, D_MODEL), MIX_WIDTH),
        "rel_bias_table": 0.5 * jax.random.normal(ks[8], (REL_BUCKETS, N_ATT_HEADS), f32),
        "cross_norm_g": gain(ks[9], (DEPTH, D_MODEL)),
        "mem_norm_g": gain(ks[10], (DEPTH, D_MODEL)),
        "w_cq": w(ks[11], (DEPTH, D_MODEL, MEM_HEADS * MEM_HEAD_DIM), D_MODEL),
        "w_ck": w(ks[12], (DEPTH, D_MODEL, MEM_HEADS * MEM_HEAD_DIM), D_MODEL),
        "w_cv": w(ks[13], (DEPTH, D_MODEL, MEM_HEADS * MEM_HEAD_DIM), D_MODEL),
        "w_co": w(ks[14], (DEPTH, MEM_HEADS * MEM_HEAD_DIM, D_MODEL), MEM_HEADS * MEM_HEAD_DIM),
        "ffn_norm_g": gain(ks[15], (DEPTH, D_MODEL)),
        "w_gate": w(ks[16], (DEPTH, D_MODEL, D_FF), D_MODEL),
        "w_up": w(ks[17], (DEPTH, D_MODEL, D_FF), D_MODEL),
        "w_down": w(ks[18], (DEPTH, D_FF, D_MODEL), D_FF),
        "final_norm_g": gain(ks[19], (D_MODEL,)),
    }

def first_block(x, mem, mix_norm_g, w_in, moba_out_g, diff_lambda, diff_subln_g, w_out, rel_bias_table,
              cross_norm_g, mem_norm_g, w_cq, w_ck, w_cv, w_co, ffn_norm_g, w_gate, w_up, w_down,
              final_norm_g):
    B_, S, _ = x.shape
    table_a = rel_bias_table[:, :A_HEADS]
    table_b = rel_bias_table[:, A_HEADS:]
    for l in range(DEPTH):
        h = rms_norm(x, mix_norm_g[l])
        proj = jnp.einsum('bsd,de->bse', h, w_in[l])
        qa, ka, va, qb, kb, vb = jnp.split(proj, IN_SPLITS, axis=-1)
        oa = moba_attention(qa.reshape(B_, S, A_HEADS, A_HEAD_DIM),
                            ka.reshape(B_, S, A_HEADS, A_HEAD_DIM),
                            va.reshape(B_, S, A_HEADS, A_HEAD_DIM), table_a)
        oa = rms_norm(oa.reshape(B_, S, A_WIDTH), moba_out_g[l])
        lambda_init = 0.8 - 0.6 * math.exp(-0.3 * l)
        lp = diff_lambda[l].astype(jnp.float32)
        lam = jnp.exp(jnp.sum(lp[0] * lp[1])) - jnp.exp(jnp.sum(lp[2] * lp[3])) + lambda_init
        ob = diff_attention(qb.reshape(B_, S, B_HEADS, 2, B_QK_DIM),
                            kb.reshape(B_, S, B_HEADS, 2, B_QK_DIM),
                            vb.reshape(B_, S, B_HEADS, B_V_DIM),
                            table_b, lam, diff_subln_g[l], lambda_init)
        ob = ob.reshape(B_, S, B_WIDTH)
        mixed = jnp.concatenate([oa, ob], axis=-1)
        x = x + jnp.einsum('bse,ed->bsd', mixed, w_out[l])
        x = x + memory_cross_attention(x, mem, cross_norm_g[l], mem_norm_g[l], w_cq[l], w_ck[l], w_cv[l], w_co[l])
        x = x + swiglu(x, ffn_norm_g[l], w_gate[l], w_up[l], w_down[l])
    return rms_norm(x, final_norm_g)


CTX_LEN = 256
GRID_W = 64

HG_HEADS = 4
HG_DK = 128
HG_DV = 128
HG_KEY_WIDTH = HG_HEADS * HG_DK
HG_WIDTH = HG_HEADS * HG_DV
HG_CHUNK = 16

CM_CHUNK = 128
CM_GROUPS = 4
CM_WIDTH = 512
CM_GROUP_DIM = CM_WIDTH // CM_GROUPS
ROWS_PER_CHUNK = CM_CHUNK // GRID_W

SPLIT_IDX = (HG_KEY_WIDTH, 2 * HG_KEY_WIDTH, 3 * HG_KEY_WIDTH, 3 * HG_KEY_WIDTH + HG_WIDTH,
             3 * HG_KEY_WIDTH + 2 * HG_WIDTH, 3 * HG_KEY_WIDTH + 2 * HG_WIDTH + 2 * CM_WIDTH)
D_IN = 3 * HG_KEY_WIDTH + 2 * HG_WIDTH + 2 * CM_WIDTH + 2 * D_MODEL

N_EXPERTS = 64
TOP_K = 8
N_EXPERT_GROUPS = 8
TOPK_GROUPS = 4
D_EXPERT = 256
D_SHARED = 256
ROUTED_SCALE = 2.5
MOE_BLOCK = 256


def rms_norm_2(x, g):
    x32 = x.astype(jnp.float32)
    y = x32 * lax.rsqrt(jnp.mean(x32 * x32, axis=-1, keepdims=True) + EPS)
    return (y * g.astype(jnp.float32)).astype(x.dtype)

def layer_norm(x, g, b):
    x32 = x.astype(jnp.float32)
    xc = x32 - jnp.mean(x32, axis=-1, keepdims=True)
    y = xc * lax.rsqrt(jnp.mean(xc * xc, axis=-1, keepdims=True) + EPS)
    return (y * g.astype(jnp.float32) + b.astype(jnp.float32)).astype(x.dtype)

def hgrn2_gates(z, lb):
    B, T, _ = z.shape
    z = z.astype(jnp.float32).reshape(B, T, HG_HEADS, HG_DK)
    lb = lb.reshape(HG_HEADS, HG_DK)
    log_f = jnp.log(lb + (1.0 - lb) * jax.nn.sigmoid(z))
    k = (1.0 - lb) * jax.nn.sigmoid(-z)
    return k, log_f

def gla_chunk_scan(q, k, v, log_f, s0, readout):
    B, T, H, DK = k.shape
    DV = v.shape[-1]
    n = T // HG_CHUNK

    def to_chunks(a):
        return a.astype(jnp.float32).reshape(B, n, HG_CHUNK, H, a.shape[-1]).transpose(1, 0, 3, 2, 4)

    kc, vc = to_chunks(k), to_chunks(v)
    bc = jnp.cumsum(to_chunks(log_f), axis=3)
    tri = jnp.tril(jnp.ones((HG_CHUNK, HG_CHUNK), dtype=bool))
    mid = HG_CHUNK // 2 - 1

    def step(S, xs):
        k_, v_, b_ = xs[0], xs[1], xs[2]
        b_last = b_[:, :, -1:, :]
        S_new = jnp.exp(b_last[:, :, 0, :, None]) * S + jnp.einsum('bhsd,bhsv->bhdv', k_ * jnp.exp(b_last - b_), v_)
        if not readout:
            return S_new, None
        q_ = xs[3]
        b_mid = b_[:, :, mid:mid + 1, :]
        A = jnp.einsum('bhtd,bhsd->bhts', q_ * jnp.exp(b_ - b_mid), k_ * jnp.exp(b_mid - b_))
        A = jnp.where(tri, A, 0.0)
        o = jnp.einsum('bhts,bhsv->bhtv', A, v_) + jnp.einsum('bhtd,bhdv->bhtv', q_ * jnp.exp(b_), S)
        return S_new, o

    xs = (kc, vc, bc, to_chunks(q)) if readout else (kc, vc, bc)
    S_fin, o = lax.scan(step, s0, xs)
    if readout:
        o = o.transpose(1, 0, 3, 2, 4).reshape(B, T, H, DV)
    return o, S_fin

def chunk_spatial_gating(p, n_chunks, ln_g, ln_b, w_s, b_s):
    a = jax.nn.gelu(p)
    u, v = jnp.split(a, 2, axis=-1)
    v = layer_norm(v, ln_g, ln_b)
    B, T, _ = v.shape
    v = v.reshape(B, n_chunks, CM_CHUNK, CM_GROUPS, CM_GROUP_DIM)
    z = jnp.einsum('gpq,bnqgc->bnpgc', w_s, v) + b_s[None, None, :, :, None]
    return u * z.reshape(B, T, CM_WIDTH)

def token_mixer(h_lat, h_ctx, w_in, lb, g_out, ln_g, ln_b, w_s, b_s, w_a, w_b, w_o,
                n_lat_chunks, n_ctx_chunks, need_ctx):
    B, T, _ = h_lat.shape
    L = h_ctx.shape[1]
    p_lat = h_lat @ w_in
    p_ctx = h_ctx @ w_in
    ql, fl_fwd, fl_bwd, il, gl, cml, gtl = jnp.split(p_lat, SPLIT_IDX, axis=-1)
    qc, fc_fwd, fc_bwd, ic, gc, cmc, gtc = jnp.split(p_ctx, SPLIT_IDX, axis=-1)

    q_lat = jax.nn.silu(ql).reshape(B, T, HG_HEADS, HG_DK)
    v_lat = il.reshape(B, T, HG_HEADS, HG_DV)
    q_ctx = jax.nn.silu(qc).reshape(B, L, HG_HEADS, HG_DK) if need_ctx else None
    v_ctx = ic.reshape(B, L, HG_HEADS, HG_DV)
    s0 = jnp.zeros((B, HG_HEADS, HG_DK, HG_DV), jnp.float32)

    lat_outs, ctx_outs = [], []
    for d, (f_lat, f_ctx) in enumerate(((fl_fwd, fc_fwd), (fl_bwd, fc_bwd))):
        rev = (lambda a: a[:, ::-1]) if d == 1 else (lambda a: a)
        k_l, lf_l = hgrn2_gates(f_lat, lb[d])
        k_c, lf_c = hgrn2_gates(f_ctx, lb[d])
        q_c = rev(q_ctx) if need_ctx else None
        oc, s_ctx = gla_chunk_scan(q_c, rev(k_c), rev(v_ctx), rev(lf_c), s0, need_ctx)
        ol, _ = gla_chunk_scan(rev(q_lat), rev(k_l), rev(v_lat), rev(lf_l), s_ctx, True)
        lat_outs.append(rev(ol))
        if need_ctx:
            ctx_outs.append(rev(oc))

    def merge(o, g, cm, gt, n_chunks, dtype):
        n_tok = o.shape[1]
        g = g.reshape(B, n_tok, HG_HEADS, HG_DV).astype(jnp.float32)
        a = (rms_norm_2(o, g_out) * jax.nn.silu(g)).reshape(B, n_tok, HG_WIDTH).astype(dtype)
        bm = chunk_spatial_gating(cm, n_chunks, ln_g, ln_b, w_s, b_s)
        ga, gb = jnp.split(gt, 2, axis=-1)
        y = jax.nn.sigmoid(ga) * (a @ w_a) + jax.nn.sigmoid(gb) * (bm @ w_b)
        return y @ w_o

    y_lat = merge(lat_outs[0] + lat_outs[1], gl, cml, gtl, n_lat_chunks, h_lat.dtype)
    y_ctx = merge(ctx_outs[0] + ctx_outs[1], gc, cmc, gtc, n_ctx_chunks, h_ctx.dtype) if need_ctx else None
    return y_lat, y_ctx

def swiglu_2(h, w_gu, w_down):
    gate, up = jnp.split(h @ w_gu, 2, axis=-1)
    return (jax.nn.silu(gate) * up) @ w_down

def moe_ffn(h, w_router, b_router, w_gu, w_down, w_sh_gu, w_sh_down):
    N, D = h.shape
    scores = jax.nn.sigmoid((h @ w_router).astype(jnp.float32))
    sel = scores + b_router.astype(jnp.float32)
    grp = sel.reshape(N, N_EXPERT_GROUPS, N_EXPERTS // N_EXPERT_GROUPS)
    grp_score = jnp.sum(lax.top_k(grp, 2)[0], axis=-1)
    _, top_g = lax.top_k(grp_score, TOPK_GROUPS)
    gmask = jnp.any(top_g[:, :, None] == jnp.arange(N_EXPERT_GROUPS)[None, None, :], axis=1)
    sel = jnp.where(jnp.repeat(gmask, N_EXPERTS // N_EXPERT_GROUPS, axis=1), sel, -jnp.inf)
    _, top_e = lax.top_k(sel, TOP_K)
    w = jnp.take_along_axis(scores, top_e, axis=1)
    w = w / jnp.sum(w, axis=-1, keepdims=True) * ROUTED_SCALE

    M = N * TOP_K
    flat_e = top_e.reshape(M).astype(jnp.int32)
    flat_tok = jnp.repeat(jnp.arange(N, dtype=jnp.int32), TOP_K)
    flat_w = w.reshape(M)
    counts = jnp.bincount(flat_e, length=N_EXPERTS).astype(jnp.int32)
    padded = (counts + MOE_BLOCK - 1) // MOE_BLOCK * MOE_BLOCK
    pad_end = jnp.cumsum(padded)
    pad_start = pad_end - padded
    start = jnp.cumsum(counts) - counts
    order = jnp.argsort(flat_e)
    se, stok, sw = flat_e[order], flat_tok[order], flat_w[order]
    dest = pad_start[se] + jnp.arange(M, dtype=jnp.int32) - start[se]
    NB = -(-M // MOE_BLOCK) + N_EXPERTS
    row_tok = jnp.full((NB * MOE_BLOCK,), N, jnp.int32).at[dest].set(stok)
    row_w = jnp.zeros((NB * MOE_BLOCK,), jnp.float32).at[dest].set(sw)
    block_e = jnp.clip(jnp.searchsorted(pad_end, jnp.arange(NB, dtype=jnp.int32) * MOE_BLOCK, side='right'),
                       0, N_EXPERTS - 1)
    h_pad = jnp.concatenate([h, jnp.zeros((1, D), h.dtype)], axis=0)

    def expert_block(acc, blk):
        tok, wts, e = blk
        out = swiglu_2(h_pad[tok], w_gu[e], w_down[e])
        return acc.at[tok].add(out * wts[:, None].astype(out.dtype)), None

    acc, _ = lax.scan(expert_block, jnp.zeros((N + 1, D), h.dtype),
                      (row_tok.reshape(NB, MOE_BLOCK), row_w.reshape(NB, MOE_BLOCK), block_e))
    return acc[:N] + swiglu_2(h, w_sh_gu, w_sh_down)

def second_inputs(seed: int = 0) -> dict:
    key = jax.random.key(seed)
    ks = jax.random.split(key, 26)

    def nrm(k, shape, scale):
        return jax.random.normal(k, shape, jnp.float32) * scale

    def gain(k, shape):
        return 1.0 + nrm(k, shape, 0.05)

    D = D_MODEL
    return {
        'x': nrm(ks[0], (BATCH, SEQ, D), 1.0),
        'c': nrm(ks[1], (BATCH, D), 1.0),
        'ctx': nrm(ks[2], (BATCH, CTX_LEN, D), 1.0),
        'c_ctx': nrm(ks[3], (D,), 1.0),
        'w_ada': nrm(ks[4], (DEPTH, D, 6 * D), 0.5 * D ** -0.5),
        'b_ada': nrm(ks[5], (DEPTH, 6 * D), 0.02),
        'g_pre_mix': gain(ks[6], (DEPTH, D)),
        'g_post_mix': gain(ks[7], (DEPTH, D)),
        'g_pre_ffn': gain(ks[8], (DEPTH, D)),
        'g_post_ffn': gain(ks[9], (DEPTH, D)),
        'w_in': nrm(ks[10], (DEPTH, D, D_IN), D ** -0.5),
        'lb_logits': nrm(ks[11], (2, DEPTH + 1, HG_KEY_WIDTH), 0.1),
        'g_hgrn_out': gain(ks[12], (DEPTH, HG_DV)),
        'cm_ln_g': gain(ks[13], (DEPTH, CM_WIDTH)),
        'cm_ln_b': nrm(ks[14], (DEPTH, CM_WIDTH), 0.02),
        'w_spatial': nrm(ks[15], (DEPTH, CM_GROUPS, CM_CHUNK, CM_CHUNK), CM_CHUNK ** -0.5),
        'b_spatial': 1.0 + nrm(ks[16], (DEPTH, CM_CHUNK, CM_GROUPS), 0.1),
        'w_branch_a': nrm(ks[17], (DEPTH, HG_WIDTH, D), HG_WIDTH ** -0.5),
        'w_branch_b': nrm(ks[18], (DEPTH, CM_WIDTH, D), CM_WIDTH ** -0.5),
        'w_out': nrm(ks[19], (DEPTH, D, D), D ** -0.5),
        'w_router': nrm(ks[20], (DEPTH, D, N_EXPERTS), D ** -0.5),
        'b_router': nrm(ks[21], (DEPTH, N_EXPERTS), 0.01),
        'w_expert_gu': nrm(ks[22], (DEPTH, N_EXPERTS, D, 2 * D_EXPERT), D ** -0.5),
        'w_expert_down': nrm(ks[23], (DEPTH, N_EXPERTS, D_EXPERT, D), D_EXPERT ** -0.5),
        'w_shared_gu': nrm(ks[24], (DEPTH, D, 2 * D_SHARED), D ** -0.5),
        'w_shared_down': nrm(ks[25], (DEPTH, D_SHARED, D), D_SHARED ** -0.5),
    }

def second_block(x, c, ctx, c_ctx, w_ada, b_ada, g_pre_mix, g_post_mix, g_pre_ffn, g_post_ffn, w_in,
              lb_logits, g_hgrn_out, cm_ln_g, cm_ln_b, w_spatial, b_spatial, w_branch_a, w_branch_b,
              w_out, w_router, b_router, w_expert_gu, w_expert_down, w_shared_gu, w_shared_down):
    B, T, D = x.shape
    L = ctx.shape[1]
    rows = T // GRID_W
    n_lat_chunks = rows // ROWS_PER_CHUNK
    n_ctx_chunks = L // CM_CHUNK
    lower_bounds = jnp.cumsum(jax.nn.softmax(lb_logits.astype(jnp.float32), axis=1), axis=1)
    silu_c = jax.nn.silu(c)
    silu_cc = jax.nn.silu(c_ctx)
    x_lat, x_ctx = x, ctx
    for l in range(DEPTH):
        need_ctx = l < DEPTH - 1
        mod_lat = (silu_c @ w_ada[l] + b_ada[l])[:, None, :]
        mod_ctx = silu_cc @ w_ada[l] + b_ada[l]
        sh1, sc1, gt1, sh2, sc2, gt2 = jnp.split(mod_lat, 6, axis=-1)
        csh1, csc1, cgt1, csh2, csc2, cgt2 = jnp.split(mod_ctx, 6, axis=-1)

        h_lat = rms_norm_2(x_lat, g_pre_mix[l]) * (1.0 + sc1) + sh1
        h_ctx = rms_norm_2(x_ctx, g_pre_mix[l]) * (1.0 + csc1) + csh1
        y_lat, y_ctx = token_mixer(h_lat, h_ctx, w_in[l], lower_bounds[:, l], g_hgrn_out[l], cm_ln_g[l],
                                   cm_ln_b[l], w_spatial[l], b_spatial[l], w_branch_a[l], w_branch_b[l],
                                   w_out[l], n_lat_chunks, n_ctx_chunks, need_ctx)
        x_lat = x_lat + gt1 * rms_norm_2(y_lat, g_post_mix[l])
        if need_ctx:
            x_ctx = x_ctx + cgt1 * rms_norm_2(y_ctx, g_post_mix[l])

        h2_lat = (rms_norm_2(x_lat, g_pre_ffn[l]) * (1.0 + sc2) + sh2).reshape(B * T, D)
        if need_ctx:
            h2_ctx = (rms_norm_2(x_ctx, g_pre_ffn[l]) * (1.0 + csc2) + csh2).reshape(B * L, D)
            f_all = moe_ffn(jnp.concatenate([h2_lat, h2_ctx], axis=0), w_router[l], b_router[l],
                            w_expert_gu[l], w_expert_down[l], w_shared_gu[l], w_shared_down[l])
            f_lat, f_ctx = f_all[:B * T], f_all[B * T:]
            x_ctx = x_ctx + cgt2 * rms_norm_2(f_ctx.reshape(B, L, D), g_post_ffn[l])
        else:
            f_lat = moe_ffn(h2_lat, w_router[l], b_router[l], w_expert_gu[l], w_expert_down[l],
                            w_shared_gu[l], w_shared_down[l])
        x_lat = x_lat + gt2 * rms_norm_2(f_lat.reshape(B, T, D), g_post_ffn[l])
    return x_lat


def setup_inputs(seed=0):
    out = dict(first_inputs(seed))
    for name, value in second_inputs(seed + 1).items():
        if name != "x":
            out[name + "_2"] = value
    return out


def reference(
    x, mem, mix_norm_g, w_in, moba_out_g, diff_lambda, diff_subln_g, w_out, rel_bias_table,
    cross_norm_g, mem_norm_g, w_cq, w_ck, w_cv, w_co, ffn_norm_g, w_gate, w_up, w_down,
    final_norm_g, c_2, ctx_2, c_ctx_2, w_ada_2, b_ada_2, g_pre_mix_2, g_post_mix_2, g_pre_ffn_2,
    g_post_ffn_2, w_in_2, lb_logits_2, g_hgrn_out_2, cm_ln_g_2, cm_ln_b_2, w_spatial_2,
    b_spatial_2, w_branch_a_2, w_branch_b_2, w_out_2, w_router_2, b_router_2, w_expert_gu_2,
    w_expert_down_2, w_shared_gu_2, w_shared_down_2,
):
    x = first_block(
        x, mem, mix_norm_g, w_in, moba_out_g, diff_lambda, diff_subln_g, w_out, rel_bias_table,
        cross_norm_g, mem_norm_g, w_cq, w_ck, w_cv, w_co, ffn_norm_g, w_gate, w_up, w_down,
        final_norm_g,
    )
    return second_block(
        x, c_2, ctx_2, c_ctx_2, w_ada_2, b_ada_2, g_pre_mix_2, g_post_mix_2, g_pre_ffn_2,
        g_post_ffn_2, w_in_2, lb_logits_2, g_hgrn_out_2, cm_ln_g_2, cm_ln_b_2, w_spatial_2,
        b_spatial_2, w_branch_a_2, w_branch_b_2, w_out_2, w_router_2, b_router_2, w_expert_gu_2,
        w_expert_down_2, w_shared_gu_2, w_shared_down_2,
    )


_drawn_inputs = setup_inputs


def setup_inputs(seed=0):
    import zlib

    import numpy as np

    out = dict(_drawn_inputs(seed))
    spreads = {}
    factors = {'cross_norm_g': 6.343,
     'mem_norm_g': 5.256,
     'ctx_2': 5.607,
     'c_ctx_2': 4.809,
     'g_post_ffn_2': 3.995,
     'lb_logits_2': 5.882,
     'g_hgrn_out_2': 2.806,
     'cm_ln_b_2': 4.539}
    for name, (base, spread) in spreads.items():
        noise = np.random.default_rng([zlib.crc32(name.encode()), seed]).standard_normal(out[name].shape)
        drawn = base * np.exp(spread * noise) if base else spread * noise
        out[name] = jnp.asarray(drawn.astype(out[name].dtype))
    for name, factor in factors.items():
        out[name] = (out[name] * factor).astype(out[name].dtype)
    return out
```

```python
import math
from contextlib import ExitStack

import concourse.bass as bass
from concourse import mybir
import numpy as np

F32 = mybir.dt.float32
I32 = mybir.dt.int32
ALU = mybir.AluOpType
ACT = mybir.ActivationFunctionType
AX_X = mybir.AxisListType.X

P = 128
EPS = 1e-6
NEG_INF = -1e30
LOCAL_LEVELS = 4
SCAN_CHUNK = 16
REL_BUCKETS, REL_MAX_DIST = 32, 128
LAMBDA_INIT = 0.8 - 0.6 * math.exp(-0.3 * 0)
ROUTED_SCALE = 2.5
TOP_K, TOPK_GROUPS, N_GROUPS = 8, 4, 8



class Count:

    def __init__(self, sem):
        self.sem, self.value = sem, 0


class Done:

    def __init__(self, count, value, loop):
        self.count, self.value, self.loop = count, value, loop


class Before:

    done = None


class Both:

    def __init__(self, *moments):
        self.moments = []
        for m in moments:
            self.moments += m.moments if isinstance(m, Both) else [m]


def flat(moments):
    return [m for m in Both(*moments).moments if m is not None]


class Loop:
    def __init__(self, n):
        self.n, self.start, self.step = n, {}, {}


class Program:

    def __init__(self, nc, ctx):
        self.nc, self.ctx = nc, ctx
        self.counts, self.carried, self.loop = [], [], None
        self.queues = {e: [] for e in ("sync", "scalar", "vector", "gpsimd", "tensor")}
        self.engine_count = {e: self.count(f"done_{e}") for e in self.queues}

    def count(self, name):
        self.counts.append(Count(self.ctx.enter_context(self.nc.semaphore(name))))
        return self.counts[-1]

    def put(self, engine, fn, after=(), count=None, by=1):
        count = count or self.engine_count[engine]
        if self.loop is not None:
            assert count in self.loop.start, "made before the loop"
        count.value += by
        q = self.queues[engine] if self.loop is None else self.loop.queues[engine]
        q.append((fn, flat(after), count, by))
        return Done(count, count.value, self.loop)

    def pe(self, fn, *after):
        return self.put("tensor", fn, after)

    def dve(self, fn, *after):
        return self.put("vector", fn, after)

    def act(self, fn, *after):
        return self.put("scalar", fn, after)

    def pool(self, fn, *after):
        return self.put("gpsimd", fn, after)

    def dma(self, engine, fn, count, *after):
        return self.put(engine, fn, after, count, 16)

    def begin(self, n):
        self.loop = Loop(n)
        self.loop.queues = {e: [] for e in self.queues}
        self.loop.start = {c: c.value for c in self.counts}
        self.loop.carried = []
        for table in self.carried:
            for key, old in table.items():
                before = Before()
                table[key] = Both(old, before)
                self.loop.carried.append((table, key, old, before, table[key]))

    def end(self):
        loop, self.loop = self.loop, None
        for c, start in loop.start.items():
            loop.step[c] = c.value - start
            c.value = start + loop.n * loop.step[c]
        for table, key, old, before, entry in loop.carried:
            if table[key] is entry:
                table[key] = old
            else:
                before.done = table[key]
        for e, q in loop.queues.items():
            if q:
                self.queues[e].append(loop)

    def emit(self, block):
        for name, put_body in (("sync", block.sync), ("scalar", block.scalar), ("vector", block.vector),
                               ("gpsimd", block.gpsimd), ("tensor", block.tensor)):
            def body(eng, name=name):
                reached = {}
                for entry in self.queues[name]:
                    if isinstance(entry, Loop):
                        self.emit_loop(eng, name, entry, reached)
                        continue
                    fn, after, count, by = entry
                    for a in after:
                        self.wait(eng, a, reached)
                    fn(eng, None).then_inc(count.sem, by)
            put_body(body)

    def wait(self, eng, a, reached):
        v = a.value if a.loop is None else a.value + (a.loop.n - 1) * a.loop.step[a.count]
        if reached.get(a.count, 0) < v:
            reached[a.count] = v
            eng.wait_ge(a.count.sem, v)

    def emit_loop(self, eng, name, loop, reached):
        queue = loop.queues[name]
        for _, after, _, _ in queue:
            for a in after:
                if isinstance(a, Done) and a.loop is not loop:
                    self.wait(eng, a, reached)
        with eng.Fori(0, loop.n) as i:
            for fn, after, count, by in queue:
                need = {}
                for a in after:
                    if isinstance(a, Before):
                        if a.done is None:
                            continue
                        for d in flat([a.done]):
                            if isinstance(d, Done) and d.loop is loop:
                                need[d.count] = max(need.get(d.count, 1), d.value - loop.step[d.count])
                                assert d.value > loop.step[d.count], "has to have counted before the loop"
                    elif a.loop is loop:
                        need[a.count] = max(need.get(a.count, 1), a.value)
                for c, v in need.items():
                    eng.wait_ge(c.sem, v + i * loop.step[c])
                fn(eng, i).then_inc(count.sem, by)



def bucket_of(dist):
    exact = REL_BUCKETS // 2
    if dist < exact:
        return dist
    large = exact + int(math.log(dist / exact) / math.log(REL_MAX_DIST / exact) * (REL_BUCKETS - exact) + 1e-9)
    return min(large, REL_BUCKETS - 1)


def bucket_rows(seq):
    rows = np.zeros((REL_BUCKETS + 1, 2 * seq), np.float32)
    for n in range(2 * seq):
        dist = seq - 1 - n
        rows[bucket_of(dist) if dist >= 0 else REL_BUCKETS, n] = 1.0
    return rows


def decay_masks():
    fwd = np.zeros((P, LOCAL_LEVELS, P), np.float32)
    for t in range(P):
        base = t // SCAN_CHUNK * SCAN_CHUNK
        mid = base + SCAN_CHUNK // 2 - 1
        fwd[mid + 1:t + 1, 0, t] = 1.0
        fwd[t + 1:mid + 1, 0, t] = -1.0
        for level in range(1, LOCAL_LEVELS):
            size = SCAN_CHUNK << level
            border = t // size * size + size // 2
            fwd[border:t + 1, level, t] = 1.0
            fwd[t + 1:border, level, t] = 1.0
    bwd = fwd[::-1, :, ::-1]
    s, t = np.meshgrid(np.arange(P), np.arange(P), indexing="ij")
    edges = np.stack([s > t, s <= t, s < t, s >= t, s >= 0], 1).astype(np.float32)
    return np.concatenate([fwd, bwd, edges], 1)


def pair_masks():
    fwd = np.zeros((P, LOCAL_LEVELS, P), np.float32)
    s, t = np.meshgrid(np.arange(P), np.arange(P), indexing="ij")
    fwd[:, 0] = (s // SCAN_CHUNK == t // SCAN_CHUNK) & (s <= t)
    for level in range(1, LOCAL_LEVELS):
        size = SCAN_CHUNK << level
        fwd[:, level] = (s // size == t // size) & (s % size < size // 2) & (t % size >= size // 2)
    return np.concatenate([fwd, fwd[::-1, :, ::-1]], 1)


MASK_GT, MASK_LE, MASK_LT, MASK_GE, MASK_ALL = range(2 * LOCAL_LEVELS, 2 * LOCAL_LEVELS + 5)



def build_program(nc, a, out, scratch_bias):
    with ExitStack() as ctx:
        queue_program(nc, ctx, a, out, scratch_bias)


def queue_program(nc, ctx, a, out, scratch_bias):
    prog = Program(nc, ctx)
    pe, dve, act, pool = prog.pe, prog.dve, prog.act, prog.pool

    def sb(name, *shape, dtype=F32):
        return ctx.enter_context(nc.sbuf_tensor(name, list(shape), dtype))

    _, SEQ, D = a["x"].shape
    NT = SEQ // P
    KD = D // P
    UNIT = 512
    A_HEADS, A_DIM = 8, 64
    B_HEADS, B_V = 4, 128
    A_W = A_HEADS * A_DIM
    B_W = B_HEADS * B_V
    MAPS = A_HEADS + 2 * B_HEADS
    M_HEADS, M_DIM = 4, D // 4
    D_FF = a["w_gate"].shape[2]
    GW = 512
    GH = 4
    N_EXP = a["w_expert_gu_2"].shape[1]
    D_EXP = a["w_expert_down_2"].shape[2]
    IN2 = a["w_in_2"].shape[2]

    bank = [ctx.enter_context(nc.psum_tensor(f"bank{b}", [P, 512], F32)) for b in range(8)]
    bank_read = {b: None for b in range(8)}

    ident = sb("ident", P, P)
    slots = [sb(f"weights{n}", P, KD, UNIT) for n in range(2)]
    slot_used = {0: None, 1: None}
    hidden_read = {0: None, 1: None}
    prog.carried = [bank_read, slot_used, hidden_read]
    slot_count = [prog.count(f"weights{n}_landed") for n in range(2)]
    x_res = sb("x_res", P, NT, D)
    normed = sb("normed", P, NT, D)
    act_t = sb("act_t", P, KD, SEQ)
    mem_t = sb("mem_t", P, KD, SEQ)
    work = sb("work", P, 27136)
    rows_c = sb("rows_c", P, P)
    cols = sb("cols", P, P)
    small = sb("small", P, 256)
    half_neg = sb("half_neg", P, 16)
    junk = sb("junk", P, D)

    misc = prog.count("misc_loads")
    out_count = prog.count("out_stored")

    def region(at, *shape):
        size = int(np.prod(shape))
        view = work[:, at:at + size]
        names = "abcd"[:len(shape)]
        sizes = {n: x for n, x in zip(names[1:], shape[1:])}
        return view if len(shape) == 1 else view.rearrange(f"p ({' '.join(names)}) -> p {' '.join(names)}", **sizes)

    def everything():
        return Both(*[Done(c, c.value, None) for c in prog.engine_count.values()])

    def load(dst, src, *after, engine="scalar", count=None):
        return prog.dma(engine, lambda e, i: e.dma_start(dst, src), count or prog.count(f"load_{len(prog.counts)}"),
                        *after)

    for engine in ("scalar", "vector", "gpsimd", "tensor"):
        prog.put(engine, lambda e, i: e.nop(), by=64)

    stack, at = {}, 0
    clear_rows = dve(lambda e, i: e.memset(rows_c[:, :], 0.0))
    row_loads = []
    for name in ("mix_norm_g", "cross_norm_g", "mem_norm_g", "ffn_norm_g", "moba_out_g", "diff_subln_g",
                 "g_hgrn_out_2", "g_pre_mix_2", "g_pre_ffn_2", "c_2", "c_ctx_2"):
        v = a[name]
        flat = v.rearrange("a b -> (a b)") if len(v.shape) == 2 else v
        n = flat.shape[0] // P
        stack[name] = slice(at, at + n)
        row_loads.append(prog.dma("scalar", lambda e, i, at=at, n=n, flat=flat: e.dma_start(
            rows_c[at:at + n, :], flat.rearrange("(k p) -> k p", p=P)), misc, clear_rows))
        at += n
    rows_landed = row_loads[-1]
    mirror = sb("mirror", P, P)
    mirror_landed = load(mirror[:, :], a["mirror"], engine="sync")
    ident_landed = load(ident[:, :], a["ident"], engine="sync")
    x_landed = load(x_res[:, :, :], a["x"][0].rearrange("(t p) d -> p t d", p=P), engine="sync")
    powers = pool(lambda e, i: e.memset(half_neg[:, :], -0.5))

    tr = pe(lambda e, i: e.transpose(bank[4][:, 0:P], rows_c[:, :], ident[:, :]), rows_landed, ident_landed)
    gains = dve(lambda e, i: e.tensor_copy(cols[:, :], bank[4][:, 0:P]), tr)
    bank_read[4] = gains


    junk_written = {0: None}
    prog.carried.append(junk_written)

    def sum_squares(src, total, scale, *after):
        width = src.shape[-1]
        junk_written[0] = act(lambda e, i: e.activation(junk[:, 0:width], src, ACT.Square, scale=scale,
                                                        accum_out=total), junk_written[0], *after)
        return junk_written[0]

    def rstd_of(name, sums, scale, n, *after):
        mean = pool(lambda e, i: e.tensor_scalar(sums, sums, scale, EPS, ALU.mult, ALU.add), powers, *after)
        return pool(lambda e, i: e.tensor_tensor(sums, sums, half_neg[:, 0:n], ALU.pow), mean)

    def transposed(src, n_blocks, banks, evacuate, *after):
        moments = []
        jobs = [(t, k0) for t in range(NT) for k0 in range(0, n_blocks, 4)]
        for n, (t, k0) in enumerate(jobs):
            b = banks[n % len(banks)]
            width = min(4, n_blocks - k0)

            def run(e, i, t=t, k0=k0, b=b, width=width):
                for k in range(width):
                    last = e.transpose(bank[b][:, k * P:(k + 1) * P], src(t, k0 + k), ident[:, :])
                return last
            waits = [x[t] if isinstance(x, list) else x for x in after]
            done = pe(run, bank_read[b], *waits)
            moments.append(evacuate(b, t, k0, width, done))
            bank_read[b] = moments[-1]
        return moments[-1]

    def wide(b, width):
        return bank[b][:, 0:width * P].rearrange("p (k t) -> p k t", t=P)

    def norm_t(src, dst, gain, n_free, *after, shift=None, col=0):
        scaled = []
        for t in range(NT):
            total = small[:, col + t:col + t + 1]
            sq = sum_squares(src[:, t, :], total, 1.0, *after)
            r = rstd_of("norm", total, 1.0 / D, 1, sq)
            scaled.append(dve(lambda e, i, t=t, total=total: e.tensor_scalar(
                normed[:, t, :], src[:, t, :], total, None, ALU.mult), r, normed_read[0]))

        def evacuate(b, t, k0, width, done):
            out_ap = dst[:, k0:k0 + width, t * P:(t + 1) * P]
            g = gain[:, k0:k0 + width].unsqueeze(2).to_broadcast([P, width, P])
            m = dve(lambda e, i: e.tensor_tensor(out_ap, wide(b, width), g, ALU.mult), done, n_free, gains)
            if shift is None:
                return m
            s = shift[:, k0:k0 + width].unsqueeze(2).to_broadcast([P, width, P])
            return dve(lambda e, i: e.tensor_tensor(out_ap, out_ap, s, ALU.add), m)
        m = transposed(lambda t, k: normed[:, t, k * P:(k + 1) * P], KD, [4, 5, 6, 7], evacuate, scaled)
        normed_read[0] = bank_read[7]
        return m

    normed_read = [None]

    def linear(n_units, sources, left, left_ready, evacuate, kd=KD, first=0, side=None):
        def one(j, s):
            for part in range(len(sources(0))):
                def start(e, i, part=part):
                    place, view = sources(j if i is None else 2 * i + (first + s))[part]
                    return e.dma_start(place(slots[s]), view)
                landed = prog.dma("sync", start, slot_count[s], slot_used[s])
            for t in range(NT):
                b = 2 * s + t

                def run(e, i, t=t, b=b):
                    for k in range(kd):
                        mm = e.matmul(bank[b][:, :], left[:, k, t * P:(t + 1) * P], slots[s][:, k, :],
                                      start=(k == 0), stop=(k == kd - 1))
                    return mm
                done = pe(run, landed, bank_read[b], left_ready)
                bank_read[b] = evacuate(lambda i: j if i is None else 2 * i + (first + s), t, b, done)
            slot_used[s] = done
            if side:
                side(s)

        turns = n_units // 2 if n_units >= 3 and first % 2 == 0 and (n_units >= 5 or first or side) else 0
        if turns:
            prog.begin(turns)
            one(0, 0)
            one(1, 1)
            prog.end()
        for j in range(first + 2 * turns, first + n_units):
            one(j, j % 2)

    def columns(w, n0=0, width=UNIT):
        view = w.rearrange("(k p) n -> p k n", p=P)
        kd = view.shape[1]
        return lambda j: [(lambda slot: slot[:, 0:kd, 0:width], view[:, :, bass.ds(n0 + j * UNIT, width)])]

    ones = sb("ones", P, P)
    ones_set = pool(lambda e, i: e.memset(ones[:, :], 1.0))
    side_slot = sb("side_slot", P, KD, UNIT)
    ada_acc = sb("ada_acc", P, 3, UNIT)
    silu_c = sb("silu_c", P, 2, KD)
    c_cols = cols[:, stack["c_2"].start:stack["c_ctx_2"].stop].rearrange("p (a k) -> p a k", a=2)
    silu_ready = act(lambda e, i: e.activation(silu_c[:, :, :], c_cols, ACT.Silu), gains)
    bias_row_clear = dve(lambda e, i: e.memset(ada_acc[:, 2, :], 0.0))
    side_read = {"slot": None, "lat": None, "ctx": None, "bias": bias_row_clear}
    prog.carried.append(side_read)
    side_count, side_bias_count = prog.count("ada_landed"), prog.count("ada_bias_landed")
    mod_rows = region(20992, 6, D)
    mod_cols = sb("mod_cols", P, 6, KD)
    ctx_cols = sb("ctx_cols", P, 3, KD)
    ada_v = a["w_ada_2"][0].rearrange("(k p) n -> p k n", p=P)
    ada_bias = a["b_ada_2"]

    def ada_side(first, with_ctx):
        def side(s):
            def j(i):
                return 2 * i + (first + s)
            landed = prog.dma("sync", lambda e, i: e.dma_start(
                side_slot[:, :, :], ada_v[:, :, bass.ds(j(i) * UNIT, UNIT)]), side_count, side_read["slot"])
            bias_landed_ = prog.dma("sync", lambda e, i: e.dma_start(
                ada_acc[0:1, 2, :], ada_bias[:, bass.ds(j(i) * UNIT, UNIT)]), side_bias_count, side_read["bias"])
            for who, name in enumerate(("lat", "ctx") if with_ctx else ("lat",)):
                add, free = ada_acc[:, 2, :], side_read[name]
                for k in range(KD):
                    summed = dve(lambda e, i, k=k, add=add, who=who: e.scalar_tensor_tensor(
                        ada_acc[:, who, :], side_slot[:, k, :], silu_c[:, who, k:k + 1], add, ALU.mult, ALU.add),
                        landed, bias_landed_, free, silu_ready)
                    add, free = ada_acc[:, who, :], summed
                    if k == 0:
                        side_read["bias"] = summed
                side_read["slot"] = summed

                def run(e, i, who=who):
                    if who == 0:
                        e.matmul(bank[6][:, :], ones[:, :], ada_acc[:, 0, :], start=True, stop=True)
                    for c in range(UNIT // P):
                        mm = e.matmul(bank[7][:, 4 * who + c:4 * who + c + 1], ada_acc[:, who, c * P:(c + 1) * P],
                                      ones[:, 0:1], start=True, stop=True)
                    return mm
                done = pe(run, summed, bank_read[6], bank_read[7], ones_set)
                side_read[name] = done
                cols_to = (mod_cols, ctx_cols)[who][:, :, :].rearrange("p a k -> p (a k)")
                if who == 0:
                    bank_read[6] = act(lambda e, i: e.activation(
                        mod_rows[:, :, :].rearrange("p a n -> p (a n)")[:, bass.ds(j(i) * UNIT, UNIT)],
                        bank[6][:, :], ACT.Copy), done)
                bank_read[7] = act(lambda e, i, who=who, cols_to=cols_to: e.activation(
                    cols_to[:, bass.ds(j(i) * 4, 4)], bank[7][:, 4 * who:4 * who + 4], ACT.Copy), done)
                last["ada"] = bank_read[7]
        return side
    last = {}

    h_ready = norm_t(x_res, act_t, cols[:, stack["mix_norm_g"]], None, x_landed, col=0)
    proj = region(0, NT, 3072)

    def to_proj(j, t, b, done):
        last["proj"] = act(lambda e, i: e.activation(proj[:, t, bass.ds(j(i) * UNIT, UNIT)], bank[b][:, :], ACT.Copy),
                           done)
        return last["proj"]
    linear(6, columns(a["w_in"][0]), act_t, h_ready, to_proj, side=ada_side(0, True))
    proj_ready = last["proj"]
    act_t_read = prog.engine_count["tensor"]
    act_t_free = Done(act_t_read, act_t_read.value, None)

    n_heads = A_HEADS + B_HEADS
    table = sb("table", REL_BUCKETS + 1, n_heads)
    buckets = region(14848, 2 * SEQ)[0:REL_BUCKETS + 1, :]
    bias_rows = region(14848 + 2 * SEQ, 2 * SEQ)[0:n_heads, :]
    bias = region(6144, n_heads, 3 * P)
    table_cleared = dve(lambda e, i: e.memset(table[:, :], NEG_INF))
    table_landed = load(table[0:REL_BUCKETS, :], a["rel_bias_table"], table_cleared)
    buckets_landed = load(buckets[:, :], a["bucket_rows"])
    bias_done = pe(lambda e, i: e.matmul(bank[4][0:n_heads, :], table[:, :], buckets[:, :], start=True, stop=True),
                   bank_read[4], table_landed, buckets_landed)
    bias_out = act(lambda e, i: e.activation(bias_rows[:, :], bank[4][0:n_heads, :], ACT.Copy), bias_done)
    bank_read[4] = bias_out
    bias_stored = load(scratch_bias[:, :], bias_rows[:, :], bias_out)
    spread = prog.count("bias_spread")
    for src_off, width, dst_off in ((0, SEQ, 0), (P, P, SEQ)):
        view = bass.AP(tensor=scratch_bias.tensor, offset=src_off,
                       ap=[[1, P], [2 * SEQ, n_heads], [1, width]])
        bias_landed = prog.dma("scalar", lambda e, i, view=view, dst_off=dst_off, width=width: e.dma_start(
            bias[:, :, dst_off:dst_off + width], view), spread, bias_stored)

    qk_t = region(10752, 2 * KD, SEQ)
    sources = [0, 128, 256, 384, 1536, 1664, 1792, 1920, 512, 640, 768, 896, 2048, 2176, 2304, 2432]
    turn = 0
    for n in range(0, 2 * KD, 2):
        b = 4 + (n // 2) % 4

        def run(e, i, n=n, b=b):
            for m in range(2):
                for t in range(NT):
                    last_ = e.transpose(bank[b][:, (2 * m + t) * P:(2 * m + t + 1) * P],
                                        proj[:, t, sources[n + m]:sources[n + m] + P], ident[:, :])
            return last_
        done = pe(run, bank_read[b], proj_ready)
        dst, srcv = qk_t[:, n:n + 2, :], bank[b][:, :].rearrange("p (k t) -> p k t", k=2)
        f = float(A_DIM) ** -0.5 if n < KD else 1.0
        if (n // 2) % 2:
            bank_read[b] = act(lambda e, i, dst=dst, srcv=srcv, f=f: e.activation(dst, srcv, ACT.Copy, scale=f), done)
            qk_act = bank_read[b]
        else:
            bank_read[b] = dve(lambda e, i, dst=dst, srcv=srcv, f=f: e.tensor_scalar(dst, srcv, f, None, ALU.mult), done)
            qk_dve = bank_read[b]

    scores = region(14848, MAPS, 3 * P)
    neg_max = small[:, 16:16 + 2 * MAPS].rearrange("p (t m) -> p t m", t=2)
    sums = small[:, 64:64 + 2 * MAPS].rearrange("p (t m) -> p t m", t=2)
    span = [(SEQ, SEQ + P), (0, SEQ)]
    exp_done = [None] * MAPS
    for m in range(MAPS):
        b = 4 + m % 4
        lo = 64 * (m % 2)

        head = m if m < A_HEADS else A_HEADS + (m - A_HEADS) // 2

        def run(e, i, m=m, b=b, lo=lo, head=head):
            q, k = qk_t[lo:lo + 64, m // 2, :], qk_t[lo:lo + 64, KD + m // 2, :]
            e.matmul(bank[b][:, 0:3 * P], mirror[:, :], bias[:, head, :], start=True, stop=False, skip_group_check=True)
            e.matmul(bank[b][:, 0:SEQ], q[:, P:SEQ], k, start=False, stop=False, skip_group_check=True)
            return e.matmul(bank[b][:, SEQ:SEQ + P], q[:, 0:P], k[:, 0:P], start=False, stop=True,
                            skip_group_check=True)
        done = pe(run, bank_read[b], qk_act, qk_dve, bias_landed, mirror_landed)
        for t in range(NT):
            maxed = dve(lambda e, i, t=t, m=m, b=b: e.tensor_reduce(
                neg_max[:, t, m:m + 1], bank[b][:, span[t][0]:span[t][1]], AX_X, ALU.max, negate=True), done)
        for t in range(NT):
            exp_done[m] = act(lambda e, i, m=m, t=t, b=b: e.activation(
                scores[:, m, span[t][0]:span[t][1]], bank[b][:, span[t][0]:span[t][1]], ACT.Exp,
                bias=neg_max[:, t, m:m + 1], accum_out=sums[:, t, m:m + 1]), maxed)
        bank_read[b] = exp_done[m]
    inverted = dve(lambda e, i: e.reciprocal(sums, sums), exp_done[-1])

    lam_in = sb("lam_in", P, 4, 64)
    lam = small[:, 128:132]
    lam_landed = load(lam_in[:, :, :], a["diff_lambda"][0].partition_broadcast(P))
    l1 = dve(lambda e, i: e.tensor_tensor(lam_in[:, 0::2, :], lam_in[:, 0::2, :], lam_in[:, 1::2, :], ALU.mult),
             lam_landed)
    l2 = dve(lambda e, i: e.tensor_reduce(lam[:, 0:2], lam_in[:, 0::2, :], AX_X, ALU.add), l1)
    l3 = act(lambda e, i: e.activation(lam[:, 0:2], lam[:, 0:2], ACT.Exp), l2)
    l4 = dve(lambda e, i: e.tensor_tensor(lam[:, 2:3], lam[:, 1:2], lam[:, 0:1], ALU.subtract), l3)
    neg_lam = dve(lambda e, i: e.tensor_scalar(lam[:, 3:4], lam[:, 2:3], -LAMBDA_INIT, None, ALU.add), l4)
    b_second = sums[:, :, A_HEADS + 1::2]
    scaled_second = dve(lambda e, i: e.tensor_scalar(b_second, b_second, lam[:, 3:4], None, ALU.mult),
                        neg_lam, inverted)
    for h in range(B_HEADS):
        m0 = A_HEADS + 2 * h
        for t in range(NT):
            p0, p1 = scores[:, m0, span[t][0]:span[t][1]], scores[:, m0 + 1, span[t][0]:span[t][1]]
            s1 = dve(lambda e, i, p1=p1, m0=m0, t=t: e.tensor_scalar(p1, p1, sums[:, t, m0 + 1:m0 + 2], None, ALU.mult),
                     scaled_second)
            combined = dve(lambda e, i, p0=p0, p1=p1, m0=m0, t=t: e.scalar_tensor_tensor(
                p0, p0, sums[:, t, m0:m0 + 1], p1, ALU.mult, ALU.add), s1)

    p_t = region(6144, n_heads, 3, P)
    bias_used = done
    for h in range(n_heads):
        m = h if h < A_HEADS else A_HEADS + 2 * (h - A_HEADS)
        b = 4 + h % 4

        def run(e, i, m=m, b=b):
            for c in range(3):
                last_ = e.transpose(bank[b][:, c * P:(c + 1) * P], scores[:, m, c * P:(c + 1) * P], ident[:, :])
            return last_
        done = pe(run, bank_read[b], exp_done[m] if h < A_HEADS else combined)
        dst, srcv = p_t[:, h, :, :], wide(b, 3)
        if h % 2:
            bank_read[b] = act(lambda e, i, dst=dst, srcv=srcv: e.activation(dst, srcv, ACT.Copy), done, bias_used)
            pt_act = bank_read[b]
        else:
            bank_read[b] = dve(lambda e, i, dst=dst, srcv=srcv: e.tensor_copy(dst, srcv), done, bias_used)
            pt_dve = bank_read[b]

    mixed = normed
    for t in range(NT):
        for kind, (h0, hn, dv, v0) in enumerate(((0, A_HEADS, A_DIM, 1024), (A_HEADS, B_HEADS, B_V, 2560))):
            b = 2 * kind + t

            def run(e, i, t=t, h0=h0, hn=hn, dv=dv, v0=v0, b=b):
                for h in range(hn):
                    o = bank[b][:, h * dv:(h + 1) * dv]
                    blocks = [(2, 0)] if t == 0 else [(0, 0), (1, 1)]
                    for c, key_tile in blocks:
                        last_ = e.matmul(o, p_t[:, h0 + h, c, :], proj[:, key_tile, v0 + h * dv:v0 + (h + 1) * dv],
                                         start=(c == blocks[0][0]), stop=(c == blocks[-1][0]))
                return last_
            done = pe(run, bank_read[b], pt_act, pt_dve)
            dst = mixed[:, t, kind * A_W:kind * A_W + hn * dv].rearrange("p (h d) -> p h d", h=hn)
            srcv = bank[b][:, :].rearrange("p (h d) -> p h d", h=hn)
            if kind == 0:
                r = sums[:, t, 0:A_HEADS].unsqueeze(2).to_broadcast([P, A_HEADS, A_DIM])
                bank_read[b] = dve(lambda e, i, dst=dst, srcv=srcv, r=r: e.tensor_tensor(dst, srcv, r, ALU.mult),
                                   done, normed_read[0])
            else:
                bank_read[b] = dve(lambda e, i, dst=dst, srcv=srcv: e.tensor_copy(dst, srcv), done, normed_read[0])
        mixed_written = bank_read[2 + t]
        ss = small[:, 136 + 5 * t:141 + 5 * t]
        sq = sum_squares(mixed[:, t, 0:A_W], ss[:, 0:1], A_W ** -0.5, mixed_written)
        for h in range(B_HEADS):
            sq = sum_squares(mixed[:, t, A_W + h * B_V:A_W + (h + 1) * B_V], ss[:, 1 + h:2 + h], B_V ** -0.5,
                             mixed_written)
        r = rstd_of("mixed", ss, 1.0, 5, sq)
        na = dve(lambda e, i, t=t, ss=ss: e.tensor_scalar(mixed[:, t, 0:A_W], mixed[:, t, 0:A_W], ss[:, 0:1],
                                                          None, ALU.mult), r)
        part = mixed[:, t, A_W:D].rearrange("p (h d) -> p h d", h=B_HEADS)
        nb = dve(lambda e, i, part=part, ss=ss: e.tensor_tensor(
            part, part, ss[:, 1:5].unsqueeze(2).to_broadcast([P, B_HEADS, B_V]), ALU.mult), r)
        last["mixed%d" % t] = nb
    mix_gain = small[:, 152:160]
    g1 = dve(lambda e, i: e.tensor_copy(mix_gain[:, 0:4], cols[:, stack["moba_out_g"]]), gains)
    sub = cols[:, stack["diff_subln_g"]]
    g2 = dve(lambda e, i: e.tensor_scalar(mix_gain[:, 4:8], sub.to_broadcast([P, B_HEADS]), 1.0 - LAMBDA_INIT, None,
                                          ALU.mult), gains)

    def gained(dst, gain, free, ready):
        def evacuate(b, t, k0, width, done):
            out_ap = dst[:, k0:k0 + width, t * P:(t + 1) * P]
            if gain is None:
                return act(lambda e, i: e.activation(out_ap, wide(b, width), ACT.Copy), done, free)
            g = gain[:, k0:k0 + width].unsqueeze(2).to_broadcast([P, width, P])
            return dve(lambda e, i: e.tensor_tensor(out_ap, wide(b, width), g, ALU.mult), done, free, ready)
        return evacuate
    mixed_t = transposed(lambda t, k: mixed[:, t, k * P:(k + 1) * P], KD, [4, 5, 6, 7],
                         gained(act_t, mix_gain, act_t_free, g2), [last["mixed0"], last["mixed1"]])
    normed_read[0] = bank_read[7]

    def add_to_x(j, t, b, done):
        def run(e, i):
            part = x_res[:, t, bass.ds(j(i) * UNIT, UNIT)]
            return e.tensor_tensor(part, part, bank[b][:, :], ALU.add)
        last["x"] = dve(run, done)
        return last["x"]

    def pe_so_far():
        c = prog.engine_count["tensor"]
        return Done(c, c.value, None)

    linear(2, columns(a["w_out"][0]), act_t, mixed_t, add_to_x)
    x1_ready = last["x"]
    act_t_free = pe_so_far()

    mem_rows = region(0, NT, D)
    mem_landed = load(mem_rows, a["mem"][0].rearrange("(t p) d -> p t d", p=P), act_t_free, engine="sync")
    m_ready = norm_t(mem_rows, mem_t, cols[:, stack["mem_norm_g"]], None, mem_landed, col=2)
    keys = region(2048, NT, D)
    values = region(4096, NT, D)
    queries = region(6144, NT, D)

    def copy_to(dst, key, *after):
        def evacuate(j, t, b, done):
            last[key] = act(lambda e, i: e.activation(dst[:, t, bass.ds(j(i) * UNIT, UNIT)], bank[b][:, :], ACT.Copy),
                            done, *after)
            return last[key]
        return evacuate
    linear(2, columns(a["w_ck"][0]), mem_t, m_ready, copy_to(keys, "keys"))
    linear(2, columns(a["w_cv"][0]), mem_t, m_ready, copy_to(values, "values"))
    c_ready = norm_t(x_res, act_t, cols[:, stack["cross_norm_g"]], act_t_free, x1_ready, col=4)
    linear(2, columns(a["w_cq"][0]), act_t, c_ready, copy_to(queries, "queries"))
    act_t_free = pe_so_far()
    kc_t = region(8192, KD, SEQ)
    qc_t = region(10240, KD, SEQ)
    kt_ready = transposed(lambda t, k: keys[:, t, k * P:(k + 1) * P], KD, [4, 5, 6, 7],
                          gained(kc_t, None, mixed_t, None), last["keys"])
    qt_ready = transposed(lambda t, k: queries[:, t, k * P:(k + 1) * P], KD, [4, 5, 6, 7],
                          gained(qc_t, None, mixed_t, None), last["queries"])
    c_probs = region(12288, M_HEADS, NT, SEQ)
    c_max = small[:, 160:168].rearrange("p (h t) -> p h t", h=M_HEADS)
    c_sum = small[:, 168:176].rearrange("p (h t) -> p h t", h=M_HEADS)
    c_scale = float(M_DIM) ** -0.5
    for h in range(M_HEADS):
        def run(e, i, h=h):
            for t in range(NT):
                for k in range(2):
                    last_ = e.matmul(bank[4 + h][:, t * SEQ:(t + 1) * SEQ], qc_t[:, 2 * h + k, t * P:(t + 1) * P],
                                     kc_t[:, 2 * h + k, :], start=(k == 0), stop=(k == 1))
            return last_
        done = pe(run, bank_read[4 + h], kt_ready, qt_ready)
        view = bank[4 + h][:, :].rearrange("p (t m) -> p t m", t=NT)
        mx = dve(lambda e, i, h=h, view=view: e.tensor_reduce(c_max[:, h, :], view, AX_X, ALU.max, negate=True), done)
        mx = dve(lambda e, i, h=h: e.tensor_scalar(c_max[:, h, :], c_max[:, h, :], c_scale, None, ALU.mult), mx)
        for t in range(NT):
            ex = act(lambda e, i, h=h, t=t, view=view: e.activation(
                c_probs[:, h, t, :], view[:, t, :], ACT.Exp, bias=c_max[:, h, t:t + 1], scale=c_scale,
                accum_out=c_sum[:, h, t:t + 1]), mx, mixed_t)
        bank_read[4 + h] = ex
    c_inv = dve(lambda e, i: e.reciprocal(c_sum, c_sum), ex)
    cp_t = region(8192, M_HEADS, 2, SEQ)
    logits_done = done
    for h in range(M_HEADS):
        def run(e, i, h=h):
            for c in range(2):
                for t in range(NT):
                    last_ = e.transpose(bank[4 + h][:, c * SEQ + t * P:c * SEQ + (t + 1) * P],
                                        c_probs[:, h, t, c * P:(c + 1) * P], ident[:, :])
            return last_
        done = pe(run, bank_read[4 + h])
        bank_read[4 + h] = dve(lambda e, i, h=h: e.tensor_copy(
            cp_t[:, h, :, :], bank[4 + h][:, :].rearrange("p (c t) -> p c t", c=2)), done, logits_done)
    cpt_ready = bank_read[7]
    for t in range(NT):
        for pair in range(2):
            b = 2 * pair + t

            def run(e, i, t=t, pair=pair, b=b):
                for g in range(2):
                    h = 2 * pair + g
                    for c in range(2):
                        last_ = e.matmul(bank[b][:, g * M_DIM:(g + 1) * M_DIM], cp_t[:, h, c, t * P:(t + 1) * P],
                                         values[:, c, h * M_DIM:(h + 1) * M_DIM], start=(c == 0), stop=(c == 1))
                return last_
            done = pe(run, bank_read[b], cpt_ready, last["values"])
            dst = normed[:, t, pair * 512:(pair + 1) * 512].rearrange("p (h d) -> p h d", h=2)
            srcv = bank[b][:, :].rearrange("p (h d) -> p h d", h=2)
            r = c_sum[:, 2 * pair:2 * pair + 2, t].unsqueeze(2).to_broadcast([P, 2, M_DIM])
            bank_read[b] = dve(lambda e, i, dst=dst, srcv=srcv, r=r: e.tensor_tensor(dst, srcv, r, ALU.mult),
                               done, c_inv, normed_read[0])
    oc_ready = bank_read[3]
    oc_t = transposed(lambda t, k: normed[:, t, k * P:(k + 1) * P], KD, [4, 5, 6, 7],
                      gained(act_t, None, act_t_free, None), oc_ready)
    normed_read[0] = bank_read[7]
    linear(2, columns(a["w_co"][0]), act_t, oc_t, add_to_x)
    x2_ready = last["x"]
    act_t_free = pe_so_far()

    f_ready = norm_t(x_res, act_t, cols[:, stack["ffn_norm_g"]], act_t_free, x2_ready, col=6)
    KF = D_FF // P
    HALF = UNIT // 2
    hidden = [region(19968 + s * NT * HALF, NT, HALF) for s in range(2)]
    hidden_t = region(14336, KF, SEQ)
    gate_v = a["w_gate"][0].rearrange("(k p) n -> p k n", p=P)
    up_v = a["w_up"][0].rearrange("(k p) n -> p k n", p=P)

    def gate_up(j):
        return [(lambda slot: slot[:, :, 0:HALF], gate_v[:, :, bass.ds(j * HALF, HALF)]),
                (lambda slot: slot[:, :, HALF:UNIT], up_v[:, :, bass.ds(j * HALF, HALF)])]

    def glu(j, t, b, done):
        s = b // 2
        first_in_body = t == 0
        g = act(lambda e, i: e.activation(hidden[s][:, t, :], bank[b][:, 0:HALF], ACT.Silu), done,
                hidden_read[s])
        u = dve(lambda e, i: e.tensor_tensor(hidden[s][:, t, :], hidden[s][:, t, :], bank[b][:, HALF:UNIT], ALU.mult), g)
        if t == NT - 1:
            tb = 4 + s

            def run(e, i):
                for k in range(2):
                    for tt in range(NT):
                        last_ = e.transpose(bank[tb][:, k * SEQ + tt * P:k * SEQ + (tt + 1) * P],
                                            hidden[s][:, tt, k * P:(k + 1) * P], ident[:, :])
                return last_
            turned = pe(run, u, bank_read[tb])
            hidden_read[s] = turned
            last["hidden"] = act(lambda e, i: e.activation(
                hidden_t[:, bass.ds(j(i) * 2, 2), :], bank[tb][:, :].rearrange("p (k t) -> p k t", k=2), ACT.Copy),
                turned)
            bank_read[tb] = last["hidden"]
        return u

    linear(6, gate_up, act_t, f_ready, glu, side=ada_side(6, False))
    linear(D_FF // HALF - 6, gate_up, act_t, f_ready, glu, first=6)
    ffn_done = last["hidden"]
    act_t_free = pe_so_far()

    down_v = a["w_down"][0].rearrange("(k p) n -> p k n", p=P)
    for r0 in range(0, KF, KD):
        kd = min(KD, KF - r0)
        for half in range(2):
            s = half
            landed = prog.dma("sync", lambda e, i, s=s, kd=kd, r0=r0, half=half: e.dma_start(
                slots[s][:, 0:kd, :], down_v[:, r0:r0 + kd, half * UNIT:(half + 1) * UNIT]), slot_count[s],
                slot_used[s])
            for t in range(NT):
                b = 2 * s + t

                def run(e, i, t=t, b=b, kd=kd, r0=r0, s=s):
                    for k in range(kd):
                        last_ = e.matmul(bank[b][:, :], hidden_t[:, r0 + k, t * P:(t + 1) * P], slots[s][:, k, :],
                                         start=(r0 + k == 0), stop=(r0 + k == KF - 1))
                    return last_
                done = pe(run, landed, bank_read[b], ffn_done)
                if r0 + kd == KF:
                    part = x_res[:, t, half * UNIT:(half + 1) * UNIT]
                    bank_read[b] = dve(lambda e, i, part=part, b=b: e.tensor_tensor(part, part, bank[b][:, :], ALU.add),
                                       done)
                else:
                    bank_read[b] = None
            slot_used[s] = done
    x3_ready = bank_read[3]
    row_g = mod_rows[:, 3, :]
    fin_landed = load(row_g[:, :], a["final_norm_g"].partition_broadcast(P))
    for t in range(NT):
        total = small[:, 8 + t:9 + t]
        sq = sum_squares(x_res[:, t, :], total, 1.0, x3_ready)
        r = rstd_of("final", total, 1.0 / D, 1, sq)
        xf_ready = dve(lambda e, i, t=t, total=total: e.scalar_tensor_tensor(
            x_res[:, t, :], x_res[:, t, :], total, row_g[:, :], ALU.mult, ALU.mult), r, fin_landed)

    before_ctx = everything()
    held = side_slot[:, :, :].rearrange("p k n -> p (k n)")
    masks = held[:, 0:13 * P].rearrange("p (m t) -> p m t", t=P)
    pairs = held[:, 13 * P:21 * P].rearrange("p (m t) -> p m t", t=P)
    states = held[:, 21 * P:29 * P].rearrange("p (d n) -> p d n", d=2)
    masks_landed = load(masks, a["decay_masks"], before_ctx)
    pairs_landed = load(pairs, a["pair_masks"], before_ctx)
    lb = region(20992, 2, GW)
    one_lb = region(22016, 2, GW)
    lb_in = normed[:, :, :].rearrange("p t (l n) -> p t l n", l=2)
    lb_landed = load(lb_in, a["lb_logits_2"].partition_broadcast(P), before_ctx)
    lb_diff = dve(lambda e, i: e.tensor_tensor(lb, lb_in[:, :, 0, :], lb_in[:, :, 1, :], ALU.subtract), lb_landed)
    lb_one = act(lambda e, i: e.activation(one_lb, lb, ACT.Sigmoid, scale=-1.0), lb_diff)
    lb_ready = act(lambda e, i: e.activation(lb, lb, ACT.Sigmoid), lb_one)

    mod_gain = sb("mod_gain", P, 3, KD)
    def modulated(which, scale_cols, gain):
        g = dve(lambda e, i: e.scalar_tensor_tensor(mod_gain[:, which, :], scale_cols, 1.0, cols[:, gain],
                                                    ALU.add, ALU.mult), last["ada"])
        return mod_gain[:, which, :], g
    ctx_rows = region(14336, NT, D)
    ctx_landed = load(ctx_rows, a["ctx_2"][0].rearrange("(t p) d -> p t d", p=P), before_ctx)
    act_t_free = before_ctx
    gain, gain_ready = modulated(0, ctx_cols[:, 1, :], stack["g_pre_mix_2"])
    ctx_t = norm_t(ctx_rows, mem_t, gain, Both(before_ctx, gain_ready), ctx_landed, lb_diff,
                   shift=ctx_cols[:, 0, :], col=8)
    pc = region(16384, NT, 3 * GW)
    linear(3, columns(a["w_in_2"][0], n0=GW), mem_t, ctx_t, copy_to(pc, "pc"))
    lf_c = region(14336, NT, 2 * GW)

    def gates(z, lf, omb, lbv, ready):
        s1 = act(lambda e, i: e.activation(lf, z, ACT.Sigmoid), ready)
        s2 = act(lambda e, i: e.activation(z, z, ACT.Sigmoid, scale=-1.0), s1)
        f1 = dve(lambda e, i: e.tensor_tensor(lf, lf, omb, ALU.mult), s1, lb_ready)
        f2 = dve(lambda e, i: e.tensor_tensor(lf, lf, lbv, ALU.add), f1)
        lf_ready = act(lambda e, i: e.activation(lf, lf, ACT.Ln), f2)
        k_ready = dve(lambda e, i: e.tensor_tensor(z, z, omb, ALU.mult), s2)
        return lf_ready, k_ready
    lb_flat = region(20992, 2 * GW)
    one_flat = region(22016, 2 * GW)
    for t in range(NT):
        lfc_ready, kc_ready = gates(pc[:, t, 0:2 * GW], lf_c[:, t, :], one_flat, lb_flat, Both(last["pc"], ctx_t))
    kw = normed[:, :, :]
    kw_free = ctx_t
    for d in range(2):
        strict = masks[:, (MASK_GT, MASK_LT)[d], :]
        for t in range(NT):
            b = 4 + 2 * d + t

            def run(e, i, d=d, t=t, b=b, strict=strict):
                own = lf_c[:, t, d * GW:(d + 1) * GW]
                other = lf_c[:, 1 - t, d * GW:(d + 1) * GW]
                crossing = t == d
                mm = e.matmul(bank[b][:, :], strict, own, start=True, stop=not crossing)
                if crossing:
                    mm = e.matmul(bank[b][:, :], masks[:, MASK_ALL, :], other, start=False, stop=True)
                return mm
            done = pe(run, bank_read[b], lfc_ready, masks_landed)
            dst = kw[:, t, d * GW:(d + 1) * GW]
            ex = act(lambda e, i, dst=dst, b=b: e.activation(dst, bank[b][:, :], ACT.Exp), done, kw_free)
            bank_read[b] = ex
            kw_ready = dve(lambda e, i, dst=dst, d=d, t=t: e.tensor_tensor(
                dst, dst, pc[:, t, d * GW:(d + 1) * GW], ALU.mult), ex, kc_ready)
    for d in range(2):
        b = 4 + d

        def run(e, i, d=d, b=b):
            for h in range(GH):
                for t in range(NT):
                    mm = e.matmul(bank[b][:, h * P:(h + 1) * P], kw[:, t, d * GW + h * P:d * GW + (h + 1) * P],
                                  pc[:, t, 2 * GW + h * P:2 * GW + (h + 1) * P], start=(t == 0), stop=(t == NT - 1))
            return mm
        done = pe(run, bank_read[b], kw_ready)
        states_ready = bank_read[b] = act(lambda e, i, d=d, b=b: e.activation(states[:, d, :], bank[b][:, :], ACT.Copy),
                                          done)
    normed_read[0] = done
    ctx_done = everything()

    p2 = region(0, IN2 // UNIT, NT, UNIT)
    before_lat = everything()
    gain, gain_ready = modulated(1, mod_cols[:, 1, :], stack["g_pre_mix_2"])
    lat_t = norm_t(x_res, act_t, gain, Both(act_t_free, gain_ready), xf_ready, shift=mod_cols[:, 0, :], col=10)

    def to_p2(j, t, b, done):
        last["p2"] = act(lambda e, i: e.activation(p2[:, bass.ds(j(i), 1), t, :], bank[b][:, :].unsqueeze(1), ACT.Copy),
                         done, before_lat)
        return last["p2"]
    linear(IN2 // UNIT, columns(a["w_in_2"][0]), act_t, lat_t, to_p2)
    act_t_free = pe_so_far()

    lf = region(11264, 2, NT, GW)
    for d in range(2):
        for t in range(NT):
            lf_ready, k_ready = gates(p2[:, 1 + d, t, :], lf[:, d, t, :], one_lb[:, d, :], lb[:, d, :], last["p2"])
    flat2 = "p u t n -> p (u t n)"
    gates_out = act(lambda e, i: e.activation(p2[:, 7:11, :, :].rearrange(flat2), p2[:, 7:11, :, :].rearrange(flat2),
                                              ACT.Sigmoid), last["p2"])
    q_ready = act(lambda e, i: e.activation(p2[:, 0, :, :], p2[:, 0, :, :], ACT.Silu), last["p2"])
    g_ready = act(lambda e, i: e.activation(p2[:, 4, :, :], p2[:, 4, :, :], ACT.Silu), last["p2"])
    cm_ready = act(lambda e, i: e.activation(p2[:, 5:7, :, :].rearrange(flat2), p2[:, 5:7, :, :].rearrange(flat2),
                                             ACT.Gelu_apprx_tanh), last["p2"])
    q_t = region(13312, GH, SEQ)
    k_t = region(14336, 2, GH, SEQ)
    qt_ready = transposed(lambda t, k: p2[:, 0, t, k * P:(k + 1) * P], GH, [4, 5], gained(q_t, None, before_lat, None),
                          q_ready)
    for d in range(2):
        kt_ready = transposed(lambda t, k, d=d: p2[:, 1 + d, t, k * P:(k + 1) * P], GH, [6, 7],
                              gained(k_t[:, d, :, :], None, before_lat, None), k_ready)
    turned = pe_so_far()
    factors = region(16384, NT, GH, LOCAL_LEVELS, P)
    key0 = region(0, NT, GH, P)
    edge = [region(1024, GH, 4, P),
            act_t[:, :, :].rearrange("p k t -> p (k t)").rearrange("p (h b t) -> p h b t", h=GH, b=4)]
    near_far = mem_t[:, :, :].rearrange("p k t -> p (k t)").rearrange("p (a h t) -> p a h t", a=4, h=GH)
    inside, across = near_far[:, 0:2, :, :], near_far[:, 2:4, :, :]
    inside0 = normed[:, 0, 0:GH * P].rearrange("p (h t) -> p h t", h=GH)
    cleared = dve(lambda e, i: e.memset(inside, 0.0), ctx_done)
    factors_free = before_lat
    for d in range(2):
        near, far = d, 1 - d
        first_mask, second_mask = ((MASK_GT, MASK_LE), (MASK_LT, MASK_GE))[d]
        for h in range(GH):
            b = 4 + h % 4
            hs = slice(h * P, (h + 1) * P)

            def run(e, i, b=b, hs=hs, d=d, near=near, far=far, first_mask=first_mask, second_mask=second_mask):
                e.matmul(bank[b][:, 0:2 * P], lf[:, d, near, hs],
                         masks[:, first_mask:second_mask + 1, :].rearrange("p m t -> p (m t)"), start=True, stop=True)
                e.matmul(bank[b][:, 2 * P:3 * P], lf[:, d, far, hs], masks[:, second_mask, :], start=True, stop=True)
                e.matmul(bank[b][:, 3 * P:4 * P], lf[:, d, far, hs], masks[:, second_mask, :], start=True, stop=False)
                return e.matmul(bank[b][:, 3 * P:4 * P], lf[:, d, near, hs], masks[:, MASK_ALL, :], start=False,
                                stop=True)
            done = pe(run, bank_read[b], lf_ready)
            ex = bank_read[b] = act(lambda e, i, b=b, h=h, d=d: e.activation(
                edge[d][:, h, :, :], bank[b][:, :].rearrange("p (c t) -> p c t", c=4), ACT.Exp), done, turned)
        for part, (src, tile) in enumerate(((k_t[:, d], near), (q_t, near), (q_t, far), (q_t, far))):
            v = edge[d][:, :, part, :]
            o = src[:, :, tile * P:(tile + 1) * P]
            edge_ready = dve(lambda e, i, v=v, o=o: e.tensor_tensor(v, v, o, ALU.mult), ex, qt_ready, kt_ready)
        for t in range(NT):
            for h in range(GH):
                b = 4 + h % 4
                done = pe(lambda e, i, b=b, h=h, d=d, t=t: e.matmul(
                    bank[b][:, :], lf[:, d, t, h * P:(h + 1) * P],
                    masks[:, LOCAL_LEVELS * d:LOCAL_LEVELS * (d + 1), :].rearrange("p l t -> p (l t)"),
                    start=True, stop=True), bank_read[b], lf_ready)
                act(lambda e, i, b=b, h=h, t=t: e.activation(
                    factors[:, t, h, :, :], bank[b][:, :].rearrange("p (l t) -> p l t", l=LOCAL_LEVELS), ACT.Exp),
                    done, factors_free)
                ex = bank_read[b] = act(lambda e, i, b=b, h=h, t=t: e.activation(
                    key0[:, t, h, :], bank[b][:, 0:P], ACT.Exp, scale=-1.0), done, turned, factors_free)
            qv, kv = q_t[:, :, t * P:(t + 1) * P], k_t[:, d, :, t * P:(t + 1) * P]
            f0 = factors[:, t, :, 0, :]
            dve(lambda e, i, f0=f0, qv=qv: e.tensor_tensor(f0, f0, qv, ALU.mult), ex, qt_ready)
            ready = dve(lambda e, i, kv=kv, t=t: e.tensor_tensor(key0[:, t], key0[:, t], kv, ALU.mult), ex, kt_ready)
            for level in range(1, LOCAL_LEVELS):
                size = SCAN_CHUNK << level
                halves = lambda v, size=size: v.rearrange("p h (n r c) -> p h n r c", r=2, c=size // 2)
                fv = halves(factors[:, t, :, level, :])
                for role, operand in ((1 - d, qv), (d, kv)):
                    x, y = fv[:, :, :, role, :], halves(operand)[:, :, :, role, :]
                    ready = dve(lambda e, i, x=x, y=y: e.tensor_tensor(x, x, y, ALU.mult), ex, qt_ready, kt_ready)
            for level in range(LOCAL_LEVELS):
                b = level

                def run(e, i, b=b, t=t, level=level):
                    for h in range(GH):
                        keys_ = key0[:, t, h, :] if level == 0 else factors[:, t, h, level, :]
                        mm = e.matmul(bank[b][:, h * P:(h + 1) * P], keys_, factors[:, t, h, level, :],
                                      start=True, stop=True)
                    return mm
                done = pe(run, bank_read[b], ready)
                mask = pairs[:, LOCAL_LEVELS * d + level, :].bitcast(I32).unsqueeze(1).to_broadcast([P, GH, P])
                srcv = bank[b][:, :].rearrange("p (h t) -> p h t", h=GH)
                if d == 1 and level == 0:
                    c0 = dve(lambda e, i: e.memset(inside0, 0.0), normed_free if t == 0 else added)
                    c1 = dve(lambda e, i, mask=mask, srcv=srcv: e.copy_predicated(inside0, mask, srcv), done, c0,
                             pairs_landed)
                    bank_read[b] = c1
                    added = dve(lambda e, i, t=t: e.tensor_tensor(inside[:, t], inside[:, t], inside0, ALU.add), c1,
                                inside_ready)
                    inside_ready = added
                else:
                    inside_ready = bank_read[b] = dve(lambda e, i, mask=mask, srcv=srcv, t=t: e.copy_predicated(
                        inside[:, t], mask, srcv), done, cleared, pairs_landed,
                        inside_ready if (d, t, level) != (0, 0, 0) else None)
        factors_free = pe_so_far()
        normed_free = factors_free

        def run(e, i, d=d):
            for h in range(GH):
                mm = e.matmul(bank[4 + d][:, h * P:(h + 1) * P], edge[d][:, h, 0, :], edge[d][:, h, 2, :],
                              start=True, stop=True)
            return mm
        done = pe(run, bank_read[4 + d], edge_ready)
        across_ready = bank_read[4 + d] = act(lambda e, i, d=d: e.activation(
            across[:, d], bank[4 + d][:, :].rearrange("p (h t) -> p h t", h=GH), ACT.Copy), done, ctx_done)
    value = p2[:, 3, :, :]
    rec = normed
    rec_sum = small[:, 180:188].rearrange("p (t h) -> p t h", t=NT)
    for t in range(NT):
        def run(e, i, t=t):
            for h in range(GH):
                o, hs = bank[t][:, h * P:(h + 1) * P], slice(h * P, (h + 1) * P)
                e.matmul(o, inside[:, t, h, :], value[:, t, hs], start=True, stop=False)
                e.matmul(o, across[:, 1 - t, h, :], value[:, 1 - t, hs], start=False, stop=False)
                for d in range(2):
                    mm = e.matmul(o, edge[d][:, h, 1 if d == t else 3, :], states[:, d, hs], start=False, stop=(d == 1))
            return mm
        done = pe(run, bank_read[t], inside_ready, across_ready, states_ready)
        for h in range(GH):
            ss = sum_squares(bank[t][:, h * P:(h + 1) * P], rec_sum[:, t, h:h + 1], P ** -0.5, done)
        r = rstd_of("rec", rec_sum[:, t, :], 1.0, GH, ss)
        m1 = bank_read[t] = dve(lambda e, i, t=t: e.tensor_tensor(
            rec[:, t, 0:GW].rearrange("p (h d) -> p h d", h=GH), bank[t][:, :].rearrange("p (h d) -> p h d", h=GH),
            rec_sum[:, t, :].unsqueeze(2).to_broadcast([P, GH, P]), ALU.mult), r, inside_ready)
        m2 = dve(lambda e, i, t=t: e.tensor_tensor(rec[:, t, 0:GW], rec[:, t, 0:GW], p2[:, 4, t, :], ALU.mult), m1,
                 g_ready)
    rec_t = region(16384, GH, SEQ)
    hgrn = small[:, 188:192]
    hg = dve(lambda e, i: e.tensor_copy(hgrn, cols[:, stack["g_hgrn_out_2"]].to_broadcast([P, GH])), gains)
    rec_t_ready = transposed(lambda t, k: rec[:, t, k * P:(k + 1) * P], GH, [4, 5],
                             gained(rec_t, hgrn, factors_free, hg), m2)

    ln_rows = mod_rows[:, 4, :].rearrange("p (a n) -> p a n", a=2)
    ln_landed = Both(load(ln_rows[:, 0, :], a["cm_ln_g_2"][0].partition_broadcast(P), before_lat),
                     load(ln_rows[:, 1, :], a["cm_ln_b_2"][0].partition_broadcast(P), before_lat))
    b_sp = sb("b_sp", P, 4)
    ws = ada_acc[:, 0, :].rearrange("p (g q) -> p g q", g=4)
    ws_t = ada_acc[:, 1, :].rearrange("p (g q) -> p g q", g=4)
    b_sp_landed = load(b_sp[:, :], a["b_spatial_2"][0])
    ws_landed = load(ws, a["w_spatial_2"][0].rearrange("g p q -> p g q"), before_lat)

    def run(e, i):
        for g in range(4):
            mm = e.transpose(bank[6][:, g * P:(g + 1) * P], ws[:, g, :], ident[:, :])
        return mm
    done = pe(run, bank_read[6], ws_landed)
    ws_ready = bank_read[6] = act(lambda e, i: e.activation(ws_t, bank[6][:, :].rearrange("p (g q) -> p g q", g=4),
                                                            ACT.Copy), done)
    cm_stat = small[:, 192:200]
    for t in range(NT):
        v, u = p2[:, 6, t, :], p2[:, 5, t, :]
        mean, var = cm_stat[:, 2 * t:2 * t + 1], cm_stat[:, 2 * t + 1:2 * t + 2]
        s1 = dve(lambda e, i, v=v, mean=mean: e.tensor_reduce(mean, v, AX_X, ALU.add), cm_ready)
        s2 = dve(lambda e, i, mean=mean: e.tensor_scalar(mean, mean, 1.0 / GW, None, ALU.mult), s1)
        s3 = dve(lambda e, i, v=v, mean=mean: e.tensor_scalar(v, v, mean, None, ALU.subtract), s2)
        s4 = sum_squares(v, var, GW ** -0.5, s3)
        s5 = rstd_of("cm", var, 1.0, 1, s4)
        s6 = dve(lambda e, i, v=v, var=var: e.scalar_tensor_tensor(v, v, var, ln_rows[:, 0, :], ALU.mult, ALU.mult),
                 s5, ln_landed)
        s7 = dve(lambda e, i, v=v: e.tensor_tensor(v, v, ln_rows[:, 1, :], ALU.add), s6)

        def run(e, i, t=t, v=v):
            for g in range(4):
                mm = e.matmul(bank[2 + t][:, g * P:(g + 1) * P], ws_t[:, g, :], v[:, g * P:(g + 1) * P], start=True,
                              stop=True)
            return mm
        done = pe(run, bank_read[2 + t], s7, ws_ready)
        for g in range(4):
            part = u[:, g * P:(g + 1) * P]
            gated = dve(lambda e, i, part=part, g=g, t=t: e.scalar_tensor_tensor(
                part, bank[2 + t][:, g * P:(g + 1) * P], b_sp[:, g:g + 1], part, ALU.add, ALU.mult), done, cm_ready, b_sp_landed)
        bank_read[2 + t] = gated
    gate_t = region(17408, GH, SEQ)
    gate_t_ready = transposed(lambda t, k: p2[:, 5, t, k * P:(k + 1) * P], GH, [6, 7],
                              gained(gate_t, None, factors_free, None), gated)

    merged = region(18432, NT, D)
    wide_slot = [s_[:, :, :].rearrange("p k n -> p (k n)").rearrange("p (k n) -> p k n", k=4) for s_ in slots]
    for s, (name, left, ready) in enumerate((("w_branch_a_2", rec_t, rec_t_ready), ("w_branch_b_2", gate_t, gate_t_ready))):
        landed = prog.dma("sync", lambda e, i, s=s, name=name: e.dma_start(
            wide_slot[s], a[name][0].rearrange("(k p) n -> p k n", p=P)), slot_count[s], slot_used[s])
        for t in range(NT):
            for half in range(2):
                b = 4 * s + 2 * t + half

                def run(e, i, s=s, t=t, half=half, b=b, left=left):
                    for k in range(4):
                        mm = e.matmul(bank[b][:, :], left[:, k, t * P:(t + 1) * P],
                                      wide_slot[s][:, k, half * UNIT:(half + 1) * UNIT], start=(k == 0), stop=(k == 3))
                    return mm
                done = pe(run, landed, bank_read[b], ready)
                dst = merged[:, t, half * UNIT:(half + 1) * UNIT]
                g = p2[:, 7 + 2 * s + half, t, :]
                if s == 0:
                    first_done = bank_read[b] = dve(lambda e, i, dst=dst, b=b, g=g: e.tensor_tensor(
                        dst, bank[b][:, :], g, ALU.mult), done, gates_out, factors_free)
                else:
                    m = bank_read[b] = dve(lambda e, i, b=b, g=g: e.tensor_tensor(g, bank[b][:, :], g, ALU.mult),
                                           done, gates_out)
                    merged_ready = dve(lambda e, i, dst=dst, g=g: e.tensor_tensor(dst, dst, g, ALU.add), m, first_done)
        slot_used[s] = done
    merged_t = transposed(lambda t, k: merged[:, t, k * P:(k + 1) * P], KD, [4, 5, 6, 7],
                          gained(act_t, None, pe_so_far(), None), merged_ready)
    y2 = region(0, NT, D)
    y2_free = pe_so_far()
    linear(2, columns(a["w_out_2"][0]), act_t, merged_t, copy_to(y2, "y2", y2_free))
    act_t_free = pe_so_far()

    def gated_rows(which, name, *after):
        landed = load(row_g[:, :], a[name][0].partition_broadcast(P), *after)
        return dve(lambda e, i: e.tensor_tensor(mod_rows[:, which, :], mod_rows[:, which, :], row_g[:, :], ALU.mult),
                   landed)
    post1 = gated_rows(2, "g_post_mix_2", xf_ready)
    for t in range(NT):
        total = small[:, 200 + t:201 + t]
        sq = sum_squares(y2[:, t, :], total, D ** -0.5, last["y2"])
        r = rstd_of("post", total, 1.0, 1, sq)
        m = dve(lambda e, i, t=t, total=total: e.scalar_tensor_tensor(
            y2[:, t, :], y2[:, t, :], total, mod_rows[:, 2, :], ALU.mult, ALU.mult), r, post1)
        x5_ready = dve(lambda e, i, t=t: e.tensor_tensor(x_res[:, t, :], x_res[:, t, :], y2[:, t, :], ALU.add), m)
    post2 = gated_rows(5, "g_post_ffn_2", post1)

    gain, gain_ready = modulated(2, mod_cols[:, 4, :], stack["g_pre_ffn_2"])
    h2_ready = norm_t(x_res, act_t, gain, Both(act_t_free, gain_ready), x5_ready, shift=mod_cols[:, 3, :], col=12)
    w_router = region(4096, KD, N_EXP)
    router_landed = load(w_router, a["w_router_2"][0].rearrange("(k p) n -> p k n", p=P), y2_free)
    r_bias = region(4608, N_EXP)
    bias_r_landed = load(r_bias, a["b_router_2"][0].partition_broadcast(P), y2_free)
    lower = sb("lower", P, N_GROUPS, N_GROUPS)
    lo0 = pool(lambda e, i: e.memset(lower[:, :, :], 1.0))
    lower_ready = pool(lambda e, i: e.affine_select(out=lower[:, :, :], in_=lower[:, :, :],
                                                    pattern=[[1, N_GROUPS], [-1, N_GROUPS]], compare_op=ALU.is_gt,
                                                    fill=0.0, base=0, channel_multiplier=0), lo0)
    route = region(4672, NT, N_EXP)
    GE = N_EXP // N_GROUPS
    for t in range(NT):
        base = 4800 + t * 600
        score, sel = region(base, N_EXP), region(base + 64, N_EXP)
        top = region(base + 128, N_GROUPS, 8)
        grp, gsel = region(base + 192, N_GROUPS), region(base + 200, N_GROUPS)
        cmp_, eq = region(base + 208, N_GROUPS, N_GROUPS), region(base + 272, N_GROUPS, N_GROUPS)
        best, left_ = region(base + 336, 8), region(base + 344, N_EXP)
        tot = region(base + 408, 2)
        b = t

        def run(e, i, t=t, b=b):
            for k in range(KD):
                mm = e.matmul(bank[b][:, 0:N_EXP], act_t[:, k, t * P:(t + 1) * P], w_router[:, k, :], start=(k == 0),
                              stop=(k == KD - 1))
            return mm
        done = pe(run, bank_read[b], h2_ready, router_landed)
        sc = bank_read[b] = act(lambda e, i, b=b, score=score: e.activation(score, bank[b][:, 0:N_EXP], ACT.Sigmoid), done,
                                y2_free)
        c = dve(lambda e, i, sel=sel, score=score: e.tensor_tensor(sel, score, r_bias, ALU.add), sc, bias_r_landed)
        for g in range(N_GROUPS):
            tp = dve(lambda e, i, g=g, top=top, sel=sel: e.max(top[:, g, :], sel[:, g * GE:(g + 1) * GE]), c)
        c = dve(lambda e, i, grp=grp, top=top: e.tensor_tensor(grp, top[:, :, 0], top[:, :, 1], ALU.add), tp)
        mine = grp.unsqueeze(2).to_broadcast([P, N_GROUPS, N_GROUPS])
        others = grp.unsqueeze(1).to_broadcast([P, N_GROUPS, N_GROUPS])
        c1 = dve(lambda e, i, cmp_=cmp_, mine=mine, others=others: e.tensor_tensor(cmp_, others, mine, ALU.is_gt), c)
        c2 = dve(lambda e, i, eq=eq, mine=mine, others=others: e.tensor_tensor(eq, others, mine, ALU.is_equal), c)
        c2 = dve(lambda e, i, eq=eq: e.tensor_tensor(eq, eq, lower[:, :, :], ALU.mult), c2, lower_ready)
        c1 = dve(lambda e, i, cmp_=cmp_, eq=eq: e.tensor_tensor(cmp_, cmp_, eq, ALU.add), c1, c2)
        c1 = dve(lambda e, i, gsel=gsel, cmp_=cmp_: e.tensor_reduce(gsel, cmp_, AX_X, ALU.add), c1)
        c1 = dve(lambda e, i, gsel=gsel: e.tensor_scalar(gsel, gsel, TOPK_GROUPS - 0.5, None, ALU.is_lt), c1)
        by_group = lambda v: v.rearrange("p (g e) -> p g e", g=N_GROUPS)
        gm = gsel.unsqueeze(2).to_broadcast([P, N_GROUPS, GE])
        c1 = dve(lambda e, i, sel=by_group(sel), gm=gm: e.tensor_tensor(sel, sel, gm, ALU.mult), c1)
        c2 = dve(lambda e, i, grp=grp, gsel=gsel: e.tensor_scalar(grp, gsel, -NEG_INF, NEG_INF, ALU.mult, ALU.add), c1)
        low = grp.unsqueeze(2).to_broadcast([P, N_GROUPS, GE])
        c1 = dve(lambda e, i, sel=by_group(sel), low=low: e.tensor_tensor(sel, sel, low, ALU.add), c2)
        c1 = dve(lambda e, i, best=best, sel=sel: e.max(best, sel), c1)
        c1 = dve(lambda e, i, left_=left_, best=best, sel=sel: e.match_replace(left_, best, sel, 2 * NEG_INF), c1)
        c1 = dve(lambda e, i, left_=left_, sel=sel: e.tensor_tensor(left_, left_, sel, ALU.not_equal), c1)
        c1 = dve(lambda e, i, left_=left_, score=score: e.tensor_tensor(left_, left_, score, ALU.mult), c1)
        c1 = dve(lambda e, i, left_=left_, tot=tot: e.tensor_reduce(tot[:, 0:1], left_, AX_X, ALU.add), c1)
        c1 = dve(lambda e, i, tot=tot: e.reciprocal(tot[:, 1:2], tot[:, 0:1]), c1)
        routed = dve(lambda e, i, left_=left_, tot=tot, t=t: e.tensor_scalar(
            route[:, t, :], left_, tot[:, 1:2], ROUTED_SCALE, ALU.mult, ALU.mult), c1)

    exp_act = [region(6144 + s * NT * D_EXP, NT, D_EXP) for s in range(2)]
    exp_t = [region(7168 + s * 2 * SEQ, 2, SEQ) for s in range(2)]
    down_slot = [side_slot[:, 4 * s:4 * s + 4, :].rearrange("p k n -> p (k n)").rearrange("p (k n) -> p k n", k=2)
                 for s in range(2)]
    down_count = [prog.count(f"down{s}_landed") for s in range(2)]
    exp_used = {"act0": None, "act1": None, "t0": None, "t1": None, "down0": everything(), "down1": everything()}
    exp_ready = {"t0": None, "t1": None, "down0": None, "down1": None}
    prog.carried += [exp_used, exp_ready]
    zeros = region(8192, P)
    z = dve(lambda e, i: e.memset(zeros, 0.0), y2_free)

    def clear(e, i):
        for b in range(4):
            mm = e.matmul(bank[b][:, :], zeros, lb_zero, start=True, stop=False, skip_group_check=True)
        return mm
    lb_zero = region(18432, UNIT)
    acc_clear = pe(clear, z, bank_read[0], bank_read[1], bank_read[2], bank_read[3], merged_ready)
    gu_v = a["w_expert_gu_2"][0].rearrange("e (k p) n -> e p k n", p=P)
    dn_v = a["w_expert_down_2"][0].rearrange("e (k p) n -> e p k n", p=P)

    def expert(s, shared, with_down=True, with_gu=True, final=False):
        if with_gu:
            if shared:
                gu_src = lambda i: a["w_shared_gu_2"][0].rearrange("(k p) n -> p k n", p=P)
                dn_src = lambda i: a["w_shared_down_2"][0].rearrange("(k p) n -> p k n", p=P)
            else:
                gu_src = lambda i: gu_v[bass.ds(2 * i + s, 1)].rearrange("e p k n -> p (e k) n")
                dn_src = lambda i: dn_v[bass.ds(2 * i + s, 1)].rearrange("e p k n -> p (e k) n")
            gu_landed = prog.dma("sync", lambda e, i: e.dma_start(slots[s][:, :, :], gu_src(i)), slot_count[s],
                                 slot_used[s])
            exp_ready[f"down{s}"] = prog.dma("sync", lambda e, i: e.dma_start(down_slot[s], dn_src(i)), down_count[s],
                                             exp_used[f"down{s}"])
            for t in range(NT):
                b = 4 + t

                def run(e, i, t=t, b=b):
                    for k in range(KD):
                        mm = e.matmul(bank[b][:, :], act_t[:, k, t * P:(t + 1) * P], slots[s][:, k, :],
                                      start=(k == 0), stop=(k == KD - 1))
                    return mm
                done = pe(run, gu_landed, bank_read[b], h2_ready)
                g = act(lambda e, i, t=t, b=b: e.activation(exp_act[s][:, t, :], bank[b][:, 0:D_EXP], ACT.Silu), done,
                        exp_used[f"act{s}"])
                u = bank_read[b] = dve(lambda e, i, t=t, b=b: e.scalar_tensor_tensor(
                    exp_act[s][:, t, :], exp_act[s][:, t, :],
                    1.0 if shared else route[:, t, bass.ds(2 * i + s, 1)], bank[b][:, D_EXP:2 * D_EXP],
                    ALU.mult, ALU.mult), g, routed)
            slot_used[s] = done
        if with_down:
            o = 1 - s

            def run(e, i):
                for t in range(NT):
                    for half in range(2):
                        for k in range(2):
                            mm = e.matmul(bank[2 * t + half][:, :], exp_t[o][:, k, t * P:(t + 1) * P],
                                          down_slot[o][:, k, half * UNIT:(half + 1) * UNIT], start=False,
                                          stop=final, skip_group_check=True)
                return mm
            done = pe(run, exp_ready[f"t{o}"], exp_ready[f"down{o}"], acc_clear)
            exp_used[f"down{o}"] = exp_used[f"t{o}"] = done
        if with_gu:
            tb = 6 + s

            def run(e, i):
                for k in range(2):
                    for t in range(NT):
                        mm = e.transpose(bank[tb][:, k * SEQ + t * P:k * SEQ + (t + 1) * P],
                                         exp_act[s][:, t, k * P:(k + 1) * P], ident[:, :])
                return mm
            done_t = pe(run, u, bank_read[tb])
            exp_used[f"act{s}"] = done_t
            exp_ready[f"t{s}"] = bank_read[tb] = act(lambda e, i: e.activation(
                exp_t[s], bank[tb][:, :].rearrange("p (k t) -> p k t", k=2), ACT.Copy), done_t, exp_used[f"t{s}"])
        return done

    expert(1, True, with_down=False)
    prog.begin(N_EXP // 2)
    expert(0, False)
    expert(1, False)
    prog.end()
    experts_done = expert(0, False, with_gu=False, final=True)

    totals = small[:, 204:208].rearrange("p (t h) -> p t h", t=NT)
    y3 = normed
    for t in range(NT):
        for half in range(2):
            sq = sum_squares(bank[2 * t + half][:, :], totals[:, t, half:half + 1], D ** -0.5, experts_done)
        s1 = dve(lambda e, i, t=t: e.tensor_tensor(totals[:, t, 0:1], totals[:, t, 0:1], totals[:, t, 1:2], ALU.add), sq)
        r = rstd_of("post2", totals[:, t, 0:1], 1.0, 1, s1)
        for half in range(2):
            cs = slice(half * UNIT, (half + 1) * UNIT)
            m = dve(lambda e, i, t=t, half=half, cs=cs: e.scalar_tensor_tensor(
                y3[:, t, cs], bank[2 * t + half][:, :], totals[:, t, 0:1], mod_rows[:, 5, cs], ALU.mult, ALU.mult), r,
                post2)
            final = dve(lambda e, i, t=t, cs=cs: e.tensor_tensor(y3[:, t, cs], y3[:, t, cs], x_res[:, t, cs], ALU.add), m)
        stored = load(out[0, t * P:(t + 1) * P, :], y3[:, t, :], final, engine="sync", count=out_count)
    prog.put("sync", lambda e, i: e.nop(), [stored])
    with nc.Block() as block:
        prog.emit(block)


def kernel(**inputs):
    import concourse.bacc as bacc
    from concourse.bass_utils import run_bass_kernel_spmd

    arrays = {name: np.ascontiguousarray(value) for name, value in inputs.items()}
    seq = arrays["x"].shape[1]
    arrays["ident"] = np.eye(P, dtype=np.float32)
    arrays["mirror"] = np.eye(P, dtype=np.float32)[::-1].copy()
    arrays["bucket_rows"] = bucket_rows(seq)
    arrays["decay_masks"] = decay_masks()
    arrays["pair_masks"] = pair_masks()
    nc = bacc.Bacc("TRN2", target_bir_lowering=False, num_devices=1)
    views = {name: nc.dram_tensor(f"in_{name}", value.shape, F32, kind="ExternalInput").ap()
             for name, value in arrays.items()}
    out = nc.dram_tensor("out", list(arrays["x"].shape), F32, kind="ExternalOutput").ap()
    scratch_bias = nc.dram_tensor("scratch_bias", [12, 2 * seq], F32, kind="Internal").ap()
    build_program(nc, views, out, scratch_bias)
    results = run_bass_kernel_spmd(nc, [{f"in_{name}": value for name, value in arrays.items()}], core_ids=[0])
    return results.results[0]["out"]
```

```python
import math
from contextlib import ExitStack

import concourse.bass as bass
from concourse import mybir
import numpy as np

F32 = mybir.dt.float32
I32 = mybir.dt.int32
ALU = mybir.AluOpType
ACT = mybir.ActivationFunctionType
AX_X = mybir.AxisListType.X

P = 128
EPS = 1e-6
NEG_INF = -1e30
LOCAL_LEVELS = 4
SCAN_CHUNK = 16
REL_BUCKETS, REL_MAX_DIST = 32, 128
LAMBDA_INIT = 0.8 - 0.6 * math.exp(-0.3 * 0)
ROUTED_SCALE = 2.5
TOP_K, TOPK_GROUPS, N_GROUPS = 8, 4, 8
SLOTS = 64
TESTED_MAX = 1 << 12



class Count:

    def __init__(self, sem):
        self.sem, self.value = sem, 0


class Done:

    def __init__(self, count, value, loop):
        self.count, self.value, self.loop = count, value, loop


class Before:

    done = None


class Both:

    def __init__(self, *moments):
        self.moments = []
        for m in moments:
            self.moments += m.moments if isinstance(m, Both) else [m]


def flat(moments):
    return [m for m in Both(*moments).moments if m is not None]


class Loop:
    def __init__(self, n):
        self.n, self.start, self.step = n, {}, {}


class Branch:
    def __init__(self, value, limit, start):
        self.value, self.limit, self.start, self.queues, self.skipped = value, limit, start, {}, {}


def flat_queue(queue, engine=None):
    for entry in queue:
        if isinstance(entry, Branch):
            yield from flat_queue(entry.queues[engine], engine)
        else:
            yield entry


class Program:

    def __init__(self, nc, ctx):
        self.nc, self.ctx = nc, ctx
        self.counts, self.carried, self.loop, self.branches = [], [], None, []
        self.queues = {e: [] for e in ("sync", "scalar", "vector", "gpsimd", "tensor")}
        self.engine_count = {e: self.count(f"done_{e}") for e in self.queues}

    def count(self, name):
        self.counts.append(Count(self.ctx.enter_context(self.nc.semaphore(name))))
        return self.counts[-1]

    def put(self, engine, fn, after=(), count=None, by=1):
        count = count or self.engine_count[engine]
        if self.loop is not None:
            assert count in self.loop.start, "made before the loop"
        count.value += by
        self.queue_of(engine).append((fn, flat(after), count, by))
        return Done(count, count.value, self.loop)

    def queue_of(self, engine):
        if self.branches:
            return self.branches[-1].queues[engine]
        return self.queues[engine] if self.loop is None else self.loop.queues[engine]

    def when(self, value, limit):
        branch = Branch(value, limit, {c: c.value for c in self.counts})
        for e in self.queues:
            branch.queues[e] = []
        self.branches.append(branch)

    def otherwise(self):
        branch = self.branches.pop()
        for e, q in branch.queues.items():
            if q:
                branch.skipped[e] = [(c, branch.start[c], c.value - branch.start[c]) for c in {x[2] for x in flat_queue(q, e)}]
                self.queue_of(e).append(branch)

    def pe(self, fn, *after):
        return self.put("tensor", fn, after)

    def dve(self, fn, *after):
        return self.put("vector", fn, after)

    def act(self, fn, *after):
        return self.put("scalar", fn, after)

    def pool(self, fn, *after):
        return self.put("gpsimd", fn, after)

    def dma(self, engine, fn, count, *after):
        return self.put(engine, fn, after, count, 16)

    def begin(self, n):
        self.loop = Loop(n)
        self.loop.queues = {e: [] for e in self.queues}
        self.loop.start = {c: c.value for c in self.counts}
        self.loop.carried = []
        for table in self.carried:
            for key, old in table.items():
                before = Before()
                table[key] = Both(old, before)
                self.loop.carried.append((table, key, old, before, table[key]))

    def end(self):
        loop, self.loop = self.loop, None
        for c, start in loop.start.items():
            loop.step[c] = c.value - start
            c.value = start + loop.n * loop.step[c]
        for table, key, old, before, entry in loop.carried:
            if table[key] is entry:
                table[key] = old
            else:
                before.done = table[key]
        for e, q in loop.queues.items():
            if q:
                self.queues[e].append(loop)

    def emit(self, block):
        for name, put_body in (("sync", block.sync), ("scalar", block.scalar), ("vector", block.vector),
                               ("gpsimd", block.gpsimd), ("tensor", block.tensor)):
            def body(eng, name=name):
                self.emit_straight(eng, name, self.queues[name], {}, None)
            put_body(body)

    def emit_straight(self, eng, name, queue, reached, tested):
        for entry in queue:
            if isinstance(entry, Loop):
                self.emit_loop(eng, name, entry, reached)
            elif isinstance(entry, Branch):
                self.emit_branch(eng, name, entry, None, tested, lambda value: self.emit_straight(
                    eng, name, entry.queues[name], dict(reached), value))
            else:
                fn, after, count, by = entry
                for a in after:
                    self.wait(eng, a, reached)
                fn(eng, None).then_inc(count.sem, by)

    def emit_branch(self, eng, name, branch, loop, tested, body, i=None):
        value = tested if tested is not None else eng.value_load(branch.value(i), min_val=0, max_val=TESTED_MAX)
        with eng.If(value > branch.limit):
            body(value)
        with eng.Else():
            for c, start, step in branch.skipped[name]:
                eng.wait_ge(c.sem, start if loop is None else start + i * loop.step[c])
                eng.nop().then_inc(c.sem, step)

    def wait(self, eng, a, reached):
        v = a.value if a.loop is None else a.value + (a.loop.n - 1) * a.loop.step[a.count]
        if reached.get(a.count, 0) < v:
            reached[a.count] = v
            eng.wait_ge(a.count.sem, v)

    def emit_loop(self, eng, name, loop, reached):
        queue = loop.queues[name]
        for _, after, _, _ in flat_queue(queue, name):
            for a in after:
                if isinstance(a, Done) and a.loop is not loop:
                    self.wait(eng, a, reached)
        with eng.Fori(0, loop.n) as i:
            self.emit_body(eng, name, loop, queue, i, None)

    def emit_body(self, eng, name, loop, queue, i, tested):
        for entry in queue:
            if isinstance(entry, Branch):
                self.emit_branch(eng, name, entry, loop, tested, lambda value: self.emit_body(
                    eng, name, loop, entry.queues[name], i, value), i)
                continue
            fn, after, count, by = entry
            need = {}
            for a in after:
                if isinstance(a, Before):
                    if a.done is None:
                        continue
                    for d in flat([a.done]):
                        if isinstance(d, Done) and d.loop is loop:
                            need[d.count] = max(need.get(d.count, 1), d.value - loop.step[d.count])
                            assert d.value > loop.step[d.count], "has to have counted before the loop"
                elif a.loop is loop:
                    need[a.count] = max(need.get(a.count, 1), a.value)
            for c, v in need.items():
                eng.wait_ge(c.sem, v + i * loop.step[c])
            fn(eng, i).then_inc(count.sem, by)



def bucket_of(dist):
    exact = REL_BUCKETS // 2
    if dist < exact:
        return dist
    large = exact + int(math.log(dist / exact) / math.log(REL_MAX_DIST / exact) * (REL_BUCKETS - exact) + 1e-9)
    return min(large, REL_BUCKETS - 1)


def bucket_rows(seq):
    rows = np.zeros((REL_BUCKETS + 1, 2 * seq), np.float32)
    for n in range(2 * seq):
        dist = seq - 1 - n
        rows[bucket_of(dist) if dist >= 0 else REL_BUCKETS, n] = 1.0
    return rows


def decay_masks():
    fwd = np.zeros((P, LOCAL_LEVELS, P), np.float32)
    for t in range(P):
        base = t // SCAN_CHUNK * SCAN_CHUNK
        mid = base + SCAN_CHUNK // 2 - 1
        fwd[mid + 1:t + 1, 0, t] = 1.0
        fwd[t + 1:mid + 1, 0, t] = -1.0
        for level in range(1, LOCAL_LEVELS):
            size = SCAN_CHUNK << level
            border = t // size * size + size // 2
            fwd[border:t + 1, level, t] = 1.0
            fwd[t + 1:border, level, t] = 1.0
    bwd = fwd[::-1, :, ::-1]
    s, t = np.meshgrid(np.arange(P), np.arange(P), indexing="ij")
    edges = np.stack([s > t, s <= t, s < t, s >= t, s >= 0], 1).astype(np.float32)
    return np.concatenate([fwd, bwd, edges], 1)


def pair_masks():
    fwd = np.zeros((P, LOCAL_LEVELS, P), np.float32)
    s, t = np.meshgrid(np.arange(P), np.arange(P), indexing="ij")
    fwd[:, 0] = (s // SCAN_CHUNK == t // SCAN_CHUNK) & (s <= t)
    for level in range(1, LOCAL_LEVELS):
        size = SCAN_CHUNK << level
        fwd[:, level] = (s // size == t // size) & (s % size < size // 2) & (t % size >= size // 2)
    return np.concatenate([fwd, fwd[::-1, :, ::-1]], 1)


MASK_GT, MASK_LE, MASK_LT, MASK_GE, MASK_ALL = range(2 * LOCAL_LEVELS, 2 * LOCAL_LEVELS + 5)



def build_program(nc, a, out, scratch_bias):
    with ExitStack() as ctx:
        queue_program(nc, ctx, a, out, scratch_bias)


def queue_program(nc, ctx, a, out, scratch_bias):
    prog = Program(nc, ctx)
    pe, dve, act, pool = prog.pe, prog.dve, prog.act, prog.pool

    def sb(name, *shape, dtype=F32):
        return ctx.enter_context(nc.sbuf_tensor(name, list(shape), dtype))

    _, SEQ, D = a["x"].shape
    NT = SEQ // P
    KD = D // P
    UNIT = 512
    A_HEADS, A_DIM = 8, 64
    B_HEADS, B_V = 4, 128
    A_W = A_HEADS * A_DIM
    B_W = B_HEADS * B_V
    MAPS = A_HEADS + 2 * B_HEADS
    M_HEADS, M_DIM = 4, D // 4
    D_FF = a["w_gate"].shape[2]
    GW = 512
    GH = 4
    N_EXP = a["w_expert_gu_2"].shape[1]
    D_EXP = a["w_expert_down_2"].shape[2]
    IN2 = a["w_in_2"].shape[2]

    bank = [ctx.enter_context(nc.psum_tensor(f"bank{b}", [P, 512], F32)) for b in range(8)]
    bank_read = {b: None for b in range(8)}

    ident = sb("ident", P, P)
    weights = sb("weights", P, 2 * KD, UNIT)
    slots = [weights[:, n * KD:(n + 1) * KD, :] for n in range(2)]
    slot_used = {0: None, 1: None}
    hidden_read = {0: None, 1: None}
    prog.carried = [bank_read, slot_used, hidden_read]
    slot_count = [prog.count(f"weights{n}_landed") for n in range(2)]
    x_res = sb("x_res", P, NT, D)
    normed = sb("normed", P, NT, D)
    act_t = sb("act_t", P, KD, SEQ)
    mem_t = sb("mem_t", P, KD, SEQ)
    work = sb("work", P, 27136)
    rows_c = sb("rows_c", P, P)
    cols = sb("cols", P, P)
    small = sb("small", P, 256)
    half_neg = sb("half_neg", P, 16)
    junk = sb("junk", P, D)

    misc = prog.count("misc_loads")
    out_count = prog.count("out_stored")

    def region(at, *shape):
        size = int(np.prod(shape))
        view = work[:, at:at + size]
        names = "abcd"[:len(shape)]
        sizes = {n: x for n, x in zip(names[1:], shape[1:])}
        return view if len(shape) == 1 else view.rearrange(f"p ({' '.join(names)}) -> p {' '.join(names)}", **sizes)

    def everything():
        return Both(*[Done(c, c.value, None) for c in prog.engine_count.values()])

    def load(dst, src, *after, engine="scalar", count=None):
        return prog.dma(engine, lambda e, i: e.dma_start(dst, src), count or prog.count(f"load_{len(prog.counts)}"),
                        *after)

    for engine in ("scalar", "vector", "gpsimd", "tensor"):
        prog.put(engine, lambda e, i: e.nop(), by=64)

    stack, at = {}, 0
    clear_rows = dve(lambda e, i: e.memset(rows_c[:, :], 0.0))
    row_loads = []
    for name in ("mix_norm_g", "cross_norm_g", "mem_norm_g", "ffn_norm_g", "moba_out_g", "diff_subln_g",
                 "g_hgrn_out_2", "g_pre_mix_2", "g_pre_ffn_2", "c_2", "c_ctx_2"):
        v = a[name]
        flat = v.rearrange("a b -> (a b)") if len(v.shape) == 2 else v
        n = flat.shape[0] // P
        stack[name] = slice(at, at + n)
        row_loads.append(prog.dma("scalar", lambda e, i, at=at, n=n, flat=flat: e.dma_start(
            rows_c[at:at + n, :], flat.rearrange("(k p) -> k p", p=P)), misc, clear_rows))
        at += n
    rows_landed = row_loads[-1]
    mirror = sb("mirror", P, P)
    mirror_landed = load(mirror[:, :], a["mirror"], engine="sync")
    ident_landed = load(ident[:, :], a["ident"], engine="sync")
    x_landed = load(x_res[:, :, :], a["x"][0].rearrange("(t p) d -> p t d", p=P), engine="sync")
    powers = pool(lambda e, i: e.memset(half_neg[:, :], -0.5))

    tr = pe(lambda e, i: e.transpose(bank[4][:, 0:P], rows_c[:, :], ident[:, :]), rows_landed, ident_landed)
    gains = dve(lambda e, i: e.tensor_copy(cols[:, :], bank[4][:, 0:P]), tr)
    bank_read[4] = gains


    junk_written = {0: None}
    prog.carried.append(junk_written)

    def sum_squares(src, total, scale, *after):
        width = src.shape[-1]
        junk_written[0] = act(lambda e, i: e.activation(junk[:, 0:width], src, ACT.Square, scale=scale,
                                                        accum_out=total), junk_written[0], *after)
        return junk_written[0]

    def rstd_of(name, sums, scale, n, *after):
        mean = pool(lambda e, i: e.tensor_scalar(sums, sums, scale, EPS, ALU.mult, ALU.add), powers, *after)
        return pool(lambda e, i: e.tensor_tensor(sums, sums, half_neg[:, 0:n], ALU.pow), mean)

    def transposed(src, n_blocks, banks, evacuate, *after):
        moments = []
        jobs = [(t, k0) for t in range(NT) for k0 in range(0, n_blocks, 4)]
        for n, (t, k0) in enumerate(jobs):
            b = banks[n % len(banks)]
            width = min(4, n_blocks - k0)

            def run(e, i, t=t, k0=k0, b=b, width=width):
                for k in range(width):
                    last = e.transpose(bank[b][:, k * P:(k + 1) * P], src(t, k0 + k), ident[:, :])
                return last
            waits = [x[t] if isinstance(x, list) else x for x in after]
            done = pe(run, bank_read[b], *waits)
            moments.append(evacuate(b, t, k0, width, done))
            bank_read[b] = moments[-1]
        return moments[-1]

    def wide(b, width):
        return bank[b][:, 0:width * P].rearrange("p (k t) -> p k t", t=P)

    def norm_t(src, dst, gain, n_free, *after, shift=None, col=0):
        scaled = []
        for t in range(NT):
            total = small[:, col + t:col + t + 1]
            sq = sum_squares(src[:, t, :], total, 1.0, *after)
            r = rstd_of("norm", total, 1.0 / D, 1, sq)
            scaled.append(dve(lambda e, i, t=t, total=total: e.tensor_scalar(
                normed[:, t, :], src[:, t, :], total, None, ALU.mult), r, normed_read[0]))

        def evacuate(b, t, k0, width, done):
            out_ap = dst[:, k0:k0 + width, t * P:(t + 1) * P]
            g = gain[:, k0:k0 + width].unsqueeze(2).to_broadcast([P, width, P])
            m = dve(lambda e, i: e.tensor_tensor(out_ap, wide(b, width), g, ALU.mult), done, n_free, gains)
            if shift is None:
                return m
            s = shift[:, k0:k0 + width].unsqueeze(2).to_broadcast([P, width, P])
            return dve(lambda e, i: e.tensor_tensor(out_ap, out_ap, s, ALU.add), m)
        m = transposed(lambda t, k: normed[:, t, k * P:(k + 1) * P], KD, [4, 5, 6, 7], evacuate, scaled)
        normed_read[0] = bank_read[7]
        return m

    normed_read = [None]

    def linear(n_units, sources, left, left_ready, evacuate, kd=KD, first=0, side=None):
        def one(j, s):
            for part in range(len(sources(0))):
                def start(e, i, part=part):
                    place, view = sources(j if i is None else 2 * i + (first + s))[part]
                    return e.dma_start(place(slots[s]), view)
                landed = prog.dma("sync", start, slot_count[s], slot_used[s])
            for t in range(NT):
                b = 2 * s + t

                def run(e, i, t=t, b=b):
                    for k in range(kd):
                        mm = e.matmul(bank[b][:, :], left[:, k, t * P:(t + 1) * P], slots[s][:, k, :],
                                      start=(k == 0), stop=(k == kd - 1))
                    return mm
                done = pe(run, landed, bank_read[b], left_ready)
                bank_read[b] = evacuate(lambda i: j if i is None else 2 * i + (first + s), t, b, done)
            slot_used[s] = done
            if side:
                side(s)

        turns = n_units // 2 if n_units >= 3 and first % 2 == 0 and (n_units >= 5 or first or side) else 0
        if turns:
            prog.begin(turns)
            one(0, 0)
            one(1, 1)
            prog.end()
        for j in range(first + 2 * turns, first + n_units):
            one(j, j % 2)

    def columns(w, n0=0, width=UNIT):
        view = w.rearrange("(k p) n -> p k n", p=P)
        kd = view.shape[1]
        return lambda j: [(lambda slot: slot[:, 0:kd, 0:width], view[:, :, bass.ds(n0 + j * UNIT, width)])]

    ones = sb("ones", P, P)
    ones_set = pool(lambda e, i: e.memset(ones[:, :], 1.0))
    side_slot = sb("side_slot", P, KD, UNIT)
    ada_acc = sb("ada_acc", P, 3, UNIT)
    silu_c = sb("silu_c", P, 2, KD)
    c_cols = cols[:, stack["c_2"].start:stack["c_ctx_2"].stop].rearrange("p (a k) -> p a k", a=2)
    silu_ready = act(lambda e, i: e.activation(silu_c[:, :, :], c_cols, ACT.Silu), gains)
    bias_row_clear = dve(lambda e, i: e.memset(ada_acc[:, 2, :], 0.0))
    side_read = {"slot": None, "lat": None, "ctx": None, "bias": bias_row_clear}
    prog.carried.append(side_read)
    side_count, side_bias_count = prog.count("ada_landed"), prog.count("ada_bias_landed")
    mod_rows = region(20992, 6, D)
    mod_cols = sb("mod_cols", P, 6, KD)
    ctx_cols = sb("ctx_cols", P, 3, KD)
    ada_v = a["w_ada_2"][0].rearrange("(k p) n -> p k n", p=P)
    ada_bias = a["b_ada_2"]

    def ada_side(first, with_ctx):
        def side(s):
            def j(i):
                return 2 * i + (first + s)
            landed = prog.dma("sync", lambda e, i: e.dma_start(
                side_slot[:, :, :], ada_v[:, :, bass.ds(j(i) * UNIT, UNIT)]), side_count, side_read["slot"])
            bias_landed_ = prog.dma("sync", lambda e, i: e.dma_start(
                ada_acc[0:1, 2, :], ada_bias[:, bass.ds(j(i) * UNIT, UNIT)]), side_bias_count, side_read["bias"])
            for who, name in enumerate(("lat", "ctx") if with_ctx else ("lat",)):
                add, free = ada_acc[:, 2, :], side_read[name]
                for k in range(KD):
                    summed = dve(lambda e, i, k=k, add=add, who=who: e.scalar_tensor_tensor(
                        ada_acc[:, who, :], side_slot[:, k, :], silu_c[:, who, k:k + 1], add, ALU.mult, ALU.add),
                        landed, bias_landed_, free, silu_ready)
                    add, free = ada_acc[:, who, :], summed
                    if k == 0:
                        side_read["bias"] = summed
                side_read["slot"] = summed

                def run(e, i, who=who):
                    if who == 0:
                        e.matmul(bank[6][:, :], ones[:, :], ada_acc[:, 0, :], start=True, stop=True)
                    for c in range(UNIT // P):
                        mm = e.matmul(bank[7][:, 4 * who + c:4 * who + c + 1], ada_acc[:, who, c * P:(c + 1) * P],
                                      ones[:, 0:1], start=True, stop=True)
                    return mm
                done = pe(run, summed, bank_read[6], bank_read[7], ones_set)
                side_read[name] = done
                cols_to = (mod_cols, ctx_cols)[who][:, :, :].rearrange("p a k -> p (a k)")
                if who == 0:
                    bank_read[6] = act(lambda e, i: e.activation(
                        mod_rows[:, :, :].rearrange("p a n -> p (a n)")[:, bass.ds(j(i) * UNIT, UNIT)],
                        bank[6][:, :], ACT.Copy), done)
                bank_read[7] = act(lambda e, i, who=who, cols_to=cols_to: e.activation(
                    cols_to[:, bass.ds(j(i) * 4, 4)], bank[7][:, 4 * who:4 * who + 4], ACT.Copy), done)
                last["ada"] = bank_read[7]
        return side
    last = {}

    h_ready = norm_t(x_res, act_t, cols[:, stack["mix_norm_g"]], None, x_landed, col=0)
    proj = region(0, NT, 3072)

    def to_proj(j, t, b, done):
        last["proj"] = act(lambda e, i: e.activation(proj[:, t, bass.ds(j(i) * UNIT, UNIT)], bank[b][:, :], ACT.Copy),
                           done)
        return last["proj"]
    linear(6, columns(a["w_in"][0]), act_t, h_ready, to_proj, side=ada_side(0, True))
    proj_ready = last["proj"]
    act_t_read = prog.engine_count["tensor"]
    act_t_free = Done(act_t_read, act_t_read.value, None)

    n_heads = A_HEADS + B_HEADS
    table = sb("table", REL_BUCKETS + 1, n_heads)
    buckets = region(14848, 2 * SEQ)[0:REL_BUCKETS + 1, :]
    bias_rows = region(14848 + 2 * SEQ, 2 * SEQ)[0:n_heads, :]
    bias = region(6144, n_heads, 3 * P)
    table_cleared = dve(lambda e, i: e.memset(table[:, :], NEG_INF))
    table_landed = load(table[0:REL_BUCKETS, :], a["rel_bias_table"], table_cleared)
    buckets_landed = load(buckets[:, :], a["bucket_rows"])
    bias_done = pe(lambda e, i: e.matmul(bank[4][0:n_heads, :], table[:, :], buckets[:, :], start=True, stop=True),
                   bank_read[4], table_landed, buckets_landed)
    bias_out = act(lambda e, i: e.activation(bias_rows[:, :], bank[4][0:n_heads, :], ACT.Copy), bias_done)
    bank_read[4] = bias_out
    bias_stored = load(scratch_bias[:, :], bias_rows[:, :], bias_out)
    spread = prog.count("bias_spread")
    for src_off, width, dst_off in ((0, SEQ, 0), (P, P, SEQ)):
        view = bass.AP(tensor=scratch_bias.tensor, offset=src_off,
                       ap=[[1, P], [2 * SEQ, n_heads], [1, width]])
        bias_landed = prog.dma("scalar", lambda e, i, view=view, dst_off=dst_off, width=width: e.dma_start(
            bias[:, :, dst_off:dst_off + width], view), spread, bias_stored)

    qk_t = region(10752, 2 * KD, SEQ)
    sources = [0, 128, 256, 384, 1536, 1664, 1792, 1920, 512, 640, 768, 896, 2048, 2176, 2304, 2432]
    turn = 0
    for n in range(0, 2 * KD, 2):
        b = 4 + (n // 2) % 4

        def run(e, i, n=n, b=b):
            for m in range(2):
                for t in range(NT):
                    last_ = e.transpose(bank[b][:, (2 * m + t) * P:(2 * m + t + 1) * P],
                                        proj[:, t, sources[n + m]:sources[n + m] + P], ident[:, :])
            return last_
        done = pe(run, bank_read[b], proj_ready)
        dst, srcv = qk_t[:, n:n + 2, :], bank[b][:, :].rearrange("p (k t) -> p k t", k=2)
        f = float(A_DIM) ** -0.5 if n < KD else 1.0
        if (n // 2) % 2:
            bank_read[b] = act(lambda e, i, dst=dst, srcv=srcv, f=f: e.activation(dst, srcv, ACT.Copy, scale=f), done)
            qk_act = bank_read[b]
        else:
            bank_read[b] = dve(lambda e, i, dst=dst, srcv=srcv, f=f: e.tensor_scalar(dst, srcv, f, None, ALU.mult), done)
            qk_dve = bank_read[b]

    scores = region(14848, MAPS, 3 * P)
    neg_max = small[:, 16:16 + 2 * MAPS].rearrange("p (t m) -> p t m", t=2)
    sums = small[:, 64:64 + 2 * MAPS].rearrange("p (t m) -> p t m", t=2)
    span = [(SEQ, SEQ + P), (0, SEQ)]
    exp_done = [None] * MAPS
    for m in range(MAPS):
        b = 4 + m % 4
        lo = 64 * (m % 2)

        head = m if m < A_HEADS else A_HEADS + (m - A_HEADS) // 2

        def run(e, i, m=m, b=b, lo=lo, head=head):
            q, k = qk_t[lo:lo + 64, m // 2, :], qk_t[lo:lo + 64, KD + m // 2, :]
            e.matmul(bank[b][:, 0:3 * P], mirror[:, :], bias[:, head, :], start=True, stop=False, skip_group_check=True)
            e.matmul(bank[b][:, 0:SEQ], q[:, P:SEQ], k, start=False, stop=False, skip_group_check=True)
            return e.matmul(bank[b][:, SEQ:SEQ + P], q[:, 0:P], k[:, 0:P], start=False, stop=True,
                            skip_group_check=True)
        done = pe(run, bank_read[b], qk_act, qk_dve, bias_landed, mirror_landed)
        for t in range(NT):
            maxed = dve(lambda e, i, t=t, m=m, b=b: e.tensor_reduce(
                neg_max[:, t, m:m + 1], bank[b][:, span[t][0]:span[t][1]], AX_X, ALU.max, negate=True), done)
        for t in range(NT):
            exp_done[m] = act(lambda e, i, m=m, t=t, b=b: e.activation(
                scores[:, m, span[t][0]:span[t][1]], bank[b][:, span[t][0]:span[t][1]], ACT.Exp,
                bias=neg_max[:, t, m:m + 1], accum_out=sums[:, t, m:m + 1]), maxed)
        bank_read[b] = exp_done[m]
    inverted = dve(lambda e, i: e.reciprocal(sums, sums), exp_done[-1])

    lam_in = sb("lam_in", P, 4, 64)
    lam = small[:, 128:132]
    lam_landed = load(lam_in[:, :, :], a["diff_lambda"][0].partition_broadcast(P))
    l1 = dve(lambda e, i: e.tensor_tensor(lam_in[:, 0::2, :], lam_in[:, 0::2, :], lam_in[:, 1::2, :], ALU.mult),
             lam_landed)
    l2 = dve(lambda e, i: e.tensor_reduce(lam[:, 0:2], lam_in[:, 0::2, :], AX_X, ALU.add), l1)
    l3 = act(lambda e, i: e.activation(lam[:, 0:2], lam[:, 0:2], ACT.Exp), l2)
    l4 = dve(lambda e, i: e.tensor_tensor(lam[:, 2:3], lam[:, 1:2], lam[:, 0:1], ALU.subtract), l3)
    neg_lam = dve(lambda e, i: e.tensor_scalar(lam[:, 3:4], lam[:, 2:3], -LAMBDA_INIT, None, ALU.add), l4)
    b_second = sums[:, :, A_HEADS + 1::2]
    scaled_second = dve(lambda e, i: e.tensor_scalar(b_second, b_second, lam[:, 3:4], None, ALU.mult),
                        neg_lam, inverted)
    for h in range(B_HEADS):
        m0 = A_HEADS + 2 * h
        for t in range(NT):
            p0, p1 = scores[:, m0, span[t][0]:span[t][1]], scores[:, m0 + 1, span[t][0]:span[t][1]]
            s1 = dve(lambda e, i, p1=p1, m0=m0, t=t: e.tensor_scalar(p1, p1, sums[:, t, m0 + 1:m0 + 2], None, ALU.mult),
                     scaled_second)
            combined = dve(lambda e, i, p0=p0, p1=p1, m0=m0, t=t: e.scalar_tensor_tensor(
                p0, p0, sums[:, t, m0:m0 + 1], p1, ALU.mult, ALU.add), s1)

    p_t = region(6144, n_heads, 3, P)
    bias_used = done
    for h in range(n_heads):
        m = h if h < A_HEADS else A_HEADS + 2 * (h - A_HEADS)
        b = 4 + h % 4

        def run(e, i, m=m, b=b):
            for c in range(3):
                last_ = e.transpose(bank[b][:, c * P:(c + 1) * P], scores[:, m, c * P:(c + 1) * P], ident[:, :])
            return last_
        done = pe(run, bank_read[b], exp_done[m] if h < A_HEADS else combined)
        dst, srcv = p_t[:, h, :, :], wide(b, 3)
        if h % 2:
            bank_read[b] = act(lambda e, i, dst=dst, srcv=srcv: e.activation(dst, srcv, ACT.Copy), done, bias_used)
            pt_act = bank_read[b]
        else:
            bank_read[b] = dve(lambda e, i, dst=dst, srcv=srcv: e.tensor_copy(dst, srcv), done, bias_used)
            pt_dve = bank_read[b]

    mixed = normed
    for t in range(NT):
        for kind, (h0, hn, dv, v0) in enumerate(((0, A_HEADS, A_DIM, 1024), (A_HEADS, B_HEADS, B_V, 2560))):
            b = 2 * kind + t

            def run(e, i, t=t, h0=h0, hn=hn, dv=dv, v0=v0, b=b):
                for h in range(hn):
                    o = bank[b][:, h * dv:(h + 1) * dv]
                    blocks = [(2, 0)] if t == 0 else [(0, 0), (1, 1)]
                    for c, key_tile in blocks:
                        last_ = e.matmul(o, p_t[:, h0 + h, c, :], proj[:, key_tile, v0 + h * dv:v0 + (h + 1) * dv],
                                         start=(c == blocks[0][0]), stop=(c == blocks[-1][0]))
                return last_
            done = pe(run, bank_read[b], pt_act, pt_dve)
            dst = mixed[:, t, kind * A_W:kind * A_W + hn * dv].rearrange("p (h d) -> p h d", h=hn)
            srcv = bank[b][:, :].rearrange("p (h d) -> p h d", h=hn)
            if kind == 0:
                r = sums[:, t, 0:A_HEADS].unsqueeze(2).to_broadcast([P, A_HEADS, A_DIM])
                bank_read[b] = dve(lambda e, i, dst=dst, srcv=srcv, r=r: e.tensor_tensor(dst, srcv, r, ALU.mult),
                                   done, normed_read[0])
            else:
                bank_read[b] = dve(lambda e, i, dst=dst, srcv=srcv: e.tensor_copy(dst, srcv), done, normed_read[0])
        mixed_written = bank_read[2 + t]
        ss = small[:, 136 + 5 * t:141 + 5 * t]
        sq = sum_squares(mixed[:, t, 0:A_W], ss[:, 0:1], A_W ** -0.5, mixed_written)
        for h in range(B_HEADS):
            sq = sum_squares(mixed[:, t, A_W + h * B_V:A_W + (h + 1) * B_V], ss[:, 1 + h:2 + h], B_V ** -0.5,
                             mixed_written)
        r = rstd_of("mixed", ss, 1.0, 5, sq)
        na = dve(lambda e, i, t=t, ss=ss: e.tensor_scalar(mixed[:, t, 0:A_W], mixed[:, t, 0:A_W], ss[:, 0:1],
                                                          None, ALU.mult), r)
        part = mixed[:, t, A_W:D].rearrange("p (h d) -> p h d", h=B_HEADS)
        nb = dve(lambda e, i, part=part, ss=ss: e.tensor_tensor(
            part, part, ss[:, 1:5].unsqueeze(2).to_broadcast([P, B_HEADS, B_V]), ALU.mult), r)
        last["mixed%d" % t] = nb
    mix_gain = small[:, 152:160]
    g1 = dve(lambda e, i: e.tensor_copy(mix_gain[:, 0:4], cols[:, stack["moba_out_g"]]), gains)
    sub = cols[:, stack["diff_subln_g"]]
    g2 = dve(lambda e, i: e.tensor_scalar(mix_gain[:, 4:8], sub.to_broadcast([P, B_HEADS]), 1.0 - LAMBDA_INIT, None,
                                          ALU.mult), gains)

    def gained(dst, gain, free, ready):
        def evacuate(b, t, k0, width, done):
            out_ap = dst[:, k0:k0 + width, t * P:(t + 1) * P]
            if gain is None:
                return act(lambda e, i: e.activation(out_ap, wide(b, width), ACT.Copy), done, free)
            g = gain[:, k0:k0 + width].unsqueeze(2).to_broadcast([P, width, P])
            return dve(lambda e, i: e.tensor_tensor(out_ap, wide(b, width), g, ALU.mult), done, free, ready)
        return evacuate
    mixed_t = transposed(lambda t, k: mixed[:, t, k * P:(k + 1) * P], KD, [4, 5, 6, 7],
                         gained(act_t, mix_gain, act_t_free, g2), [last["mixed0"], last["mixed1"]])
    normed_read[0] = bank_read[7]

    def add_to_x(j, t, b, done):
        def run(e, i):
            part = x_res[:, t, bass.ds(j(i) * UNIT, UNIT)]
            return e.tensor_tensor(part, part, bank[b][:, :], ALU.add)
        last["x"] = dve(run, done)
        return last["x"]

    def pe_so_far():
        c = prog.engine_count["tensor"]
        return Done(c, c.value, None)

    linear(2, columns(a["w_out"][0]), act_t, mixed_t, add_to_x)
    x1_ready = last["x"]
    act_t_free = pe_so_far()

    mem_rows = region(0, NT, D)
    mem_landed = load(mem_rows, a["mem"][0].rearrange("(t p) d -> p t d", p=P), act_t_free, engine="sync")
    m_ready = norm_t(mem_rows, mem_t, cols[:, stack["mem_norm_g"]], None, mem_landed, col=2)
    keys = region(2048, NT, D)
    values = region(4096, NT, D)
    queries = region(6144, NT, D)

    def copy_to(dst, key, *after):
        def evacuate(j, t, b, done):
            last[key] = act(lambda e, i: e.activation(dst[:, t, bass.ds(j(i) * UNIT, UNIT)], bank[b][:, :], ACT.Copy),
                            done, *after)
            return last[key]
        return evacuate
    linear(2, columns(a["w_ck"][0]), mem_t, m_ready, copy_to(keys, "keys"))
    linear(2, columns(a["w_cv"][0]), mem_t, m_ready, copy_to(values, "values"))
    c_ready = norm_t(x_res, act_t, cols[:, stack["cross_norm_g"]], act_t_free, x1_ready, col=4)
    linear(2, columns(a["w_cq"][0]), act_t, c_ready, copy_to(queries, "queries"))
    act_t_free = pe_so_far()
    kc_t = region(8192, KD, SEQ)
    qc_t = region(10240, KD, SEQ)
    kt_ready = transposed(lambda t, k: keys[:, t, k * P:(k + 1) * P], KD, [4, 5, 6, 7],
                          gained(kc_t, None, mixed_t, None), last["keys"])
    qt_ready = transposed(lambda t, k: queries[:, t, k * P:(k + 1) * P], KD, [4, 5, 6, 7],
                          gained(qc_t, None, mixed_t, None), last["queries"])
    c_probs = region(12288, M_HEADS, NT, SEQ)
    c_max = small[:, 160:168].rearrange("p (h t) -> p h t", h=M_HEADS)
    c_sum = small[:, 168:176].rearrange("p (h t) -> p h t", h=M_HEADS)
    c_scale = float(M_DIM) ** -0.5
    for h in range(M_HEADS):
        def run(e, i, h=h):
            for t in range(NT):
                for k in range(2):
                    last_ = e.matmul(bank[4 + h][:, t * SEQ:(t + 1) * SEQ], qc_t[:, 2 * h + k, t * P:(t + 1) * P],
                                     kc_t[:, 2 * h + k, :], start=(k == 0), stop=(k == 1))
            return last_
        done = pe(run, bank_read[4 + h], kt_ready, qt_ready)
        view = bank[4 + h][:, :].rearrange("p (t m) -> p t m", t=NT)
        mx = dve(lambda e, i, h=h, view=view: e.tensor_reduce(c_max[:, h, :], view, AX_X, ALU.max, negate=True), done)
        mx = dve(lambda e, i, h=h: e.tensor_scalar(c_max[:, h, :], c_max[:, h, :], c_scale, None, ALU.mult), mx)
        for t in range(NT):
            ex = act(lambda e, i, h=h, t=t, view=view: e.activation(
                c_probs[:, h, t, :], view[:, t, :], ACT.Exp, bias=c_max[:, h, t:t + 1], scale=c_scale,
                accum_out=c_sum[:, h, t:t + 1]), mx, mixed_t)
        bank_read[4 + h] = ex
    c_inv = dve(lambda e, i: e.reciprocal(c_sum, c_sum), ex)
    cp_t = region(8192, M_HEADS, 2, SEQ)
    logits_done = done
    for h in range(M_HEADS):
        def run(e, i, h=h):
            for c in range(2):
                for t in range(NT):
                    last_ = e.transpose(bank[4 + h][:, c * SEQ + t * P:c * SEQ + (t + 1) * P],
                                        c_probs[:, h, t, c * P:(c + 1) * P], ident[:, :])
            return last_
        done = pe(run, bank_read[4 + h])
        bank_read[4 + h] = dve(lambda e, i, h=h: e.tensor_copy(
            cp_t[:, h, :, :], bank[4 + h][:, :].rearrange("p (c t) -> p c t", c=2)), done, logits_done)
    cpt_ready = bank_read[7]
    for t in range(NT):
        for pair in range(2):
            b = 2 * pair + t

            def run(e, i, t=t, pair=pair, b=b):
                for g in range(2):
                    h = 2 * pair + g
                    for c in range(2):
                        last_ = e.matmul(bank[b][:, g * M_DIM:(g + 1) * M_DIM], cp_t[:, h, c, t * P:(t + 1) * P],
                                         values[:, c, h * M_DIM:(h + 1) * M_DIM], start=(c == 0), stop=(c == 1))
                return last_
            done = pe(run, bank_read[b], cpt_ready, last["values"])
            dst = normed[:, t, pair * 512:(pair + 1) * 512].rearrange("p (h d) -> p h d", h=2)
            srcv = bank[b][:, :].rearrange("p (h d) -> p h d", h=2)
            r = c_sum[:, 2 * pair:2 * pair + 2, t].unsqueeze(2).to_broadcast([P, 2, M_DIM])
            bank_read[b] = dve(lambda e, i, dst=dst, srcv=srcv, r=r: e.tensor_tensor(dst, srcv, r, ALU.mult),
                               done, c_inv, normed_read[0])
    oc_ready = bank_read[3]
    oc_t = transposed(lambda t, k: normed[:, t, k * P:(k + 1) * P], KD, [4, 5, 6, 7],
                      gained(act_t, None, act_t_free, None), oc_ready)
    normed_read[0] = bank_read[7]
    linear(2, columns(a["w_co"][0]), act_t, oc_t, add_to_x)
    x2_ready = last["x"]
    act_t_free = pe_so_far()

    f_ready = norm_t(x_res, act_t, cols[:, stack["ffn_norm_g"]], act_t_free, x2_ready, col=6)
    KF = D_FF // P
    HALF = UNIT // 2
    hidden = [region(19968 + s * NT * HALF, NT, HALF) for s in range(2)]
    hidden_t = region(14336, KF, SEQ)
    gate_v = a["w_gate"][0].rearrange("(k p) n -> p k n", p=P)
    up_v = a["w_up"][0].rearrange("(k p) n -> p k n", p=P)

    def gate_up(j):
        return [(lambda slot: slot[:, :, 0:HALF], gate_v[:, :, bass.ds(j * HALF, HALF)]),
                (lambda slot: slot[:, :, HALF:UNIT], up_v[:, :, bass.ds(j * HALF, HALF)])]

    def glu(j, t, b, done):
        s = b // 2
        first_in_body = t == 0
        g = act(lambda e, i: e.activation(hidden[s][:, t, :], bank[b][:, 0:HALF], ACT.Silu), done,
                hidden_read[s])
        u = dve(lambda e, i: e.tensor_tensor(hidden[s][:, t, :], hidden[s][:, t, :], bank[b][:, HALF:UNIT], ALU.mult), g)
        if t == NT - 1:
            tb = 4 + s

            def run(e, i):
                for k in range(2):
                    for tt in range(NT):
                        last_ = e.transpose(bank[tb][:, k * SEQ + tt * P:k * SEQ + (tt + 1) * P],
                                            hidden[s][:, tt, k * P:(k + 1) * P], ident[:, :])
                return last_
            turned = pe(run, u, bank_read[tb])
            hidden_read[s] = turned
            last["hidden"] = act(lambda e, i: e.activation(
                hidden_t[:, bass.ds(j(i) * 2, 2), :], bank[tb][:, :].rearrange("p (k t) -> p k t", k=2), ACT.Copy),
                turned)
            bank_read[tb] = last["hidden"]
        return u

    linear(6, gate_up, act_t, f_ready, glu, side=ada_side(6, False))
    linear(D_FF // HALF - 6, gate_up, act_t, f_ready, glu, first=6)
    ffn_done = last["hidden"]
    act_t_free = pe_so_far()

    down_v = a["w_down"][0].rearrange("(k p) n -> p k n", p=P)
    for r0 in range(0, KF, KD):
        kd = min(KD, KF - r0)
        for half in range(2):
            s = half
            landed = prog.dma("sync", lambda e, i, s=s, kd=kd, r0=r0, half=half: e.dma_start(
                slots[s][:, 0:kd, :], down_v[:, r0:r0 + kd, half * UNIT:(half + 1) * UNIT]), slot_count[s],
                slot_used[s])
            for t in range(NT):
                b = 2 * s + t

                def run(e, i, t=t, b=b, kd=kd, r0=r0, s=s):
                    for k in range(kd):
                        last_ = e.matmul(bank[b][:, :], hidden_t[:, r0 + k, t * P:(t + 1) * P], slots[s][:, k, :],
                                         start=(r0 + k == 0), stop=(r0 + k == KF - 1))
                    return last_
                done = pe(run, landed, bank_read[b], ffn_done)
                if r0 + kd == KF:
                    part = x_res[:, t, half * UNIT:(half + 1) * UNIT]
                    bank_read[b] = dve(lambda e, i, part=part, b=b: e.tensor_tensor(part, part, bank[b][:, :], ALU.add),
                                       done)
                else:
                    bank_read[b] = None
            slot_used[s] = done
    x3_ready = bank_read[3]
    row_g = mod_rows[:, 3, :]
    fin_landed = load(row_g[:, :], a["final_norm_g"].partition_broadcast(P))
    for t in range(NT):
        total = small[:, 8 + t:9 + t]
        sq = sum_squares(x_res[:, t, :], total, 1.0, x3_ready)
        r = rstd_of("final", total, 1.0 / D, 1, sq)
        xf_ready = dve(lambda e, i, t=t, total=total: e.scalar_tensor_tensor(
            x_res[:, t, :], x_res[:, t, :], total, row_g[:, :], ALU.mult, ALU.mult), r, fin_landed)

    before_ctx = everything()
    held = side_slot[:, :, :].rearrange("p k n -> p (k n)")
    masks = held[:, 0:13 * P].rearrange("p (m t) -> p m t", t=P)
    pairs = held[:, 13 * P:21 * P].rearrange("p (m t) -> p m t", t=P)
    states = held[:, 21 * P:29 * P].rearrange("p (d n) -> p d n", d=2)
    masks_landed = load(masks, a["decay_masks"], before_ctx)
    pairs_landed = load(pairs, a["pair_masks"], before_ctx)
    lb = region(20992, 2, GW)
    one_lb = region(22016, 2, GW)
    lb_in = normed[:, :, :].rearrange("p t (l n) -> p t l n", l=2)
    lb_landed = load(lb_in, a["lb_logits_2"].partition_broadcast(P), before_ctx)
    lb_diff = dve(lambda e, i: e.tensor_tensor(lb, lb_in[:, :, 0, :], lb_in[:, :, 1, :], ALU.subtract), lb_landed)
    lb_one = act(lambda e, i: e.activation(one_lb, lb, ACT.Sigmoid, scale=-1.0), lb_diff)
    lb_ready = act(lambda e, i: e.activation(lb, lb, ACT.Sigmoid), lb_one)

    mod_gain = sb("mod_gain", P, 3, KD)
    def modulated(which, scale_cols, gain):
        g = dve(lambda e, i: e.scalar_tensor_tensor(mod_gain[:, which, :], scale_cols, 1.0, cols[:, gain],
                                                    ALU.add, ALU.mult), last["ada"])
        return mod_gain[:, which, :], g
    ctx_rows = region(14336, NT, D)
    ctx_landed = load(ctx_rows, a["ctx_2"][0].rearrange("(t p) d -> p t d", p=P), before_ctx)
    act_t_free = before_ctx
    gain, gain_ready = modulated(0, ctx_cols[:, 1, :], stack["g_pre_mix_2"])
    ctx_t = norm_t(ctx_rows, mem_t, gain, Both(before_ctx, gain_ready), ctx_landed, lb_diff,
                   shift=ctx_cols[:, 0, :], col=8)
    pc = region(16384, NT, 3 * GW)
    linear(3, columns(a["w_in_2"][0], n0=GW), mem_t, ctx_t, copy_to(pc, "pc"))
    lf_c = region(14336, NT, 2 * GW)

    def gates(z, lf, omb, lbv, ready):
        s1 = act(lambda e, i: e.activation(lf, z, ACT.Sigmoid), ready)
        s2 = act(lambda e, i: e.activation(z, z, ACT.Sigmoid, scale=-1.0), s1)
        f1 = dve(lambda e, i: e.tensor_tensor(lf, lf, omb, ALU.mult), s1, lb_ready)
        f2 = dve(lambda e, i: e.tensor_tensor(lf, lf, lbv, ALU.add), f1)
        lf_ready = act(lambda e, i: e.activation(lf, lf, ACT.Ln), f2)
        k_ready = dve(lambda e, i: e.tensor_tensor(z, z, omb, ALU.mult), s2)
        return lf_ready, k_ready
    lb_flat = region(20992, 2 * GW)
    one_flat = region(22016, 2 * GW)
    for t in range(NT):
        lfc_ready, kc_ready = gates(pc[:, t, 0:2 * GW], lf_c[:, t, :], one_flat, lb_flat, Both(last["pc"], ctx_t))
    kw = normed[:, :, :]
    kw_free = ctx_t
    for d in range(2):
        strict = masks[:, (MASK_GT, MASK_LT)[d], :]
        for t in range(NT):
            b = 4 + 2 * d + t

            def run(e, i, d=d, t=t, b=b, strict=strict):
                own = lf_c[:, t, d * GW:(d + 1) * GW]
                other = lf_c[:, 1 - t, d * GW:(d + 1) * GW]
                crossing = t == d
                mm = e.matmul(bank[b][:, :], strict, own, start=True, stop=not crossing)
                if crossing:
                    mm = e.matmul(bank[b][:, :], masks[:, MASK_ALL, :], other, start=False, stop=True)
                return mm
            done = pe(run, bank_read[b], lfc_ready, masks_landed)
            dst = kw[:, t, d * GW:(d + 1) * GW]
            ex = act(lambda e, i, dst=dst, b=b: e.activation(dst, bank[b][:, :], ACT.Exp), done, kw_free)
            bank_read[b] = ex
            kw_ready = dve(lambda e, i, dst=dst, d=d, t=t: e.tensor_tensor(
                dst, dst, pc[:, t, d * GW:(d + 1) * GW], ALU.mult), ex, kc_ready)
    for d in range(2):
        b = 4 + d

        def run(e, i, d=d, b=b):
            for h in range(GH):
                for t in range(NT):
                    mm = e.matmul(bank[b][:, h * P:(h + 1) * P], kw[:, t, d * GW + h * P:d * GW + (h + 1) * P],
                                  pc[:, t, 2 * GW + h * P:2 * GW + (h + 1) * P], start=(t == 0), stop=(t == NT - 1))
            return mm
        done = pe(run, bank_read[b], kw_ready)
        states_ready = bank_read[b] = act(lambda e, i, d=d, b=b: e.activation(states[:, d, :], bank[b][:, :], ACT.Copy),
                                          done)
    normed_read[0] = done
    ctx_done = everything()

    p2 = region(0, IN2 // UNIT, NT, UNIT)
    before_lat = everything()
    gain, gain_ready = modulated(1, mod_cols[:, 1, :], stack["g_pre_mix_2"])
    lat_t = norm_t(x_res, act_t, gain, Both(act_t_free, gain_ready), xf_ready, shift=mod_cols[:, 0, :], col=10)

    def to_p2(j, t, b, done):
        last["p2"] = act(lambda e, i: e.activation(p2[:, bass.ds(j(i), 1), t, :], bank[b][:, :].unsqueeze(1), ACT.Copy),
                         done, before_lat)
        return last["p2"]
    linear(IN2 // UNIT, columns(a["w_in_2"][0]), act_t, lat_t, to_p2)
    act_t_free = pe_so_far()

    lf = region(11264, 2, NT, GW)
    for d in range(2):
        for t in range(NT):
            lf_ready, k_ready = gates(p2[:, 1 + d, t, :], lf[:, d, t, :], one_lb[:, d, :], lb[:, d, :], last["p2"])
    flat2 = "p u t n -> p (u t n)"
    gates_out = act(lambda e, i: e.activation(p2[:, 7:11, :, :].rearrange(flat2), p2[:, 7:11, :, :].rearrange(flat2),
                                              ACT.Sigmoid), last["p2"])
    q_ready = act(lambda e, i: e.activation(p2[:, 0, :, :], p2[:, 0, :, :], ACT.Silu), last["p2"])
    g_ready = act(lambda e, i: e.activation(p2[:, 4, :, :], p2[:, 4, :, :], ACT.Silu), last["p2"])
    cm_ready = act(lambda e, i: e.activation(p2[:, 5:7, :, :].rearrange(flat2), p2[:, 5:7, :, :].rearrange(flat2),
                                             ACT.Gelu_apprx_tanh), last["p2"])
    q_t = region(13312, GH, SEQ)
    k_t = region(14336, 2, GH, SEQ)
    qt_ready = transposed(lambda t, k: p2[:, 0, t, k * P:(k + 1) * P], GH, [4, 5], gained(q_t, None, before_lat, None),
                          q_ready)
    for d in range(2):
        kt_ready = transposed(lambda t, k, d=d: p2[:, 1 + d, t, k * P:(k + 1) * P], GH, [6, 7],
                              gained(k_t[:, d, :, :], None, before_lat, None), k_ready)
    turned = pe_so_far()
    factors = region(16384, NT, GH, LOCAL_LEVELS, P)
    key0 = region(0, NT, GH, P)
    edge = [region(1024, GH, 4, P),
            act_t[:, :, :].rearrange("p k t -> p (k t)").rearrange("p (h b t) -> p h b t", h=GH, b=4)]
    near_far = mem_t[:, :, :].rearrange("p k t -> p (k t)").rearrange("p (a h t) -> p a h t", a=4, h=GH)
    inside, across = near_far[:, 0:2, :, :], near_far[:, 2:4, :, :]
    inside0 = normed[:, 0, 0:GH * P].rearrange("p (h t) -> p h t", h=GH)
    cleared = dve(lambda e, i: e.memset(inside, 0.0), ctx_done)
    factors_free = before_lat
    for d in range(2):
        near, far = d, 1 - d
        first_mask, second_mask = ((MASK_GT, MASK_LE), (MASK_LT, MASK_GE))[d]
        for h in range(GH):
            b = 4 + h % 4
            hs = slice(h * P, (h + 1) * P)

            def run(e, i, b=b, hs=hs, d=d, near=near, far=far, first_mask=first_mask, second_mask=second_mask):
                e.matmul(bank[b][:, 0:2 * P], lf[:, d, near, hs],
                         masks[:, first_mask:second_mask + 1, :].rearrange("p m t -> p (m t)"), start=True, stop=True)
                e.matmul(bank[b][:, 2 * P:3 * P], lf[:, d, far, hs], masks[:, second_mask, :], start=True, stop=True)
                e.matmul(bank[b][:, 3 * P:4 * P], lf[:, d, far, hs], masks[:, second_mask, :], start=True, stop=False)
                return e.matmul(bank[b][:, 3 * P:4 * P], lf[:, d, near, hs], masks[:, MASK_ALL, :], start=False,
                                stop=True)
            done = pe(run, bank_read[b], lf_ready)
            ex = bank_read[b] = act(lambda e, i, b=b, h=h, d=d: e.activation(
                edge[d][:, h, :, :], bank[b][:, :].rearrange("p (c t) -> p c t", c=4), ACT.Exp), done, turned)
        for part, (src, tile) in enumerate(((k_t[:, d], near), (q_t, near), (q_t, far), (q_t, far))):
            v = edge[d][:, :, part, :]
            o = src[:, :, tile * P:(tile + 1) * P]
            edge_ready = dve(lambda e, i, v=v, o=o: e.tensor_tensor(v, v, o, ALU.mult), ex, qt_ready, kt_ready)
        for t in range(NT):
            for h in range(GH):
                b = 4 + h % 4
                done = pe(lambda e, i, b=b, h=h, d=d, t=t: e.matmul(
                    bank[b][:, :], lf[:, d, t, h * P:(h + 1) * P],
                    masks[:, LOCAL_LEVELS * d:LOCAL_LEVELS * (d + 1), :].rearrange("p l t -> p (l t)"),
                    start=True, stop=True), bank_read[b], lf_ready)
                act(lambda e, i, b=b, h=h, t=t: e.activation(
                    factors[:, t, h, :, :], bank[b][:, :].rearrange("p (l t) -> p l t", l=LOCAL_LEVELS), ACT.Exp),
                    done, factors_free)
                ex = bank_read[b] = act(lambda e, i, b=b, h=h, t=t: e.activation(
                    key0[:, t, h, :], bank[b][:, 0:P], ACT.Exp, scale=-1.0), done, turned, factors_free)
            qv, kv = q_t[:, :, t * P:(t + 1) * P], k_t[:, d, :, t * P:(t + 1) * P]
            f0 = factors[:, t, :, 0, :]
            dve(lambda e, i, f0=f0, qv=qv: e.tensor_tensor(f0, f0, qv, ALU.mult), ex, qt_ready)
            ready = dve(lambda e, i, kv=kv, t=t: e.tensor_tensor(key0[:, t], key0[:, t], kv, ALU.mult), ex, kt_ready)
            for level in range(1, LOCAL_LEVELS):
                size = SCAN_CHUNK << level
                halves = lambda v, size=size: v.rearrange("p h (n r c) -> p h n r c", r=2, c=size // 2)
                fv = halves(factors[:, t, :, level, :])
                for role, operand in ((1 - d, qv), (d, kv)):
                    x, y = fv[:, :, :, role, :], halves(operand)[:, :, :, role, :]
                    ready = dve(lambda e, i, x=x, y=y: e.tensor_tensor(x, x, y, ALU.mult), ex, qt_ready, kt_ready)
            for level in range(LOCAL_LEVELS):
                b = level

                def run(e, i, b=b, t=t, level=level):
                    for h in range(GH):
                        keys_ = key0[:, t, h, :] if level == 0 else factors[:, t, h, level, :]
                        mm = e.matmul(bank[b][:, h * P:(h + 1) * P], keys_, factors[:, t, h, level, :],
                                      start=True, stop=True)
                    return mm
                done = pe(run, bank_read[b], ready)
                mask = pairs[:, LOCAL_LEVELS * d + level, :].bitcast(I32).unsqueeze(1).to_broadcast([P, GH, P])
                srcv = bank[b][:, :].rearrange("p (h t) -> p h t", h=GH)
                if d == 1 and level == 0:
                    c0 = dve(lambda e, i: e.memset(inside0, 0.0), normed_free if t == 0 else added)
                    c1 = dve(lambda e, i, mask=mask, srcv=srcv: e.copy_predicated(inside0, mask, srcv), done, c0,
                             pairs_landed)
                    bank_read[b] = c1
                    added = dve(lambda e, i, t=t: e.tensor_tensor(inside[:, t], inside[:, t], inside0, ALU.add), c1,
                                inside_ready)
                    inside_ready = added
                else:
                    inside_ready = bank_read[b] = dve(lambda e, i, mask=mask, srcv=srcv, t=t: e.copy_predicated(
                        inside[:, t], mask, srcv), done, cleared, pairs_landed,
                        inside_ready if (d, t, level) != (0, 0, 0) else None)
        factors_free = pe_so_far()
        normed_free = factors_free

        def run(e, i, d=d):
            for h in range(GH):
                mm = e.matmul(bank[4 + d][:, h * P:(h + 1) * P], edge[d][:, h, 0, :], edge[d][:, h, 2, :],
                              start=True, stop=True)
            return mm
        done = pe(run, bank_read[4 + d], edge_ready)
        across_ready = bank_read[4 + d] = act(lambda e, i, d=d: e.activation(
            across[:, d], bank[4 + d][:, :].rearrange("p (h t) -> p h t", h=GH), ACT.Copy), done, ctx_done)
    value = p2[:, 3, :, :]
    rec = normed
    rec_sum = small[:, 180:188].rearrange("p (t h) -> p t h", t=NT)
    for t in range(NT):
        def run(e, i, t=t):
            for h in range(GH):
                o, hs = bank[t][:, h * P:(h + 1) * P], slice(h * P, (h + 1) * P)
                e.matmul(o, inside[:, t, h, :], value[:, t, hs], start=True, stop=False)
                e.matmul(o, across[:, 1 - t, h, :], value[:, 1 - t, hs], start=False, stop=False)
                for d in range(2):
                    mm = e.matmul(o, edge[d][:, h, 1 if d == t else 3, :], states[:, d, hs], start=False, stop=(d == 1))
            return mm
        done = pe(run, bank_read[t], inside_ready, across_ready, states_ready)
        for h in range(GH):
            ss = sum_squares(bank[t][:, h * P:(h + 1) * P], rec_sum[:, t, h:h + 1], P ** -0.5, done)
        r = rstd_of("rec", rec_sum[:, t, :], 1.0, GH, ss)
        m1 = bank_read[t] = dve(lambda e, i, t=t: e.tensor_tensor(
            rec[:, t, 0:GW].rearrange("p (h d) -> p h d", h=GH), bank[t][:, :].rearrange("p (h d) -> p h d", h=GH),
            rec_sum[:, t, :].unsqueeze(2).to_broadcast([P, GH, P]), ALU.mult), r, inside_ready)
        m2 = dve(lambda e, i, t=t: e.tensor_tensor(rec[:, t, 0:GW], rec[:, t, 0:GW], p2[:, 4, t, :], ALU.mult), m1,
                 g_ready)
    rec_t = region(16384, GH, SEQ)
    hgrn = small[:, 188:192]
    hg = dve(lambda e, i: e.tensor_copy(hgrn, cols[:, stack["g_hgrn_out_2"]].to_broadcast([P, GH])), gains)
    rec_t_ready = transposed(lambda t, k: rec[:, t, k * P:(k + 1) * P], GH, [4, 5],
                             gained(rec_t, hgrn, factors_free, hg), m2)

    ln_rows = mod_rows[:, 4, :].rearrange("p (a n) -> p a n", a=2)
    ln_landed = Both(load(ln_rows[:, 0, :], a["cm_ln_g_2"][0].partition_broadcast(P), before_lat),
                     load(ln_rows[:, 1, :], a["cm_ln_b_2"][0].partition_broadcast(P), before_lat))
    b_sp = sb("b_sp", P, 4)
    ws = ada_acc[:, 0, :].rearrange("p (g q) -> p g q", g=4)
    ws_t = ada_acc[:, 1, :].rearrange("p (g q) -> p g q", g=4)
    b_sp_landed = load(b_sp[:, :], a["b_spatial_2"][0])
    ws_landed = load(ws, a["w_spatial_2"][0].rearrange("g p q -> p g q"), before_lat)

    def run(e, i):
        for g in range(4):
            mm = e.transpose(bank[6][:, g * P:(g + 1) * P], ws[:, g, :], ident[:, :])
        return mm
    done = pe(run, bank_read[6], ws_landed)
    ws_ready = bank_read[6] = act(lambda e, i: e.activation(ws_t, bank[6][:, :].rearrange("p (g q) -> p g q", g=4),
                                                            ACT.Copy), done)
    cm_stat = small[:, 192:200]
    for t in range(NT):
        v, u = p2[:, 6, t, :], p2[:, 5, t, :]
        mean, var = cm_stat[:, 2 * t:2 * t + 1], cm_stat[:, 2 * t + 1:2 * t + 2]
        s1 = dve(lambda e, i, v=v, mean=mean: e.tensor_reduce(mean, v, AX_X, ALU.add), cm_ready)
        s2 = dve(lambda e, i, mean=mean: e.tensor_scalar(mean, mean, 1.0 / GW, None, ALU.mult), s1)
        s3 = dve(lambda e, i, v=v, mean=mean: e.tensor_scalar(v, v, mean, None, ALU.subtract), s2)
        s4 = sum_squares(v, var, GW ** -0.5, s3)
        s5 = rstd_of("cm", var, 1.0, 1, s4)
        s6 = dve(lambda e, i, v=v, var=var: e.scalar_tensor_tensor(v, v, var, ln_rows[:, 0, :], ALU.mult, ALU.mult),
                 s5, ln_landed)
        s7 = dve(lambda e, i, v=v: e.tensor_tensor(v, v, ln_rows[:, 1, :], ALU.add), s6)

        def run(e, i, t=t, v=v):
            for g in range(4):
                mm = e.matmul(bank[2 + t][:, g * P:(g + 1) * P], ws_t[:, g, :], v[:, g * P:(g + 1) * P], start=True,
                              stop=True)
            return mm
        done = pe(run, bank_read[2 + t], s7, ws_ready)
        for g in range(4):
            part = u[:, g * P:(g + 1) * P]
            gated = dve(lambda e, i, part=part, g=g, t=t: e.scalar_tensor_tensor(
                part, bank[2 + t][:, g * P:(g + 1) * P], b_sp[:, g:g + 1], part, ALU.add, ALU.mult), done, cm_ready, b_sp_landed)
        bank_read[2 + t] = gated
    gate_t = region(17408, GH, SEQ)
    gate_t_ready = transposed(lambda t, k: p2[:, 5, t, k * P:(k + 1) * P], GH, [6, 7],
                              gained(gate_t, None, factors_free, None), gated)

    merged = region(18432, NT, D)
    wide_slot = [s_[:, :, :].rearrange("p k n -> p (k n)").rearrange("p (k n) -> p k n", k=4) for s_ in slots]
    for s, (name, left, ready) in enumerate((("w_branch_a_2", rec_t, rec_t_ready), ("w_branch_b_2", gate_t, gate_t_ready))):
        landed = prog.dma("sync", lambda e, i, s=s, name=name: e.dma_start(
            wide_slot[s], a[name][0].rearrange("(k p) n -> p k n", p=P)), slot_count[s], slot_used[s])
        for t in range(NT):
            for half in range(2):
                b = 4 * s + 2 * t + half

                def run(e, i, s=s, t=t, half=half, b=b, left=left):
                    for k in range(4):
                        mm = e.matmul(bank[b][:, :], left[:, k, t * P:(t + 1) * P],
                                      wide_slot[s][:, k, half * UNIT:(half + 1) * UNIT], start=(k == 0), stop=(k == 3))
                    return mm
                done = pe(run, landed, bank_read[b], ready)
                dst = merged[:, t, half * UNIT:(half + 1) * UNIT]
                g = p2[:, 7 + 2 * s + half, t, :]
                if s == 0:
                    first_done = bank_read[b] = dve(lambda e, i, dst=dst, b=b, g=g: e.tensor_tensor(
                        dst, bank[b][:, :], g, ALU.mult), done, gates_out, factors_free)
                else:
                    m = bank_read[b] = dve(lambda e, i, b=b, g=g: e.tensor_tensor(g, bank[b][:, :], g, ALU.mult),
                                           done, gates_out)
                    merged_ready = dve(lambda e, i, dst=dst, g=g: e.tensor_tensor(dst, dst, g, ALU.add), m, first_done)
        slot_used[s] = done
    merged_t = transposed(lambda t, k: merged[:, t, k * P:(k + 1) * P], KD, [4, 5, 6, 7],
                          gained(act_t, None, pe_so_far(), None), merged_ready)
    y2 = region(0, NT, D)
    y2_free = pe_so_far()
    merge_over = everything()
    linear(2, columns(a["w_out_2"][0]), act_t, merged_t, copy_to(y2, "y2", y2_free))
    act_t_free = pe_so_far()

    def gated_rows(which, name, *after):
        landed = load(row_g[:, :], a[name][0].partition_broadcast(P), *after)
        return dve(lambda e, i: e.tensor_tensor(mod_rows[:, which, :], mod_rows[:, which, :], row_g[:, :], ALU.mult),
                   landed)
    post1 = gated_rows(2, "g_post_mix_2", xf_ready)
    for t in range(NT):
        total = small[:, 200 + t:201 + t]
        sq = sum_squares(y2[:, t, :], total, D ** -0.5, last["y2"])
        r = rstd_of("post", total, 1.0, 1, sq)
        m = dve(lambda e, i, t=t, total=total: e.scalar_tensor_tensor(
            y2[:, t, :], y2[:, t, :], total, mod_rows[:, 2, :], ALU.mult, ALU.mult), r, post1)
        x5_ready = dve(lambda e, i, t=t: e.tensor_tensor(x_res[:, t, :], x_res[:, t, :], y2[:, t, :], ALU.add), m)
    post2 = gated_rows(5, "g_post_ffn_2", post1)

    gain, gain_ready = modulated(2, mod_cols[:, 4, :], stack["g_pre_ffn_2"])
    h2_ready = norm_t(x_res, act_t, gain, Both(act_t_free, gain_ready), x5_ready, shift=mod_cols[:, 3, :], col=12)
    w_router = region(20480, KD, N_EXP)
    router_landed = load(w_router, a["w_router_2"][0].rearrange("(k p) n -> p k n", p=P), y2_free)
    spare = ada_acc[:, :, :].rearrange("p a n -> p (a n)")
    r_bias, route = spare[:, 0:N_EXP], spare[:, 64:64 + NT * N_EXP].rearrange("p (t e) -> p t e", t=NT)
    bias_r_landed = load(r_bias, a["b_router_2"][0].partition_broadcast(P), y2_free)
    lower = sb("lower", P, N_GROUPS, N_GROUPS)
    lo0 = pool(lambda e, i: e.memset(lower[:, :, :], 1.0))
    lower_ready = pool(lambda e, i: e.affine_select(out=lower[:, :, :], in_=lower[:, :, :],
                                                    pattern=[[1, N_GROUPS], [-1, N_GROUPS]], compare_op=ALU.is_gt,
                                                    fill=0.0, base=0, channel_multiplier=0), lo0)
    stage_9 = everything()
    chosen = spare[:, 192:192 + NT * N_EXP].rearrange("p (t e) -> p t e", t=NT)
    GE = N_EXP // N_GROUPS
    for t in range(NT):
        base = t * 600
        score, sel = region(base, N_EXP), region(base + 64, N_EXP)
        top = region(base + 128, N_GROUPS, 8)
        grp, gsel = region(base + 192, N_GROUPS), region(base + 200, N_GROUPS)
        cmp_, eq = region(base + 208, N_GROUPS, N_GROUPS), region(base + 272, N_GROUPS, N_GROUPS)
        best, left_ = region(base + 336, 8), region(base + 344, N_EXP)
        tot = region(base + 408, 2)
        b = t

        def run(e, i, t=t, b=b):
            for k in range(KD):
                mm = e.matmul(bank[b][:, 0:N_EXP], act_t[:, k, t * P:(t + 1) * P], w_router[:, k, :], start=(k == 0),
                              stop=(k == KD - 1))
            return mm
        done = pe(run, bank_read[b], h2_ready, router_landed)
        sc = bank_read[b] = act(lambda e, i, b=b, score=score: e.activation(score, bank[b][:, 0:N_EXP], ACT.Sigmoid), done,
                                stage_9)
        c = dve(lambda e, i, sel=sel, score=score: e.tensor_tensor(sel, score, r_bias, ALU.add), sc, bias_r_landed)
        for g in range(N_GROUPS):
            tp = dve(lambda e, i, g=g, top=top, sel=sel: e.max(top[:, g, :], sel[:, g * GE:(g + 1) * GE]), c)
        c = dve(lambda e, i, grp=grp, top=top: e.tensor_tensor(grp, top[:, :, 0], top[:, :, 1], ALU.add), tp)
        mine = grp.unsqueeze(2).to_broadcast([P, N_GROUPS, N_GROUPS])
        others = grp.unsqueeze(1).to_broadcast([P, N_GROUPS, N_GROUPS])
        c1 = dve(lambda e, i, cmp_=cmp_, mine=mine, others=others: e.tensor_tensor(cmp_, others, mine, ALU.is_gt), c)
        c2 = dve(lambda e, i, eq=eq, mine=mine, others=others: e.tensor_tensor(eq, others, mine, ALU.is_equal), c)
        c2 = dve(lambda e, i, eq=eq: e.tensor_tensor(eq, eq, lower[:, :, :], ALU.mult), c2, lower_ready)
        c1 = dve(lambda e, i, cmp_=cmp_, eq=eq: e.tensor_tensor(cmp_, cmp_, eq, ALU.add), c1, c2)
        c1 = dve(lambda e, i, gsel=gsel, cmp_=cmp_: e.tensor_reduce(gsel, cmp_, AX_X, ALU.add), c1)
        c1 = dve(lambda e, i, gsel=gsel: e.tensor_scalar(gsel, gsel, TOPK_GROUPS - 0.5, None, ALU.is_lt), c1)
        by_group = lambda v: v.rearrange("p (g e) -> p g e", g=N_GROUPS)
        gm = gsel.unsqueeze(2).to_broadcast([P, N_GROUPS, GE])
        c1 = dve(lambda e, i, sel=by_group(sel), gm=gm: e.tensor_tensor(sel, sel, gm, ALU.mult), c1)
        c2 = dve(lambda e, i, grp=grp, gsel=gsel: e.tensor_scalar(grp, gsel, -NEG_INF, NEG_INF, ALU.mult, ALU.add), c1)
        low = grp.unsqueeze(2).to_broadcast([P, N_GROUPS, GE])
        c1 = dve(lambda e, i, sel=by_group(sel), low=low: e.tensor_tensor(sel, sel, low, ALU.add), c2)
        c1 = dve(lambda e, i, best=best, sel=sel: e.max(best, sel), c1)
        c1 = dve(lambda e, i, left_=left_, best=best, sel=sel: e.match_replace(left_, best, sel, 2 * NEG_INF), c1)
        picked = c1 = dve(lambda e, i, left_=left_, sel=sel, t=t: e.tensor_tensor(chosen[:, t, :], left_, sel,
                                                                                 ALU.not_equal), c1)
        c1 = dve(lambda e, i, left_=left_, score=score, t=t: e.tensor_tensor(left_, chosen[:, t, :], score,
                                                                             ALU.mult), c1)
        c1 = dve(lambda e, i, left_=left_, tot=tot: e.tensor_reduce(tot[:, 0:1], left_, AX_X, ALU.add), c1)
        c1 = dve(lambda e, i, tot=tot: e.reciprocal(tot[:, 1:2], tot[:, 0:1]), c1)
        routed = dve(lambda e, i, left_=left_, tot=tot, t=t: e.tensor_scalar(
            route[:, t, :], left_, tot[:, 1:2], ROUTED_SCALE, ALU.mult, ALU.mult), c1)

    expert_place = spare[:, 320:320 + NT * N_EXP].rearrange("p (t e) -> p t e", t=NT)
    slot_index = spare[:, 448:448 + SEQ]
    earlier = region(23552, P)
    most = sb("most", 1, N_EXP // 2, dtype=I32)
    earlier_landed = load(earlier, a["decay_masks"][:, MASK_LT, :], stage_9)
    index_landed = load(slot_index, a["slot_index"].partition_broadcast(P), stage_9)

    def run(e, i):
        e.matmul(bank[2][:, 0:N_EXP], earlier, chosen[:, 0, :], start=True, stop=True)
        e.matmul(bank[2][:, N_EXP:2 * N_EXP], earlier, chosen[:, 1, :], start=True, stop=False)
        e.matmul(bank[2][:, N_EXP:2 * N_EXP], ones[:, :], chosen[:, 0, :], start=False, stop=True)
        e.matmul(bank[2][:, 2 * N_EXP:3 * N_EXP], ones[:, :], chosen[:, 0, :], start=True, stop=False)
        return e.matmul(bank[2][:, 2 * N_EXP:3 * N_EXP], ones[:, :], chosen[:, 1, :], start=False, stop=True)
    counted = pe(run, picked, bank_read[2], earlier_landed)
    p1 = dve(lambda e, i: e.tensor_scalar(expert_place, chosen, -2.0 * SEQ, 2.0 * SEQ, ALU.mult, ALU.add), picked)
    placed = dve(lambda e, i: e.tensor_tensor(expert_place, expert_place, bank[2][:, 0:NT * N_EXP].rearrange(
        "p (t e) -> p t e", t=NT), ALU.add), p1, counted)
    pair_counts = bank[2][0:1, 2 * N_EXP:3 * N_EXP].rearrange("p (n two) -> p n two", two=2)
    most_ready = bank_read[2] = dve(lambda e, i: e.tensor_reduce(most[:, :], pair_counts, AX_X, ALU.max), counted)
    token_rows = normed

    def evacuate(b, t, k0, width, done):
        return act(lambda e, i: e.activation(token_rows[:, t, k0 * P:(k0 + width) * P], bank[b][:, 0:width * P], ACT.Copy),
                   done, h2_ready)
    rows_ready = transposed(lambda t, k: act_t[:, k, t * P:(t + 1) * P], KD, [4, 5, 6, 7], evacuate, h2_ready)

    gu = [region(8192, 2 * KD, UNIT), weights[:, :, :]]
    down = [region(16384, 4, D), side_slot[:, :, :].rearrange("p k n -> p (k n)").rearrange("p (k n) -> p k n", k=4)]
    gathered = [mem_t[:, :, s * P:(s + 1) * P] for s in range(2)]
    exp_hidden = [region(20992 + s * D_EXP, D_EXP) for s in range(2)]
    exp_hidden_t = [region(21504 + s * 512, 512) for s in range(2)]
    pick = [region(22528 + s * 256, NT, 2, SLOTS) for s in range(2)] + [region(25600, NT, 2, SLOTS)]
    weighted = [region(23040 + s * 256, NT, 2, SLOTS) for s in range(2)] + [region(25856, NT, 2, SLOTS)]
    result = [region(23552 + s * D, D) for s in range(2)]
    gu_count = [prog.count(f"expert_gu{s}_landed") for s in range(2)]
    down_count = [prog.count(f"expert_down{s}_landed") for s in range(2)]
    exp_used, exp_ready = {}, {}
    prog.carried += [exp_used, exp_ready]
    stage_10 = Both(placed, most_ready, everything())
    for s in range(2):
        for name in ("gathered", "hidden", "hidden_t", "result", "pick", "weighted"):
            exp_used[name, s] = exp_ready[name, s] = stage_10
        exp_ready["gu", s] = exp_ready["down", s] = None
    for name in ("pick", "weighted"):
        exp_used[name, 2] = exp_ready[name, 2] = stage_10
    exp_used["gu", 0] = exp_used["down", 0] = merge_over
    exp_used["gu", 1] = slot_used[1]
    exp_used["down", 1] = merge_over

    def load_pair(s, pair):
        gu_v = a["w_expert_gu_2"][0].rearrange("(n two) (k p) c -> n p (two k) c", two=2, p=P)
        down_v = a["w_expert_down_2"][0].rearrange("(n two) (k p) c -> n p (two k) c", two=2, p=P)

        def of(v, i):
            return v[bass.ds(pair(i), 1)].rearrange("n p k c -> p (n k) c")
        exp_ready["gu", s] = prog.dma("sync", lambda e, i: e.dma_start(gu[s], of(gu_v, i)), gu_count[s], exp_used["gu", s])
        exp_ready["down", s] = prog.dma("sync", lambda e, i: e.dma_start(down[s], of(down_v, i)), down_count[s],
                                    exp_used["down", s])

    def select(n, pair, block):
        wanted = slot_index[:, block * SLOTS:(block + 1) * SLOTS].unsqueeze(1).unsqueeze(1).to_broadcast(
            [P, NT, 2, SLOTS])

        def over_slots(v, i):
            return v[:, :, bass.ds(2 * pair(i), 2)].unsqueeze(3).to_broadcast([P, NT, 2, SLOTS])
        exp_ready["pick", n] = dve(lambda e, i: e.tensor_tensor(pick[n], wanted, over_slots(expert_place, i), ALU.is_equal),
                               placed, index_landed, exp_used["pick", n])
        exp_ready["weighted", n] = dve(lambda e, i: e.tensor_tensor(weighted[n], pick[n], over_slots(route, i), ALU.mult),
                                   exp_ready["pick", n], routed, exp_used["weighted", n])

    def gather(n, s, banks):
        halves = []
        for part in range(2):
            def run(e, i, part=part):
                for k in range(4):
                    for t in range(NT):
                        mm = e.matmul(bank[banks[part]][:, k * P:(k + 1) * P],
                                      token_rows[:, t, (4 * part + k) * P:(4 * part + k + 1) * P],
                                      pick[n][:, t, :, :].rearrange("p e s -> p (e s)"), start=(t == 0),
                                      stop=(t == NT - 1))
                return mm
            exp_used["pick", n] = pe(run, exp_ready["pick", n], rows_ready, bank_read[banks[part]])
            dst = gathered[s][:, 4 * part:4 * part + 4, :]
            src = bank[banks[part]][:, :].rearrange("p (k n) -> p k n", n=P)
            if part == 0:
                m = act(lambda e, i, dst=dst, src=src: e.activation(dst, src, ACT.Copy), exp_used["pick", n],
                        exp_used["gathered", s])
            else:
                m = dve(lambda e, i, dst=dst, src=src: e.tensor_copy(dst, src), exp_used["pick", n], exp_used["gathered", s])
            bank_read[banks[part]] = m
            halves.append(m)
        exp_ready["gathered", s] = Both(*halves)

    def gate_up(s, n, banks):
        def run(e, i):
            for k in range(KD):
                for x in range(2):
                    mm = e.matmul(bank[banks[0]][x * SLOTS:(x + 1) * SLOTS, :],
                                  gathered[s][:, k, x * SLOTS:(x + 1) * SLOTS], gu[s][:, x * KD + k, :],
                                  start=(k == 0), stop=(k == KD - 1))
            return mm
        done = exp_used["gathered", s] = exp_used["gu", s] = pe(run, exp_ready["gathered", s], exp_ready["gu", s], bank_read[banks[0]])
        g = act(lambda e, i: e.activation(exp_hidden[n], bank[banks[0]][:, 0:D_EXP], ACT.Silu), done, exp_used["hidden", n])
        bank_read[banks[0]] = exp_ready["hidden", n] = dve(lambda e, i: e.tensor_tensor(
            exp_hidden[n], exp_hidden[n], bank[banks[0]][:, D_EXP:2 * D_EXP], ALU.mult), g)

    def turn(n, m, banks):
        def run(e, i):
            for t in range(NT):
                e.transpose(bank[banks[1]][:, D_EXP + t * P:D_EXP + (t + 1) * P],
                            weighted[m][:, t, :, :].rearrange("p e s -> p (e s)"), ident[:, :])
            for k in range(2):
                mm = e.transpose(bank[banks[1]][:, k * P:(k + 1) * P], exp_hidden[n][:, k * P:(k + 1) * P], ident[:, :])
            return mm
        done = exp_used["hidden", n] = exp_used["weighted", m] = pe(run, exp_ready["hidden", n], exp_ready["weighted", m],
                                                            bank_read[banks[1]])
        exp_ready["hidden_t", n] = bank_read[banks[1]] = act(lambda e, i: e.activation(
            exp_hidden_t[n], bank[banks[1]][:, :], ACT.Copy), done, exp_used["hidden_t", n])

    def project(s, n, banks):
        halves = []
        for half in range(2):
            def run(e, i, half=half):
                for k in range(2):
                    for x in range(2):
                        mm = e.matmul(bank[banks[half]][x * SLOTS:(x + 1) * SLOTS, :],
                                      exp_hidden_t[n][:, k * P + x * SLOTS:k * P + (x + 1) * SLOTS],
                                      down[s][:, 2 * x + k, half * UNIT:(half + 1) * UNIT], start=(k == 0),
                                      stop=(k == 1))
                return mm
            done = pe(run, exp_ready["hidden_t", n], exp_ready["down", s], bank_read[banks[half]])
            dst, src = result[n][:, half * UNIT:(half + 1) * UNIT], bank[banks[half]][:, :]
            if half == 0:
                m = act(lambda e, i, dst=dst, src=src: e.activation(dst, src, ACT.Copy), done, exp_used["result", n])
            else:
                m = dve(lambda e, i, dst=dst, src=src: e.tensor_copy(dst, src), done, exp_used["result", n])
            bank_read[banks[half]] = m
            halves.append(m)
        exp_used["down", s] = done
        exp_ready["result", n] = Both(*halves)

    def scatter(n, last_one=False):
        def run(e, i):
            for t in range(NT):
                for half in range(2):
                    mm = e.matmul(bank[2 * t + half][:, :], exp_hidden_t[n][:, D_EXP + t * P:D_EXP + (t + 1) * P],
                                  result[n][:, half * UNIT:(half + 1) * UNIT], start=False, stop=last_one,
                                  skip_group_check=True)
            return mm
        exp_used["hidden_t", n] = exp_used["result", n] = pe(run, exp_ready["result", n], exp_ready["hidden_t", n])
        return exp_used["result", n]

    def pair_steps(s, pair, first=False, final=False):
        o = 1 - s
        banks, others = ((6, 7), (4, 5)) if s == 0 else ((4, 5), (6, 7))
        following = lambda i: pair(i) + 1
        if not first and not final:
            load_pair(o, following)
        gate_up(s, s, banks)
        if not final:
            select(o, following, 0)
        if not first:
            scatter(o)
        turn(s, s, banks)
        if not final:
            gather(o, o, others)
        project(s, s, banks)
        for rounds in ((1,), (2, 3)):
            prog.when(lambda i: most[0:1, bass.ds(pair(i), 1)], rounds[0] * SLOTS)
            for block in rounds:
                select(2, pair, block)
                gather(2, s, banks)
                gate_up(s, o, banks)
                turn(o, 2, banks)
                project(s, o, banks)
                scatter(o)
        for rounds in range(2):
            prog.otherwise()

    shared_gu = region(2048, KD, UNIT)
    shared_down = region(6144, 2, D)
    shared_landed = [load(shared_gu, a["w_shared_gu_2"][0].rearrange("(k p) n -> p k n", p=P), merge_over,
                          engine="sync"),
                     load(shared_down, a["w_shared_down_2"][0].rearrange("(k p) n -> p k n", p=P), merge_over,
                          engine="sync")]
    load_pair(0, lambda i: 0)
    load_pair(1, lambda i: 1)
    shared_act = region(24576, NT, D_EXP)
    shared_t = region(25088, 2, SEQ)
    for t in range(NT):
        b = 4 + t

        def run(e, i, t=t, b=b):
            for k in range(KD):
                mm = e.matmul(bank[b][:, :], act_t[:, k, t * P:(t + 1) * P], shared_gu[:, k, :],
                              start=(k == 0), stop=(k == KD - 1))
            return mm
        done = pe(run, shared_landed[0], bank_read[b], h2_ready)
        g = act(lambda e, i, t=t, b=b: e.activation(shared_act[:, t, :], bank[b][:, 0:D_EXP], ACT.Silu), done,
                stage_9)
        u = bank_read[b] = dve(lambda e, i, t=t, b=b: e.tensor_tensor(
            shared_act[:, t, :], shared_act[:, t, :], bank[b][:, D_EXP:2 * D_EXP], ALU.mult), g)

    def run(e, i):
        for k in range(2):
            for t in range(NT):
                mm = e.transpose(bank[6][:, k * SEQ + t * P:k * SEQ + (t + 1) * P],
                                 shared_act[:, t, k * P:(k + 1) * P], ident[:, :])
        return mm
    done = pe(run, u, bank_read[6])
    shared_turned = bank_read[6] = act(lambda e, i: e.activation(
        shared_t, bank[6][:, :].rearrange("p (k t) -> p k t", k=2), ACT.Copy), done, stage_9)
    select(0, lambda i: 0, 0)
    gather(0, 0, (6, 7))

    def run(e, i):
        for t in range(NT):
            for half in range(2):
                for k in range(2):
                    mm = e.matmul(bank[2 * t + half][:, :], shared_t[:, k, t * P:(t + 1) * P],
                                  shared_down[:, k, half * UNIT:(half + 1) * UNIT], start=(k == 0), stop=False,
                                  skip_group_check=True)
        return mm
    shared_done = pe(run, shared_turned, shared_landed[1], bank_read[0], bank_read[1], bank_read[2], bank_read[3])
    exp_used["result", 1] = Both(exp_used["result", 1], shared_done)

    N_PAIRS = N_EXP // 2
    pair_steps(0, lambda i: 0, first=True)
    prog.begin((N_PAIRS - 2) // 2)
    for step in (1, 2):
        pair_steps(step % 2, lambda i, step=step: 2 * i + step)
    prog.end()
    pair_steps(1, lambda i: N_PAIRS - 1, final=True)
    experts_done = scatter(1, last_one=True)

    totals = small[:, 204:208].rearrange("p (t h) -> p t h", t=NT)
    y3 = normed
    for t in range(NT):
        for half in range(2):
            sq = sum_squares(bank[2 * t + half][:, :], totals[:, t, half:half + 1], D ** -0.5, experts_done)
        s1 = dve(lambda e, i, t=t: e.tensor_tensor(totals[:, t, 0:1], totals[:, t, 0:1], totals[:, t, 1:2], ALU.add), sq)
        r = rstd_of("post2", totals[:, t, 0:1], 1.0, 1, s1)
        for half in range(2):
            cs = slice(half * UNIT, (half + 1) * UNIT)
            m = dve(lambda e, i, t=t, half=half, cs=cs: e.scalar_tensor_tensor(
                y3[:, t, cs], bank[2 * t + half][:, :], totals[:, t, 0:1], mod_rows[:, 5, cs], ALU.mult, ALU.mult), r,
                post2)
            final = dve(lambda e, i, t=t, cs=cs: e.tensor_tensor(y3[:, t, cs], y3[:, t, cs], x_res[:, t, cs], ALU.add), m)
        stored = load(out[0, t * P:(t + 1) * P, :], y3[:, t, :], final, engine="sync", count=out_count)
    prog.put("sync", lambda e, i: e.nop(), [stored])
    with nc.Block() as block:
        prog.emit(block)


def kernel(**inputs):
    import concourse.bacc as bacc
    from concourse.bass_utils import run_bass_kernel_spmd

    arrays = {name: np.ascontiguousarray(value) for name, value in inputs.items()}
    seq = arrays["x"].shape[1]
    arrays["ident"] = np.eye(P, dtype=np.float32)
    arrays["mirror"] = np.eye(P, dtype=np.float32)[::-1].copy()
    arrays["bucket_rows"] = bucket_rows(seq)
    arrays["decay_masks"] = decay_masks()
    arrays["pair_masks"] = pair_masks()
    arrays["slot_index"] = np.arange(seq, dtype=np.float32)
    nc = bacc.Bacc("TRN2", target_bir_lowering=False, num_devices=1)
    views = {name: nc.dram_tensor(f"in_{name}", value.shape, F32, kind="ExternalInput").ap()
             for name, value in arrays.items()}
    out = nc.dram_tensor("out", list(arrays["x"].shape), F32, kind="ExternalOutput").ap()
    scratch_bias = nc.dram_tensor("scratch_bias", [12, 2 * seq], F32, kind="Internal").ap()
    build_program(nc, views, out, scratch_bias)
    results = run_bass_kernel_spmd(nc, [{f"in_{name}": value for name, value in arrays.items()}], core_ids=[0])
    return results.results[0]["out"]
```

```python
import math
from contextlib import ExitStack

import concourse.bass as bass
from concourse import mybir
import numpy as np

F32 = mybir.dt.float32
I32 = mybir.dt.int32
F32R = mybir.dt.float32r
ALU = mybir.AluOpType
ACT = mybir.ActivationFunctionType
AX_X = mybir.AxisListType.X

P = 128
EPS = 1e-6
NEG_INF = -1e30
LOCAL_LEVELS = 4
SCAN_CHUNK = 16
REL_BUCKETS, REL_MAX_DIST = 32, 128
LAMBDA_INIT = 0.8 - 0.6 * math.exp(-0.3 * 0)
ROUTED_SCALE = 2.5
TOP_K, TOPK_GROUPS, N_GROUPS = 8, 4, 8
SLOTS = 64
TESTED_MAX = 1 << 12



class Count:

    def __init__(self, sem):
        self.sem, self.value = sem, 0


class Done:

    def __init__(self, count, value, loop):
        self.count, self.value, self.loop = count, value, loop


class Before:

    done = None


class Both:

    def __init__(self, *moments):
        self.moments = []
        for m in moments:
            self.moments += m.moments if isinstance(m, Both) else [m]


def flat(moments):
    return [m for m in Both(*moments).moments if m is not None]


class Loop:
    def __init__(self, n):
        self.n, self.start, self.step = n, {}, {}


class Branch:

    def __init__(self, value, limit, start):
        self.value, self.limit, self.start, self.queues, self.skipped = value, limit, start, {}, {}


def flat_queue(queue, engine=None):
    for entry in queue:
        if isinstance(entry, Branch):
            yield from flat_queue(entry.queues[engine], engine)
        else:
            yield entry


class Program:

    def __init__(self, nc, ctx):
        self.nc, self.ctx = nc, ctx
        self.counts, self.carried, self.loop, self.branches = [], [], None, []
        self.tested = {}
        self.queues = {e: [] for e in ("sync", "scalar", "vector", "gpsimd", "tensor")}
        self.engine_count = {e: self.count(f"done_{e}") for e in self.queues}

    def count(self, name):
        self.counts.append(Count(self.ctx.enter_context(self.nc.semaphore(name))))
        return self.counts[-1]

    def put(self, engine, fn, after=(), count=None, by=1):
        count = count or self.engine_count[engine]
        if self.loop is not None:
            assert count in self.loop.start, "made before the loop"
        count.value += by
        self.queue_of(engine).append((fn, flat(after), count, by))
        return Done(count, count.value, self.loop)

    def queue_of(self, engine):
        if self.branches:
            return self.branches[-1].queues[engine]
        return self.queues[engine] if self.loop is None else self.loop.queues[engine]

    def when(self, value, limit, again=False):
        branch = Branch(value, limit, {c: c.value for c in self.counts})
        branch.again = again
        branch.before = [dict(table) for table in self.carried]
        for e in self.queues:
            branch.queues[e] = []
        self.branches.append(branch)

    def otherwise(self):
        branch = self.branches.pop()
        for table, before in zip(self.carried, branch.before):
            for key, old in before.items():
                if table[key] is not old:
                    table[key] = Both(*flat([old, table[key]]))
        for e, q in branch.queues.items():
            if q:
                branch.skipped[e] = [(c, branch.start[c], c.value - branch.start[c]) for c in {x[2] for x in flat_queue(q, e)}]
                self.queue_of(e).append(branch)

    def pe(self, fn, *after):
        return self.put("tensor", fn, after)

    def dve(self, fn, *after):
        return self.put("vector", fn, after)

    def act(self, fn, *after):
        return self.put("scalar", fn, after)

    def pool(self, fn, *after):
        return self.put("gpsimd", fn, after)

    def dma(self, engine, fn, count, *after):
        return self.put(engine, fn, after, count, 16)

    def begin(self, n):
        self.loop = Loop(n)
        self.loop.queues = {e: [] for e in self.queues}
        self.loop.start = {c: c.value for c in self.counts}
        self.loop.carried = []
        for table in self.carried:
            for key, old in table.items():
                before = Before()
                table[key] = Both(old, before)
                self.loop.carried.append((table, key, old, before, table[key]))

    def end(self):
        loop, self.loop = self.loop, None
        for c, start in loop.start.items():
            loop.step[c] = c.value - start
            c.value = start + loop.n * loop.step[c]
        for table, key, old, before, entry in loop.carried:
            if table[key] is entry:
                table[key] = old
            else:
                before.done = table[key]
                table[key] = Both(*[m for m in flat([table[key]]) if not isinstance(m, Before)])
        for e, q in loop.queues.items():
            if q:
                self.queues[e].append(loop)

    def emit(self, block):
        for name, put_body in (("sync", block.sync), ("scalar", block.scalar), ("vector", block.vector),
                               ("gpsimd", block.gpsimd), ("tensor", block.tensor)):
            def body(eng, name=name):
                self.emit_straight(eng, name, self.queues[name], {}, None)
            put_body(body)

    def emit_straight(self, eng, name, queue, reached, tested):
        for entry in queue:
            if isinstance(entry, Loop):
                self.emit_loop(eng, name, entry, reached)
            elif isinstance(entry, Branch):
                self.emit_branch(eng, name, entry, None, tested, lambda value: self.emit_straight(
                    eng, name, entry.queues[name], dict(reached), value))
            else:
                fn, after, count, by = entry
                for a in after:
                    self.wait(eng, a, reached)
                fn(eng, None).then_inc(count.sem, by)

    def emit_branch(self, eng, name, branch, loop, tested, body, i=None):
        value = tested
        if branch.again:
            value = self.tested[name]
        elif value is None:
            value = self.tested[name] = eng.value_load(branch.value(i), min_val=0, max_val=TESTED_MAX)
        with eng.If(value > branch.limit):
            body(value)
        with eng.Else():
            for c, start, step in branch.skipped[name]:
                eng.wait_ge(c.sem, start if loop is None else start + i * loop.step[c])
                eng.nop().then_inc(c.sem, step)

    def wait(self, eng, a, reached):
        v = a.value if a.loop is None else a.value + (a.loop.n - 1) * a.loop.step[a.count]
        if reached.get(a.count, 0) < v:
            reached[a.count] = v
            eng.wait_ge(a.count.sem, v)

    def emit_loop(self, eng, name, loop, reached):
        queue = loop.queues[name]
        for _, after, _, _ in flat_queue(queue, name):
            for a in after:
                if isinstance(a, Done) and a.loop is not loop:
                    self.wait(eng, a, reached)
        with eng.Fori(0, loop.n) as i:
            self.emit_body(eng, name, loop, queue, i, None)

    def emit_body(self, eng, name, loop, queue, i, tested):
        for entry in queue:
            if isinstance(entry, Branch):
                self.emit_branch(eng, name, entry, loop, tested, lambda value: self.emit_body(
                    eng, name, loop, entry.queues[name], i, value), i)
                continue
            fn, after, count, by = entry
            need = {}
            for a in after:
                if isinstance(a, Before):
                    if a.done is None:
                        continue
                    for d in flat([a.done]):
                        if isinstance(d, Done) and d.loop is loop:
                            need[d.count] = max(need.get(d.count, 1), d.value - loop.step[d.count])
                            assert d.value > loop.step[d.count], "has to have counted before the loop"
                elif a.loop is loop:
                    need[a.count] = max(need.get(a.count, 1), a.value)
            for c, v in need.items():
                eng.wait_ge(c.sem, v + i * loop.step[c])
            fn(eng, i).then_inc(count.sem, by)



def bucket_of(dist):
    exact = REL_BUCKETS // 2
    if dist < exact:
        return dist
    large = exact + int(math.log(dist / exact) / math.log(REL_MAX_DIST / exact) * (REL_BUCKETS - exact) + 1e-9)
    return min(large, REL_BUCKETS - 1)


def bucket_rows(seq):
    rows = np.zeros((REL_BUCKETS + 1, 2 * seq), np.float32)
    for n in range(2 * seq):
        dist = seq - 1 - n
        rows[bucket_of(dist) if dist >= 0 else REL_BUCKETS, n] = 1.0
    return rows


def decay_masks():
    fwd = np.zeros((P, LOCAL_LEVELS, P), np.float32)
    for t in range(P):
        base = t // SCAN_CHUNK * SCAN_CHUNK
        mid = base + SCAN_CHUNK // 2 - 1
        fwd[mid + 1:t + 1, 0, t] = 1.0
        fwd[t + 1:mid + 1, 0, t] = -1.0
        for level in range(1, LOCAL_LEVELS):
            size = SCAN_CHUNK << level
            border = t // size * size + size // 2
            fwd[border:t + 1, level, t] = 1.0
            fwd[t + 1:border, level, t] = 1.0
    bwd = fwd[::-1, :, ::-1]
    s, t = np.meshgrid(np.arange(P), np.arange(P), indexing="ij")
    edges = np.stack([s > t, s <= t, s < t, s >= t, s >= 0], 1).astype(np.float32)
    return np.concatenate([fwd, bwd, edges], 1)


def pair_masks():
    fwd = np.zeros((P, LOCAL_LEVELS, P), np.float32)
    s, t = np.meshgrid(np.arange(P), np.arange(P), indexing="ij")
    fwd[:, 0] = (s // SCAN_CHUNK == t // SCAN_CHUNK) & (s <= t)
    for level in range(1, LOCAL_LEVELS):
        size = SCAN_CHUNK << level
        fwd[:, level] = (s // size == t // size) & (s % size < size // 2) & (t % size >= size // 2)
    return np.concatenate([fwd, fwd[::-1, :, ::-1]], 1)


MASK_GT, MASK_LE, MASK_LT, MASK_GE, MASK_ALL = range(2 * LOCAL_LEVELS, 2 * LOCAL_LEVELS + 5)



def build_program(nc, a, out, scratch_bias):
    with ExitStack() as ctx:
        queue_program(nc, ctx, a, out, scratch_bias)


def queue_program(nc, ctx, a, out, scratch_bias):
    prog = Program(nc, ctx)
    pe, dve, act, pool = prog.pe, prog.dve, prog.act, prog.pool

    def sb(name, *shape, dtype=F32):
        return ctx.enter_context(nc.sbuf_tensor(name, list(shape), dtype))

    _, SEQ, D = a["x"].shape
    NT = SEQ // P
    KD = D // P
    UNIT = 512
    A_HEADS, A_DIM = 8, 64
    B_HEADS, B_V = 4, 128
    A_W = A_HEADS * A_DIM
    B_W = B_HEADS * B_V
    MAPS = A_HEADS + 2 * B_HEADS
    M_HEADS, M_DIM = 4, D // 4
    D_FF = a["w_gate"].shape[2]
    GW = 512
    GH = 4
    N_EXP = a["w_expert_gu_2"].shape[1]
    D_EXP = a["w_expert_down_2"].shape[2]
    IN2 = a["w_in_2"].shape[2]

    bank = [ctx.enter_context(nc.psum_tensor(f"bank{b}", [P, 512], F32)) for b in range(8)]
    bank_read = {b: None for b in range(8)}

    ident = sb("ident", P, P)
    weights_base = nc.sbuf_base
    weights = sb("weights", P, 2 * KD, UNIT)
    slots = [weights[:, n * KD:(n + 1) * KD, :] for n in range(2)]
    slot_used = {0: None, 1: None}
    hidden_read = {0: None, 1: None}
    prog.carried = [bank_read, slot_used, hidden_read]
    slot_count = [prog.count(f"weights{n}_landed") for n in range(2)]
    x_res = sb("x_res", P, NT, D)
    normed_base = nc.sbuf_base
    normed = sb("normed", P, NT, D)
    act_t_base = nc.sbuf_base
    act_t = sb("act_t", P, KD, SEQ)
    mem_t_base = nc.sbuf_base
    mem_t = sb("mem_t", P, KD, SEQ)
    work_base = nc.sbuf_base
    work = sb("work", P, 27136)
    rows_c = sb("rows_c", P, P)
    cols = sb("cols", P, P)
    small = sb("small", P, 256)
    half_neg = sb("half_neg", P, 16)
    junk = sb("junk", P, D)

    misc = prog.count("misc_loads")
    out_count = prog.count("out_stored")

    def region(at, *shape):
        size = int(np.prod(shape))
        view = work[:, at:at + size]
        names = "abcd"[:len(shape)]
        sizes = {n: x for n, x in zip(names[1:], shape[1:])}
        return view if len(shape) == 1 else view.rearrange(f"p ({' '.join(names)}) -> p {' '.join(names)}", **sizes)

    def rounded(name, base, at, *shape):
        return nc.alloc_sbuf_tensor_at(name, [P, *shape], F32R, offset=base + 4 * at)

    def everything():
        return Both(*[Done(c, c.value, None) for c in prog.engine_count.values()])

    def load(dst, src, *after, engine="scalar", count=None):
        return prog.dma(engine, lambda e, i: e.dma_start(dst, src), count or prog.count(f"load_{len(prog.counts)}"),
                        *after)

    for engine in ("scalar", "vector", "gpsimd", "tensor"):
        prog.put(engine, lambda e, i: e.nop(), by=64)

    stack, at = {}, 0
    clear_rows = dve(lambda e, i: e.memset(rows_c[:, :], 0.0))
    row_loads = []
    for name in ("mix_norm_g", "cross_norm_g", "mem_norm_g", "ffn_norm_g", "moba_out_g", "diff_subln_g",
                 "g_hgrn_out_2", "g_pre_mix_2", "g_pre_ffn_2", "c_2", "c_ctx_2"):
        v = a[name]
        vector = v.rearrange("a b -> (a b)") if len(v.shape) == 2 else v
        n = vector.shape[0] // P
        stack[name] = slice(at, at + n)
        row_loads.append(prog.dma("scalar", lambda e, i, at=at, n=n, vector=vector: e.dma_start(
            rows_c[at:at + n, :], vector.rearrange("(k p) -> k p", p=P)), misc, clear_rows))
        at += n
    rows_landed = row_loads[-1]
    mirror = sb("mirror", P, P)
    mirror_landed = load(mirror[:, :], a["mirror"], engine="sync")
    ident_landed = load(ident[:, :], a["ident"], engine="sync")
    x_landed = load(x_res[:, :, :], a["x"][0].rearrange("(t p) d -> p t d", p=P), engine="sync")
    powers = pool(lambda e, i: e.memset(half_neg[:, :], -0.5))

    tr = pe(lambda e, i: e.transpose(bank[4][:, 0:P], rows_c[:, :], ident[:, :]), rows_landed, ident_landed)
    gains = dve(lambda e, i: e.tensor_copy(cols[:, :], bank[4][:, 0:P]), tr)
    bank_read[4] = gains


    junk_written = {0: None}
    prog.carried.append(junk_written)

    def sum_squares(src, total, scale, *after):
        width = src.shape[-1]
        junk_written[0] = act(lambda e, i: e.activation(junk[:, 0:width], src, ACT.Square, scale=scale,
                                                        accum_out=total), junk_written[0], *after)
        return junk_written[0]

    def rstd_of(name, sums, scale, n, *after):
        mean = pool(lambda e, i: e.tensor_scalar(sums, sums, scale, EPS, ALU.mult, ALU.add), powers, *after)
        return pool(lambda e, i: e.tensor_tensor(sums, sums, half_neg[:, 0:n], ALU.pow), mean)

    def transposed(src, n_blocks, banks, evacuate, *after):
        moments = []
        jobs = [(t, k0) for t in range(NT) for k0 in range(0, n_blocks, 4)]
        for n, (t, k0) in enumerate(jobs):
            b = banks[n % len(banks)]
            width = min(4, n_blocks - k0)

            def run(e, i, t=t, k0=k0, b=b, width=width):
                for k in range(width):
                    last = e.transpose(bank[b][:, k * P:(k + 1) * P], src(t, k0 + k), ident[:, :])
                return last
            waits = [x[t] if isinstance(x, list) else x for x in after]
            done = pe(run, bank_read[b], *waits)
            moments.append(evacuate(b, t, k0, width, done))
            bank_read[b] = moments[-1]
        return moments[-1]

    def halved(high, low, src, *after):
        h = act(lambda e, i: e.activation(high, src, ACT.Copy), *after)
        return dve(lambda e, i: e.tensor_tensor(low, src, high.bitcast(F32), ALU.subtract), h)

    def wide(b, width):
        return bank[b][:, 0:width * P].rearrange("p (k t) -> p k t", t=P)

    def norm_t(src, dst, gain, n_free, *after, shift=None, col=0, later=None):
        scaled = []
        for t in range(NT):
            total = small[:, col + t:col + t + 1]
            sq = sum_squares(src[:, t, :], total, 1.0, *after)
            r = rstd_of("norm", total, 1.0 / D, 1, sq)
            scaled.append(dve(lambda e, i, t=t, total=total: e.tensor_scalar(
                normed[:, t, :], src[:, t, :], total, None, ALU.mult), r, normed_read[0]))

        def evacuate(b, t, k0, width, done):
            out_ap = dst[:, k0:k0 + width, t * P:(t + 1) * P]
            g = gain[:, k0:k0 + width].unsqueeze(2).to_broadcast([P, width, P])
            m = dve(lambda e, i: e.tensor_tensor(out_ap, wide(b, width), g, ALU.mult), done, n_free, gains)
            if shift is None:
                return m
            s = shift[:, k0:k0 + width].unsqueeze(2).to_broadcast([P, width, P])
            return dve(lambda e, i: e.tensor_tensor(out_ap, out_ap, s, ALU.add), m)

        def turn_rows():
            m = transposed(lambda t, k: normed[:, t, k * P:(k + 1) * P], KD, [4, 5, 6, 7], evacuate, scaled)
            normed_read[0] = bank_read[7]
            last[later] = m
            return m
        if later is None:
            return turn_rows()
        pending.append(turn_rows)

    normed_read = [None]

    WHOLE, STEP = 2, 2
    act_low = nc.alloc_sbuf_tensor_at("act_low", [P, KD, SEQ], F32R, offset=act_t_base)
    mem_low = nc.alloc_sbuf_tensor_at("mem_low", [P, KD, SEQ], F32R, offset=mem_t_base)
    weights_low = nc.alloc_sbuf_tensor_at("weights_low", [P, 2 * KD, UNIT], F32R, offset=weights_base)
    high_used = {c: None for c in range(WHOLE, KD, STEP)}
    prog.carried.append(high_used)

    class Split:

        def __init__(self, weights_high, left_high, left_low, free):
            self.weights_high, self.left_high, self.left_low = weights_high, left_high, left_low
            for c in high_used:
                high_used[c] = Both(high_used[c], free)

    def split_left(left, high, low, kd, r0, free, *after):
        ks = slice(r0 + WHOLE, r0 + kd)
        return halved(high[:, ks, :], low[:, ks, :], left[:, ks, :], free, *after)

    def unit_product(s, landed, left, ready, kd, split, evacuate, start=True, stop=True, r0=0, between=None):
        whole = kd if split is None else WHOLE
        split_ready = {}
        if split:
            for c in range(WHOLE, kd, STEP):
                ks = slice(c, c + STEP)
                low = weights_low[:, s * KD + c:s * KD + c + STEP, :]
                split_ready[c] = halved(split.weights_high[:, c - WHOLE:c - WHOLE + STEP, :], low, slots[s][:, ks, :],
                                        landed, high_used[c])
        for t in range(NT):
            b = 2 * s + t

            def run(e, i, t=t, b=b):
                for k in range(whole):
                    mm = e.matmul(bank[b][:, :], left[:, r0 + k, t * P:(t + 1) * P], slots[s][:, k, :],
                                  start=start and k == 0, stop=stop and k == kd - 1)
                return mm
            done = pe(run, landed, bank_read[b], ready[0] if split else ready)
            if not split:
                bank_read[b] = evacuate(t, b, done)
        if split:
            finish_pending()
            if between:
                pending.append(between())
            for c in range(WHOLE, kd, STEP):
                def run(e, i, c=c):
                    for t in range(NT):
                        b, ts = 2 * s + t, slice(t * P, (t + 1) * P)
                        for k in range(c, c + STEP):
                            wh, wl = split.weights_high[:, k - WHOLE, :], weights_low[:, s * KD + k, :]
                            lh, ll = split.left_high[:, r0 + k, ts], split.left_low[:, r0 + k, ts]
                            e.matmul(bank[b][:, :], lh, wh, start=False, stop=False)
                            e.matmul(bank[b][:, :], lh, wl, start=False, stop=False)
                            mm = e.matmul(bank[b][:, :], ll, wh, start=False, stop=stop and k == kd - 1)
                    return mm
                done = high_used[c] = pe(run, split_ready[c], ready[1])
            for t in range(NT):
                bank_read[2 * s + t] = evacuate(t, 2 * s + t, done)
        slot_used[s] = done
        return done

    class Shifted:

        def __init__(self, buffer):
            self.buffer = buffer

        def __getitem__(self, index):
            p, k, n = index
            if isinstance(k, slice):
                return self.buffer[p, k.start - WHOLE:k.stop - WHOLE, n]
            return self.buffer[p, k - WHOLE, n]

    pending = []

    def finish_pending():
        todo, pending[:] = pending[:], []
        for part in todo:
            part()

    def linear(n_units, sources, left, left_ready, evacuate, kd=KD, first=0, side=None, split=None, parity=0):
        def one(j, s):
            for part in range(len(sources(0))):
                def start(e, i, part=part):
                    place, view = sources(j if i is None else 2 * i + (first + s))[part]
                    return e.dma_start(place(slots[s]), view)
                landed = prog.dma("sync", start, slot_count[s], slot_used[s])
            unit_product(s, landed, left, left_ready, kd, split,
                         lambda t, b, done: evacuate(lambda i: j if i is None else 2 * i + (first + s), t, b, done),
                         between=(lambda: side(s)) if side and split else None)
            if side and not split:
                side(s)()

        turns = n_units // 2 if n_units >= 4 or side else 0
        if turns:
            prog.begin(turns)
            one(0, 0)
            one(1, 1)
            finish_pending()
            prog.end()
        for j in range(first + 2 * turns, first + n_units):
            one(j, (j + parity) % 2)
        finish_pending()

    def columns(w, n0=0, width=UNIT):
        view = w.rearrange("(k p) n -> p k n", p=P)
        kd = view.shape[1]
        return lambda j: [(lambda slot: slot[:, 0:kd, 0:width], view[:, :, bass.ds(n0 + j * UNIT, width)])]

    ones = sb("ones", P, P)
    ones_set = pool(lambda e, i: e.memset(ones[:, :], 1.0))
    side_slot = sb("side_slot", P, KD, UNIT)
    ada_acc = sb("ada_acc", P, 3, UNIT)
    silu_c = sb("silu_c", P, 2, KD)
    c_cols = cols[:, stack["c_2"].start:stack["c_ctx_2"].stop].rearrange("p (a k) -> p a k", a=2)
    silu_ready = act(lambda e, i: e.activation(silu_c[:, :, :], c_cols, ACT.Silu), gains)
    bias_row_clear = dve(lambda e, i: e.memset(ada_acc[:, 2, :], 0.0))
    side_read = {"slot": None, "lat": None, "ctx": None, "bias": bias_row_clear}
    prog.carried.append(side_read)
    side_count, side_bias_count = prog.count("ada_landed"), prog.count("ada_bias_landed")
    mod_rows = region(20992, 6, D)
    mod_cols = sb("mod_cols", P, 6, KD)
    ctx_cols = sb("ctx_cols", P, 3, KD)
    ada_v = a["w_ada_2"][0].rearrange("(k p) n -> p k n", p=P)
    ada_bias = a["b_ada_2"]

    def ada_side(first, with_ctx):
        def side(s):
            def j(i):
                return 2 * i + (first + s)
            landed = prog.dma("sync", lambda e, i: e.dma_start(
                side_slot[:, :, :], ada_v[:, :, bass.ds(j(i) * UNIT, UNIT)]), side_count, side_read["slot"])
            bias_landed_ = prog.dma("sync", lambda e, i: e.dma_start(
                ada_acc[0:1, 2, :], ada_bias[:, bass.ds(j(i) * UNIT, UNIT)]), side_bias_count, side_read["bias"])
            sums = {}
            people = [(0, "lat"), (1, "ctx")] if with_ctx else [(0, "lat")]
            for who, name in people:
                add, free = ada_acc[:, 2, :], side_read[name]
                for k in range(KD):
                    summed = dve(lambda e, i, k=k, add=add, who=who: e.scalar_tensor_tensor(
                        ada_acc[:, who, :], side_slot[:, k, :], silu_c[:, who, k:k + 1], add, ALU.mult, ALU.add),
                        landed, bias_landed_, free, silu_ready)
                    add, free = ada_acc[:, who, :], summed
                    if k == 0:
                        side_read["bias"] = summed
                side_read["slot"] = sums[name] = summed

            def add_up():
                for who, name in people:
                    def run(e, i, who=who):
                        if who == 0:
                            e.matmul(bank[6][:, :], ones[:, :], ada_acc[:, 0, :], start=True, stop=True)
                        for c in range(UNIT // P):
                            mm = e.matmul(bank[7][:, 4 * who + c:4 * who + c + 1], ada_acc[:, who, c * P:(c + 1) * P],
                                          ones[:, 0:1], start=True, stop=True)
                        return mm
                    done = pe(run, sums[name], bank_read[6], bank_read[7], ones_set)
                    side_read[name] = done
                    cols_to = (mod_cols, ctx_cols)[who][:, :, :].rearrange("p a k -> p (a k)")
                    if who == 0:
                        bank_read[6] = act(lambda e, i: e.activation(
                            mod_rows[:, :, :].rearrange("p a n -> p (a n)")[:, bass.ds(j(i) * UNIT, UNIT)],
                            bank[6][:, :], ACT.Copy), done)
                    bank_read[7] = act(lambda e, i, who=who, cols_to=cols_to: e.activation(
                        cols_to[:, bass.ds(j(i) * 4, 4)], bank[7][:, 4 * who:4 * who + 4], ACT.Copy), done)
                    last["ada"] = bank_read[7]
            return add_up
        return side
    last = {}

    h_ready = norm_t(x_res, act_t, cols[:, stack["mix_norm_g"]], None, x_landed, col=0)
    proj = region(0, NT, 3072)

    def to_proj(j, t, b, done):
        last["proj"] = act(lambda e, i: e.activation(proj[:, t, bass.ds(j(i) * UNIT, UNIT)], bank[b][:, :], ACT.Copy),
                           done)
        return last["proj"]
    in_split = Split(rounded("in_split_weights_high", work_base, 15872, KD - WHOLE, UNIT),
                     Shifted(rounded("in_split_left_high", work_base, 18944, KD - WHOLE, SEQ)), act_low, None)
    h_ready_both = (h_ready, split_left(act_t, in_split.left_high, act_low, KD, 0, None, h_ready))
    linear(6, columns(a["w_in"][0]), act_t, h_ready_both, to_proj, side=ada_side(0, True), split=in_split)
    proj_ready = last["proj"]
    act_t_read = prog.engine_count["tensor"]
    act_t_free = Done(act_t_read, act_t_read.value, None)

    n_heads = A_HEADS + B_HEADS
    table = sb("table", REL_BUCKETS + 1, n_heads)
    buckets = region(14848, 2 * SEQ)[0:REL_BUCKETS + 1, :]
    bias_rows = region(14848 + 2 * SEQ, 2 * SEQ)[0:n_heads, :]
    bias = region(6144, n_heads, 3 * P)
    table_cleared = dve(lambda e, i: e.memset(table[:, :], NEG_INF))
    table_landed = load(table[0:REL_BUCKETS, :], a["rel_bias_table"], table_cleared)
    buckets_landed = load(buckets[:, :], a["bucket_rows"])
    bias_done = pe(lambda e, i: e.matmul(bank[4][0:n_heads, :], table[:, :], buckets[:, :], start=True, stop=True),
                   bank_read[4], table_landed, buckets_landed)
    bias_out = act(lambda e, i: e.activation(bias_rows[:, :], bank[4][0:n_heads, :], ACT.Copy), bias_done)
    bank_read[4] = bias_out
    bias_stored = load(scratch_bias[:, :], bias_rows[:, :], bias_out)
    spread = prog.count("bias_spread")
    for src_off, width, dst_off in ((0, SEQ, 0), (P, P, SEQ)):
        view = bass.AP(tensor=scratch_bias.tensor, offset=src_off,
                       ap=[[1, P], [2 * SEQ, n_heads], [1, width]])
        bias_landed = prog.dma("scalar", lambda e, i, view=view, dst_off=dst_off, width=width: e.dma_start(
            bias[:, :, dst_off:dst_off + width], view), spread, bias_stored)

    qk_t = region(10752, 2 * KD, SEQ)
    sources = [0, 128, 256, 384, 1536, 1664, 1792, 1920, 512, 640, 768, 896, 2048, 2176, 2304, 2432]
    turn = 0
    for n in range(0, 2 * KD, 2):
        b = 4 + (n // 2) % 4

        def run(e, i, n=n, b=b):
            for m in range(2):
                for t in range(NT):
                    last_ = e.transpose(bank[b][:, (2 * m + t) * P:(2 * m + t + 1) * P],
                                        proj[:, t, sources[n + m]:sources[n + m] + P], ident[:, :])
            return last_
        done = pe(run, bank_read[b], proj_ready)
        dst, srcv = qk_t[:, n:n + 2, :], bank[b][:, :].rearrange("p (k t) -> p k t", k=2)
        f = float(A_DIM) ** -0.5 if n < KD else 1.0
        if (n // 2) % 2:
            bank_read[b] = act(lambda e, i, dst=dst, srcv=srcv, f=f: e.activation(dst, srcv, ACT.Copy, scale=f), done)
            qk_act = bank_read[b]
        else:
            bank_read[b] = dve(lambda e, i, dst=dst, srcv=srcv, f=f: e.tensor_scalar(dst, srcv, f, None, ALU.mult), done)
            qk_dve = bank_read[b]

    scores = region(14848, MAPS, 3 * P)
    neg_max = small[:, 16:16 + 2 * MAPS].rearrange("p (t m) -> p t m", t=2)
    sums = small[:, 64:64 + 2 * MAPS].rearrange("p (t m) -> p t m", t=2)
    span = [(SEQ, SEQ + P), (0, SEQ)]
    exp_done = [None] * MAPS
    for m in range(MAPS):
        b = 4 + m % 4
        lo = 64 * (m % 2)

        head = m if m < A_HEADS else A_HEADS + (m - A_HEADS) // 2

        def run(e, i, m=m, b=b, lo=lo, head=head):
            q, k = qk_t[lo:lo + 64, m // 2, :], qk_t[lo:lo + 64, KD + m // 2, :]
            e.matmul(bank[b][:, 0:3 * P], mirror[:, :], bias[:, head, :], start=True, stop=False, skip_group_check=True)
            e.matmul(bank[b][:, 0:SEQ], q[:, P:SEQ], k, start=False, stop=False, skip_group_check=True)
            return e.matmul(bank[b][:, SEQ:SEQ + P], q[:, 0:P], k[:, 0:P], start=False, stop=True,
                            skip_group_check=True)
        done = pe(run, bank_read[b], qk_act, qk_dve, bias_landed, mirror_landed)
        for t in range(NT):
            maxed = dve(lambda e, i, t=t, m=m, b=b: e.tensor_reduce(
                neg_max[:, t, m:m + 1], bank[b][:, span[t][0]:span[t][1]], AX_X, ALU.max, negate=True), done)
        for t in range(NT):
            exp_done[m] = act(lambda e, i, m=m, t=t, b=b: e.activation(
                scores[:, m, span[t][0]:span[t][1]], bank[b][:, span[t][0]:span[t][1]], ACT.Exp,
                bias=neg_max[:, t, m:m + 1], accum_out=sums[:, t, m:m + 1]), maxed)
        bank_read[b] = exp_done[m]
    inverted = dve(lambda e, i: e.reciprocal(sums, sums), exp_done[-1])

    lam_in = sb("lam_in", P, 4, 64)
    lam = small[:, 128:132]
    lam_landed = load(lam_in[:, :, :], a["diff_lambda"][0].partition_broadcast(P))
    l1 = dve(lambda e, i: e.tensor_tensor(lam_in[:, 0::2, :], lam_in[:, 0::2, :], lam_in[:, 1::2, :], ALU.mult),
             lam_landed)
    l2 = dve(lambda e, i: e.tensor_reduce(lam[:, 0:2], lam_in[:, 0::2, :], AX_X, ALU.add), l1)
    l3 = act(lambda e, i: e.activation(lam[:, 0:2], lam[:, 0:2], ACT.Exp), l2)
    l4 = dve(lambda e, i: e.tensor_tensor(lam[:, 2:3], lam[:, 1:2], lam[:, 0:1], ALU.subtract), l3)
    neg_lam = dve(lambda e, i: e.tensor_scalar(lam[:, 3:4], lam[:, 2:3], -LAMBDA_INIT, None, ALU.add), l4)
    b_second = sums[:, :, A_HEADS + 1::2]
    scaled_second = dve(lambda e, i: e.tensor_scalar(b_second, b_second, lam[:, 3:4], None, ALU.mult),
                        neg_lam, inverted)
    for h in range(B_HEADS):
        m0 = A_HEADS + 2 * h
        for t in range(NT):
            p0, p1 = scores[:, m0, span[t][0]:span[t][1]], scores[:, m0 + 1, span[t][0]:span[t][1]]
            s1 = dve(lambda e, i, p1=p1, m0=m0, t=t: e.tensor_scalar(p1, p1, sums[:, t, m0 + 1:m0 + 2], None, ALU.mult),
                     scaled_second)
            combined = dve(lambda e, i, p0=p0, p1=p1, m0=m0, t=t: e.scalar_tensor_tensor(
                p0, p0, sums[:, t, m0:m0 + 1], p1, ALU.mult, ALU.add), s1)

    p_t = region(6144, n_heads, 3, P)
    bias_used = done
    for h in range(n_heads):
        m = h if h < A_HEADS else A_HEADS + 2 * (h - A_HEADS)
        b = 4 + h % 4

        def run(e, i, m=m, b=b):
            for c in range(3):
                last_ = e.transpose(bank[b][:, c * P:(c + 1) * P], scores[:, m, c * P:(c + 1) * P], ident[:, :])
            return last_
        done = pe(run, bank_read[b], exp_done[m] if h < A_HEADS else combined)
        dst, srcv = p_t[:, h, :, :], wide(b, 3)
        if h % 2:
            bank_read[b] = act(lambda e, i, dst=dst, srcv=srcv: e.activation(dst, srcv, ACT.Copy), done, bias_used)
            pt_act = bank_read[b]
        else:
            bank_read[b] = dve(lambda e, i, dst=dst, srcv=srcv: e.tensor_copy(dst, srcv), done, bias_used)
            pt_dve = bank_read[b]

    mixed = normed
    for t in range(NT):
        for kind, (h0, hn, dv, v0) in enumerate(((0, A_HEADS, A_DIM, 1024), (A_HEADS, B_HEADS, B_V, 2560))):
            b = 2 * kind + t

            def run(e, i, t=t, h0=h0, hn=hn, dv=dv, v0=v0, b=b):
                for h in range(hn):
                    o = bank[b][:, h * dv:(h + 1) * dv]
                    blocks = [(2, 0)] if t == 0 else [(0, 0), (1, 1)]
                    for c, key_tile in blocks:
                        last_ = e.matmul(o, p_t[:, h0 + h, c, :], proj[:, key_tile, v0 + h * dv:v0 + (h + 1) * dv],
                                         start=(c == blocks[0][0]), stop=(c == blocks[-1][0]))
                return last_
            done = pe(run, bank_read[b], pt_act, pt_dve)
            dst = mixed[:, t, kind * A_W:kind * A_W + hn * dv].rearrange("p (h d) -> p h d", h=hn)
            srcv = bank[b][:, :].rearrange("p (h d) -> p h d", h=hn)
            if kind == 0:
                r = sums[:, t, 0:A_HEADS].unsqueeze(2).to_broadcast([P, A_HEADS, A_DIM])
                bank_read[b] = dve(lambda e, i, dst=dst, srcv=srcv, r=r: e.tensor_tensor(dst, srcv, r, ALU.mult),
                                   done, normed_read[0])
            else:
                bank_read[b] = dve(lambda e, i, dst=dst, srcv=srcv: e.tensor_copy(dst, srcv), done, normed_read[0])
        mixed_written = bank_read[2 + t]
        ss = small[:, 136 + 5 * t:141 + 5 * t]
        sq = sum_squares(mixed[:, t, 0:A_W], ss[:, 0:1], A_W ** -0.5, mixed_written)
        for h in range(B_HEADS):
            sq = sum_squares(mixed[:, t, A_W + h * B_V:A_W + (h + 1) * B_V], ss[:, 1 + h:2 + h], B_V ** -0.5,
                             mixed_written)
        r = rstd_of("mixed", ss, 1.0, 5, sq)
        na = dve(lambda e, i, t=t, ss=ss: e.tensor_scalar(mixed[:, t, 0:A_W], mixed[:, t, 0:A_W], ss[:, 0:1],
                                                          None, ALU.mult), r)
        part = mixed[:, t, A_W:D].rearrange("p (h d) -> p h d", h=B_HEADS)
        nb = dve(lambda e, i, part=part, ss=ss: e.tensor_tensor(
            part, part, ss[:, 1:5].unsqueeze(2).to_broadcast([P, B_HEADS, B_V]), ALU.mult), r)
        last["mixed%d" % t] = nb
    mix_gain = small[:, 152:160]
    g1 = dve(lambda e, i: e.tensor_copy(mix_gain[:, 0:4], cols[:, stack["moba_out_g"]]), gains)
    sub = cols[:, stack["diff_subln_g"]]
    g2 = dve(lambda e, i: e.tensor_scalar(mix_gain[:, 4:8], sub.to_broadcast([P, B_HEADS]), 1.0 - LAMBDA_INIT, None,
                                          ALU.mult), gains)

    def gained(dst, gain, free, ready):
        def evacuate(b, t, k0, width, done):
            out_ap = dst[:, k0:k0 + width, t * P:(t + 1) * P]
            if gain is None:
                return act(lambda e, i: e.activation(out_ap, wide(b, width), ACT.Copy), done, free)
            g = gain[:, k0:k0 + width].unsqueeze(2).to_broadcast([P, width, P])
            return dve(lambda e, i: e.tensor_tensor(out_ap, wide(b, width), g, ALU.mult), done, free, ready)
        return evacuate
    mixed_t = transposed(lambda t, k: mixed[:, t, k * P:(k + 1) * P], KD, [4, 5, 6, 7],
                         gained(act_t, mix_gain, act_t_free, g2), [last["mixed0"], last["mixed1"]])
    normed_read[0] = bank_read[7]

    def add_to_x(j, t, b, done):
        def run(e, i):
            part = x_res[:, t, bass.ds(j(i) * UNIT, UNIT)]
            return e.tensor_tensor(part, part, bank[b][:, :], ALU.add)
        last["x"] = dve(run, done)
        return last["x"]

    def pe_so_far():
        c = prog.engine_count["tensor"]
        return Done(c, c.value, None)

    mix_split = Split(rounded("mix_split_weights_high", work_base, 14848, KD - WHOLE, UNIT),
                 Shifted(rounded("mix_split_left_high", work_base, 17920, KD - WHOLE, SEQ)), act_low, everything())
    mixed_t_both = (mixed_t, split_left(act_t, mix_split.left_high, act_low, KD, 0, everything(), mixed_t))
    linear(2, columns(a["w_out"][0]), act_t, mixed_t_both, add_to_x, split=mix_split)
    x1_ready = last["x"]
    act_t_free = pe_so_far()

    mod_gain = sb("mod_gain", P, 3, KD)
    def modulated(which, scale_cols, gain):
        g = dve(lambda e, i: e.scalar_tensor_tensor(mod_gain[:, which, :], scale_cols, 1.0, cols[:, gain],
                                                    ALU.add, ALU.mult), last["ada"])
        return mod_gain[:, which, :], g

    mem_rows = region(0, NT, D)
    mem_landed = load(mem_rows, a["mem"][0].rearrange("(t p) d -> p t d", p=P), act_t_free, engine="sync")
    m_ready = norm_t(mem_rows, mem_t, cols[:, stack["mem_norm_g"]], None, mem_landed, col=2)
    ctx_rows = region(0, NT, D)
    ctx_landed = load(ctx_rows, a["ctx_2"][0].rearrange("(t p) d -> p t d", p=P), m_ready, engine="sync")
    keys = region(2048, NT, D)
    values = region(4096, NT, D)
    queries = region(6144, NT, D)

    def copy_to(dst, key, *after):
        def evacuate(j, t, b, done):
            last[key] = act(lambda e, i: e.activation(dst[:, t, bass.ds(j(i) * UNIT, UNIT)], bank[b][:, :], ACT.Copy),
                            done, *after)
            return last[key]
        return evacuate
    mem_split = Split(rounded("mem_split_weights_high", work_base, 14336, KD - WHOLE, UNIT),
                 Shifted(rounded("mem_split_left_high", work_base, 17408, KD - WHOLE, SEQ)), mem_low, everything())
    m_ready_both = (m_ready, split_left(mem_t, mem_split.left_high, mem_low, KD, 0, everything(), m_ready))
    linear(2, columns(a["w_ck"][0]), mem_t, m_ready_both, copy_to(keys, "keys"), split=mem_split)
    linear(2, columns(a["w_cv"][0]), mem_t, m_ready_both, copy_to(values, "values"), split=mem_split)
    mem_used = pe_so_far()
    c_ready = norm_t(x_res, act_t, cols[:, stack["cross_norm_g"]], act_t_free, x1_ready, col=4)
    query_split = Split(rounded("query_split_weights_high", work_base, 14336, KD - WHOLE, UNIT),
                 Shifted(rounded("query_split_left_high", work_base, 18944, KD - WHOLE, SEQ)), act_low, everything())
    c_ready_both = (c_ready, split_left(act_t, query_split.left_high, act_low, KD, 0, everything(), c_ready))
    linear(2, columns(a["w_cq"][0]), act_t, c_ready_both, copy_to(queries, "queries"), split=query_split)
    act_t_free = pe_so_far()
    kc_t = region(8192, KD, SEQ)
    qc_t = region(10240, KD, SEQ)
    kt_ready = transposed(lambda t, k: keys[:, t, k * P:(k + 1) * P], KD, [4, 5, 6, 7],
                          gained(kc_t, None, mixed_t, None), last["keys"])
    qt_ready = transposed(lambda t, k: queries[:, t, k * P:(k + 1) * P], KD, [4, 5, 6, 7],
                          gained(qc_t, None, mixed_t, None), last["queries"])
    c_probs = region(12288, M_HEADS, NT, SEQ)
    c_max = small[:, 160:168].rearrange("p (h t) -> p h t", h=M_HEADS)
    c_sum = small[:, 168:176].rearrange("p (h t) -> p h t", h=M_HEADS)
    c_scale = float(M_DIM) ** -0.5
    for h in range(M_HEADS):
        def run(e, i, h=h):
            for t in range(NT):
                for k in range(2):
                    last_ = e.matmul(bank[4 + h][:, t * SEQ:(t + 1) * SEQ], qc_t[:, 2 * h + k, t * P:(t + 1) * P],
                                     kc_t[:, 2 * h + k, :], start=(k == 0), stop=(k == 1))
            return last_
        done = pe(run, bank_read[4 + h], kt_ready, qt_ready)
        view = bank[4 + h][:, :].rearrange("p (t m) -> p t m", t=NT)
        mx = dve(lambda e, i, h=h, view=view: e.tensor_reduce(c_max[:, h, :], view, AX_X, ALU.max, negate=True), done)
        mx = dve(lambda e, i, h=h: e.tensor_scalar(c_max[:, h, :], c_max[:, h, :], c_scale, None, ALU.mult), mx)
        for t in range(NT):
            ex = act(lambda e, i, h=h, t=t, view=view: e.activation(
                c_probs[:, h, t, :], view[:, t, :], ACT.Exp, bias=c_max[:, h, t:t + 1], scale=c_scale,
                accum_out=c_sum[:, h, t:t + 1]), mx, mixed_t)
        bank_read[4 + h] = ex
    c_inv = dve(lambda e, i: e.reciprocal(c_sum, c_sum), ex)
    cp_t = region(8192, M_HEADS, 2, SEQ)
    logits_done = done
    for h in range(M_HEADS):
        def run(e, i, h=h):
            for c in range(2):
                for t in range(NT):
                    last_ = e.transpose(bank[4 + h][:, c * SEQ + t * P:c * SEQ + (t + 1) * P],
                                        c_probs[:, h, t, c * P:(c + 1) * P], ident[:, :])
            return last_
        done = pe(run, bank_read[4 + h])
        bank_read[4 + h] = dve(lambda e, i, h=h: e.tensor_copy(
            cp_t[:, h, :, :], bank[4 + h][:, :].rearrange("p (c t) -> p c t", c=2)), done, logits_done)
    cpt_ready = bank_read[7]
    for t in range(NT):
        for pair in range(2):
            b = 2 * pair + t

            def run(e, i, t=t, pair=pair, b=b):
                for g in range(2):
                    h = 2 * pair + g
                    for c in range(2):
                        last_ = e.matmul(bank[b][:, g * M_DIM:(g + 1) * M_DIM], cp_t[:, h, c, t * P:(t + 1) * P],
                                         values[:, c, h * M_DIM:(h + 1) * M_DIM], start=(c == 0), stop=(c == 1))
                return last_
            done = pe(run, bank_read[b], cpt_ready, last["values"])
            dst = normed[:, t, pair * 512:(pair + 1) * 512].rearrange("p (h d) -> p h d", h=2)
            srcv = bank[b][:, :].rearrange("p (h d) -> p h d", h=2)
            r = c_sum[:, 2 * pair:2 * pair + 2, t].unsqueeze(2).to_broadcast([P, 2, M_DIM])
            bank_read[b] = dve(lambda e, i, dst=dst, srcv=srcv, r=r: e.tensor_tensor(dst, srcv, r, ALU.mult),
                               done, c_inv, normed_read[0])
    oc_ready = bank_read[3]
    oc_t = transposed(lambda t, k: normed[:, t, k * P:(k + 1) * P], KD, [4, 5, 6, 7],
                      gained(act_t, None, act_t_free, None), oc_ready)
    normed_read[0] = bank_read[7]
    cross_split = Split(rounded("cross_split_weights_high", work_base, 14336, KD - WHOLE, UNIT),
                 Shifted(rounded("cross_split_left_high", work_base, 17408, KD - WHOLE, SEQ)), act_low, everything())
    oc_t_both = (oc_t, split_left(act_t, cross_split.left_high, act_low, KD, 0, everything(), oc_t))
    ctx_gain, ctx_gain_ready = modulated(0, ctx_cols[:, 1, :], stack["g_pre_mix_2"])
    norm_t(ctx_rows, mem_t, ctx_gain, Both(mem_used, ctx_gain_ready), ctx_landed, shift=ctx_cols[:, 0, :], col=8,
           later="ctx_t")
    linear(2, columns(a["w_co"][0]), act_t, oc_t_both, add_to_x, split=cross_split)
    x2_ready = last["x"]
    act_t_free = pe_so_far()

    f_ready = norm_t(x_res, act_t, cols[:, stack["ffn_norm_g"]], act_t_free, x2_ready, col=6)
    KF = D_FF // P
    HALF = UNIT // 2
    hidden = [region(19968 + s * NT * HALF, NT, HALF) for s in range(2)]
    hidden_t = region(14336, KF, SEQ)
    gate_v = a["w_gate"][0].rearrange("(k p) n -> p k n", p=P)
    up_v = a["w_up"][0].rearrange("(k p) n -> p k n", p=P)

    def gate_up(j):
        return [(lambda slot: slot[:, :, 0:HALF], gate_v[:, :, bass.ds(j * HALF, HALF)]),
                (lambda slot: slot[:, :, HALF:UNIT], up_v[:, :, bass.ds(j * HALF, HALF)])]

    def glu(j, t, b, done):
        s = b // 2
        g = act(lambda e, i: e.activation(hidden[s][:, t, :], bank[b][:, 0:HALF], ACT.Silu), done,
                hidden_read[s])
        u = dve(lambda e, i: e.tensor_tensor(hidden[s][:, t, :], hidden[s][:, t, :], bank[b][:, HALF:UNIT], ALU.mult), g)
        if t == NT - 1:
            tb = 4 + s

            def run(e, i):
                for k in range(2):
                    for tt in range(NT):
                        last_ = e.transpose(bank[tb][:, k * SEQ + tt * P:k * SEQ + (tt + 1) * P],
                                            hidden[s][:, tt, k * P:(k + 1) * P], ident[:, :])
                return last_

            def turn_hidden():
                hidden_read[s] = pe(run, u, bank_read[tb])
                last["hidden"] = bank_read[tb] = act(lambda e, i: e.activation(
                    hidden_t[:, bass.ds(j(i) * 2, 2), :], bank[tb][:, :].rearrange("p (k t) -> p k t", k=2), ACT.Copy),
                    hidden_read[s])
            pending.append(turn_hidden)
        return u

    ffn_split = Split(rounded("ffn_split_weights_high", work_base, 0, KD - WHOLE, UNIT),
                 Shifted(rounded("ffn_split_left_high", work_base, 3072, KD - WHOLE, SEQ)), act_low, everything())
    f_ready_both = (f_ready, split_left(act_t, ffn_split.left_high, act_low, KD, 0, everything(), f_ready))
    linear(6, gate_up, act_t, f_ready_both, glu, side=ada_side(6, False), split=ffn_split)
    linear(D_FF // HALF - 6, gate_up, act_t, f_ready_both, glu, first=6, split=ffn_split)
    ffn_done = last["hidden"]
    act_t_free = pe_so_far()
    ctx_t = last["ctx_t"]
    ctx_split = Split(ffn_split.weights_high, ffn_split.left_high, mem_low, None)
    ctx_t_both = (ctx_t, split_left(mem_t, ctx_split.left_high, mem_low, KD, 0, act_t_free, ctx_t))

    down_v = a["w_down"][0].rearrange("(k p) n -> p k n", p=P)
    down_split = Split(ffn_split.weights_high, rounded("hidden_high", work_base, 6144, KF, SEQ),
                       rounded("hidden_low", work_base, 14336, KF, SEQ), None)

    def add_half(half):
        def evacuate(t, b, done):
            part = x_res[:, t, half * UNIT:(half + 1) * UNIT]
            return dve(lambda e, i: e.tensor_tensor(part, part, bank[b][:, :], ALU.add), done)
        return evacuate
    for r0 in range(0, KF, KD):
        kd = min(KD, KF - r0)
        hidden_split = split_left(hidden_t, down_split.left_high, down_split.left_low, kd, r0, None, ffn_done)
        for half in range(2):
            landed = prog.dma("sync", lambda e, i, kd=kd, r0=r0, half=half: e.dma_start(
                slots[half][:, 0:kd, :], down_v[:, r0:r0 + kd, half * UNIT:(half + 1) * UNIT]), slot_count[half],
                slot_used[half])
            last_chunk = r0 + kd == KF
            unit_product(half, landed, hidden_t, (ffn_done, hidden_split), kd, down_split,
                         add_half(half) if last_chunk else lambda t, b, done: None,
                         start=r0 == 0, stop=last_chunk, r0=r0)
    x3_ready = bank_read[3]

    before_ctx = everything()
    row_g = mod_rows[:, 3, :]
    held = side_slot[:, :, :].rearrange("p k n -> p (k n)")
    masks = held[:, 0:13 * P].rearrange("p (m t) -> p m t", t=P)
    pairs = held[:, 13 * P:21 * P].rearrange("p (m t) -> p m t", t=P)
    states = held[:, 21 * P:29 * P].rearrange("p (d n) -> p d n", d=2)
    lb = region(20992, 2, GW)
    one_lb = region(22016, 2, GW)
    lb_in = normed[:, :, :].rearrange("p t (l n) -> p t l n", l=2)
    xf_ready = lb_ready = lb_diff = masks_landed = pairs_landed = None

    def final_norm():
        nonlocal xf_ready, lb_ready, lb_diff, masks_landed, pairs_landed
        fin_landed = load(row_g[:, :], a["final_norm_g"].partition_broadcast(P))
        for t in range(NT):
            total = small[:, 8 + t:9 + t]
            sq = sum_squares(x_res[:, t, :], total, 1.0, x3_ready)
            r = rstd_of("final", total, 1.0 / D, 1, sq)
            xf_ready = dve(lambda e, i, t=t, total=total: e.scalar_tensor_tensor(
                x_res[:, t, :], x_res[:, t, :], total, row_g[:, :], ALU.mult, ALU.mult), r, fin_landed)
        masks_landed = load(masks, a["decay_masks"], before_ctx)
        pairs_landed = load(pairs, a["pair_masks"], before_ctx)
        lb_landed = load(lb_in, a["lb_logits_2"].partition_broadcast(P), before_ctx)
        lb_diff = dve(lambda e, i: e.tensor_tensor(lb, lb_in[:, :, 0, :], lb_in[:, :, 1, :], ALU.subtract), lb_landed)
        lb_one = act(lambda e, i: e.activation(one_lb, lb, ACT.Sigmoid, scale=-1.0), lb_diff)
        lb_ready = act(lambda e, i: e.activation(lb, lb, ACT.Sigmoid), lb_one)
    pending.append(final_norm)
    pc = region(17920, NT, 3 * GW)
    lf_c = region(11264, NT, 2 * GW)

    def gates(z, lf, d, free):
        def evacuate(j, t, b, done):
            s1 = act(lambda e, i: e.activation(lf(t), bank[b][:, :], ACT.Sigmoid), done, free)
            s2 = act(lambda e, i: e.activation(z(t), bank[b][:, :], ACT.Sigmoid, scale=-1.0), done)
            f1 = dve(lambda e, i: e.tensor_tensor(lf(t), lf(t), one_lb[:, d, :], ALU.mult), s1, lb_ready)
            last["forget"] = dve(lambda e, i: e.tensor_tensor(lf(t), lf(t), lb[:, d, :], ALU.add), f1)
            last["key"] = dve(lambda e, i: e.tensor_tensor(z(t), z(t), one_lb[:, d, :], ALU.mult), s2)
            return s2
        return evacuate
    linear(1, columns(a["w_in_2"][0], n0=3 * GW), mem_t, ctx_t_both, copy_to(pc[:, :, 2 * GW:3 * GW], "pc"),
           split=ctx_split)
    for d in range(2):
        linear(1, columns(a["w_in_2"][0], n0=(1 + d) * GW), mem_t, ctx_t_both,
               gates(lambda t, d=d: pc[:, t, d * GW:(d + 1) * GW], lambda t, d=d: lf_c[:, t, d * GW:(d + 1) * GW], d,
                     ctx_t), split=ctx_split, parity=1 - d)
    lfc_ready = act(lambda e, i: e.activation(lf_c, lf_c, ACT.Ln), last["forget"])
    kc_ready = last["key"]
    gain, gain_ready = modulated(1, mod_cols[:, 1, :], stack["g_pre_mix_2"])
    lat_t = norm_t(x_res, act_t, gain, Both(before_ctx, gain_ready), xf_ready, lb_diff, shift=mod_cols[:, 0, :], col=10)
    kw = normed[:, :, :]
    kw_free = lat_t
    kw_ready = states_ready = None

    def weigh_keys():
        nonlocal kw_ready
        for d in range(2):
            strict = masks[:, (MASK_GT, MASK_LT)[d], :]
            for t in range(NT):
                b = 4 + 2 * d + t

                def run(e, i, d=d, t=t, b=b, strict=strict):
                    own = lf_c[:, t, d * GW:(d + 1) * GW]
                    other = lf_c[:, 1 - t, d * GW:(d + 1) * GW]
                    crossing = t == d
                    mm = e.matmul(bank[b][:, :], strict, own, start=True, stop=not crossing)
                    if crossing:
                        mm = e.matmul(bank[b][:, :], masks[:, MASK_ALL, :], other, start=False, stop=True)
                    return mm
                done = pe(run, bank_read[b], lfc_ready, masks_landed)
                dst = kw[:, t, d * GW:(d + 1) * GW]
                ex = act(lambda e, i, dst=dst, b=b: e.activation(dst, bank[b][:, :], ACT.Exp), done, kw_free)
                bank_read[b] = ex
                kw_ready = dve(lambda e, i, dst=dst, d=d, t=t: e.tensor_tensor(
                    dst, dst, pc[:, t, d * GW:(d + 1) * GW], ALU.mult), ex, kc_ready)
        pending.append(add_states)

    def add_states():
        nonlocal states_ready
        for d in range(2):
            b = 4 + d

            def run(e, i, d=d, b=b):
                for h in range(GH):
                    for t in range(NT):
                        mm = e.matmul(bank[b][:, h * P:(h + 1) * P], kw[:, t, d * GW + h * P:d * GW + (h + 1) * P],
                                      pc[:, t, 2 * GW + h * P:2 * GW + (h + 1) * P], start=(t == 0), stop=(t == NT - 1))
                return mm
            done = pe(run, bank_read[b], kw_ready)
            states_ready = bank_read[b] = act(lambda e, i, d=d, b=b: e.activation(states[:, d, :], bank[b][:, :], ACT.Copy),
                                              done)
            normed_read[0] = done

    p2 = region(0, IN2 // UNIT, NT, UNIT)
    before_lat = before_ctx
    lat_split = Split(rounded("lat_split_weights_high", work_base, 13312, KD - WHOLE, UNIT),
                      Shifted(rounded("lat_split_left_high", work_base, 16384, KD - WHOLE, SEQ)), act_low,
                      before_lat)
    lat_t_both = (lat_t, split_left(act_t, lat_split.left_high, act_low, KD, 0, before_lat, lat_t))
    lf = region(11264, 2, NT, GW)

    def project(unit, n_units, function, parity=0):
        def evacuate(j, t, b, done):
            last["p2"] = act(lambda e, i: e.activation(p2[:, bass.ds(unit + j(i), 1), t, :],
                                                       bank[b][:, :].unsqueeze(1), function), done, before_lat)
            return last["p2"]
        linear(n_units, columns(a["w_in_2"][0], n0=unit * UNIT), act_t, lat_t_both, evacuate, split=lat_split,
               parity=parity)
        return last["p2"]
    gates_out = project(7, 4, ACT.Sigmoid)
    pending.append(weigh_keys)
    cm_ready = project(5, 2, ACT.Gelu_apprx_tanh)
    ctx_done = everything()

    project(3, 1, ACT.Copy)
    g_ready = project(4, 1, ACT.Silu, parity=1)
    q_ready = project(0, 1, ACT.Silu)
    for d in range(2):
        linear(1, columns(a["w_in_2"][0], n0=(1 + d) * UNIT), act_t, lat_t_both,
               gates(lambda t, d=d: p2[:, 1 + d, t, :], lambda t, d=d: lf[:, d, t, :], d, ctx_done),
               split=lat_split, parity=1 - d)
    act_t_free = pe_so_far()

    def gated_rows(which, name, *after):
        landed = load(row_g[:, :], a[name][0].partition_broadcast(P), *after, engine="sync")
        return dve(lambda e, i: e.tensor_tensor(mod_rows[:, which, :], mod_rows[:, which, :], row_g[:, :], ALU.mult),
                   landed)
    post1 = gated_rows(2, "g_post_mix_2", xf_ready)
    post2 = gated_rows(5, "g_post_ffn_2", post1)
    w_router = region(20480, KD, N_EXP)
    router_landed = load(w_router, a["w_router_2"][0].rearrange("(k p) n -> p k n", p=P), ctx_done, engine="sync")
    spare = ada_acc[:, :, :].rearrange("p a n -> p (a n)")
    r_bias, slot_index = spare[:, 1024:1024 + N_EXP], spare[:, 1088:1088 + SEQ]
    earlier = spare[:, 1344:1344 + P]
    bias_r_landed = load(r_bias, a["b_router_2"][0].partition_broadcast(P), ctx_done, engine="sync")
    index_landed = load(slot_index, a["slot_index"].partition_broadcast(P), ctx_done, engine="sync")
    earlier_landed = load(earlier, a["decay_masks"][:, MASK_LT, :], ctx_done, engine="sync")

    lf_ready = act(lambda e, i: e.activation(lf, lf, ACT.Ln), last["forget"])
    k_ready = last["key"]
    q_t = region(13312, GH, SEQ)
    k_t = region(14336, 2, GH, SEQ)
    qt_ready = transposed(lambda t, k: p2[:, 0, t, k * P:(k + 1) * P], GH, [4, 5], gained(q_t, None, before_lat, None),
                          q_ready)
    for d in range(2):
        kt_ready = transposed(lambda t, k, d=d: p2[:, 1 + d, t, k * P:(k + 1) * P], GH, [6, 7],
                              gained(k_t[:, d, :, :], None, before_lat, None), k_ready)
    turned = pe_so_far()
    factors = region(16384, NT, GH, LOCAL_LEVELS, P)
    key0 = region(0, NT, GH, P)
    edge = [region(1024, GH, 4, P),
            act_t[:, :, :].rearrange("p k t -> p (k t)").rearrange("p (h b t) -> p h b t", h=GH, b=4)]
    near_far = mem_t[:, :, :].rearrange("p k t -> p (k t)").rearrange("p (a h t) -> p a h t", a=4, h=GH)
    inside, across = near_far[:, 0:2, :, :], near_far[:, 2:4, :, :]
    inside0 = normed[:, 0, 0:GH * P].rearrange("p (h t) -> p h t", h=GH)
    cleared = dve(lambda e, i: e.memset(inside, 0.0), ctx_done)
    factors_free = ctx_done
    for d in range(2):
        near, far = d, 1 - d
        first_mask, second_mask = ((MASK_GT, MASK_LE), (MASK_LT, MASK_GE))[d]
        for h in range(GH):
            b = 4 + h % 4
            hs = slice(h * P, (h + 1) * P)

            def run(e, i, b=b, hs=hs, d=d, near=near, far=far, first_mask=first_mask, second_mask=second_mask):
                e.matmul(bank[b][:, 0:2 * P], lf[:, d, near, hs],
                         masks[:, first_mask:second_mask + 1, :].rearrange("p m t -> p (m t)"), start=True, stop=True)
                e.matmul(bank[b][:, 2 * P:3 * P], lf[:, d, far, hs], masks[:, second_mask, :], start=True, stop=True)
                e.matmul(bank[b][:, 3 * P:4 * P], lf[:, d, far, hs], masks[:, second_mask, :], start=True, stop=False)
                return e.matmul(bank[b][:, 3 * P:4 * P], lf[:, d, near, hs], masks[:, MASK_ALL, :], start=False,
                                stop=True)
            done = pe(run, bank_read[b], lf_ready)
            ex = bank_read[b] = act(lambda e, i, b=b, h=h, d=d: e.activation(
                edge[d][:, h, :, :], bank[b][:, :].rearrange("p (c t) -> p c t", c=4), ACT.Exp), done, turned)
        for part, (src, tile) in enumerate(((k_t[:, d], near), (q_t, near), (q_t, far), (q_t, far))):
            v = edge[d][:, :, part, :]
            o = src[:, :, tile * P:(tile + 1) * P]
            edge_ready = dve(lambda e, i, v=v, o=o: e.tensor_tensor(v, v, o, ALU.mult), ex, qt_ready, kt_ready)
        for t in range(NT):
            for h in range(GH):
                b = 4 + h % 4
                done = pe(lambda e, i, b=b, h=h, d=d, t=t: e.matmul(
                    bank[b][:, :], lf[:, d, t, h * P:(h + 1) * P],
                    masks[:, LOCAL_LEVELS * d:LOCAL_LEVELS * (d + 1), :].rearrange("p l t -> p (l t)"),
                    start=True, stop=True), bank_read[b], lf_ready)
                act(lambda e, i, b=b, h=h, t=t: e.activation(
                    factors[:, t, h, :, :], bank[b][:, :].rearrange("p (l t) -> p l t", l=LOCAL_LEVELS), ACT.Exp),
                    done, factors_free)
                ex = bank_read[b] = act(lambda e, i, b=b, h=h, t=t: e.activation(
                    key0[:, t, h, :], bank[b][:, 0:P], ACT.Exp, scale=-1.0), done, turned, factors_free)
            qv, kv = q_t[:, :, t * P:(t + 1) * P], k_t[:, d, :, t * P:(t + 1) * P]
            f0 = factors[:, t, :, 0, :]
            dve(lambda e, i, f0=f0, qv=qv: e.tensor_tensor(f0, f0, qv, ALU.mult), ex, qt_ready)
            ready = dve(lambda e, i, kv=kv, t=t: e.tensor_tensor(key0[:, t], key0[:, t], kv, ALU.mult), ex, kt_ready)
            for level in range(1, LOCAL_LEVELS):
                size = SCAN_CHUNK << level
                halves = lambda v, size=size: v.rearrange("p h (n r c) -> p h n r c", r=2, c=size // 2)
                fv = halves(factors[:, t, :, level, :])
                for role, operand in ((1 - d, qv), (d, kv)):
                    x, y = fv[:, :, :, role, :], halves(operand)[:, :, :, role, :]
                    ready = dve(lambda e, i, x=x, y=y: e.tensor_tensor(x, x, y, ALU.mult), ex, qt_ready, kt_ready)
            for level in range(LOCAL_LEVELS):
                b = level

                def run(e, i, b=b, t=t, level=level):
                    for h in range(GH):
                        keys_ = key0[:, t, h, :] if level == 0 else factors[:, t, h, level, :]
                        mm = e.matmul(bank[b][:, h * P:(h + 1) * P], keys_, factors[:, t, h, level, :],
                                      start=True, stop=True)
                    return mm
                done = pe(run, bank_read[b], ready)
                mask = pairs[:, LOCAL_LEVELS * d + level, :].bitcast(I32).unsqueeze(1).to_broadcast([P, GH, P])
                srcv = bank[b][:, :].rearrange("p (h t) -> p h t", h=GH)
                if d == 1 and level == 0:
                    c0 = dve(lambda e, i: e.memset(inside0, 0.0), normed_free if t == 0 else added)
                    c1 = dve(lambda e, i, mask=mask, srcv=srcv: e.copy_predicated(inside0, mask, srcv), done, c0,
                             pairs_landed)
                    bank_read[b] = c1
                    added = dve(lambda e, i, t=t: e.tensor_tensor(inside[:, t], inside[:, t], inside0, ALU.add), c1,
                                inside_ready)
                    inside_ready = added
                else:
                    inside_ready = bank_read[b] = dve(lambda e, i, mask=mask, srcv=srcv, t=t: e.copy_predicated(
                        inside[:, t], mask, srcv), done, cleared, pairs_landed,
                        inside_ready if (d, t, level) != (0, 0, 0) else None)
        factors_free = pe_so_far()
        normed_free = factors_free

        def run(e, i, d=d):
            for h in range(GH):
                mm = e.matmul(bank[4 + d][:, h * P:(h + 1) * P], edge[d][:, h, 0, :], edge[d][:, h, 2, :],
                              start=True, stop=True)
            return mm
        done = pe(run, bank_read[4 + d], edge_ready)
        across_ready = bank_read[4 + d] = act(lambda e, i, d=d: e.activation(
            across[:, d], bank[4 + d][:, :].rearrange("p (h t) -> p h t", h=GH), ACT.Copy), done, ctx_done)
    value = p2[:, 3, :, :]
    rec = normed
    rec_sum = small[:, 180:188].rearrange("p (t h) -> p t h", t=NT)
    for t in range(NT):
        def run(e, i, t=t):
            for h in range(GH):
                o, hs = bank[t][:, h * P:(h + 1) * P], slice(h * P, (h + 1) * P)
                e.matmul(o, inside[:, t, h, :], value[:, t, hs], start=True, stop=False)
                e.matmul(o, across[:, 1 - t, h, :], value[:, 1 - t, hs], start=False, stop=False)
                for d in range(2):
                    mm = e.matmul(o, edge[d][:, h, 1 if d == t else 3, :], states[:, d, hs], start=False, stop=(d == 1))
            return mm
        done = pe(run, bank_read[t], inside_ready, across_ready, states_ready)
        for h in range(GH):
            ss = sum_squares(bank[t][:, h * P:(h + 1) * P], rec_sum[:, t, h:h + 1], P ** -0.5, done)
        r = rstd_of("rec", rec_sum[:, t, :], 1.0, GH, ss)
        m1 = bank_read[t] = dve(lambda e, i, t=t: e.tensor_tensor(
            rec[:, t, 0:GW].rearrange("p (h d) -> p h d", h=GH), bank[t][:, :].rearrange("p (h d) -> p h d", h=GH),
            rec_sum[:, t, :].unsqueeze(2).to_broadcast([P, GH, P]), ALU.mult), r, inside_ready)
        m2 = dve(lambda e, i, t=t: e.tensor_tensor(rec[:, t, 0:GW], rec[:, t, 0:GW], p2[:, 4, t, :], ALU.mult), m1,
                 g_ready)
    rec_t = region(16384, GH, SEQ)
    hgrn = small[:, 188:192]
    hg = dve(lambda e, i: e.tensor_copy(hgrn, cols[:, stack["g_hgrn_out_2"]].to_broadcast([P, GH])), gains)
    rec_t_ready = transposed(lambda t, k: rec[:, t, k * P:(k + 1) * P], GH, [4, 5],
                             gained(rec_t, hgrn, factors_free, hg), m2)

    ln_rows = mod_rows[:, 4, :].rearrange("p (a n) -> p a n", a=2)
    ln_landed = Both(load(ln_rows[:, 0, :], a["cm_ln_g_2"][0].partition_broadcast(P), before_lat),
                     load(ln_rows[:, 1, :], a["cm_ln_b_2"][0].partition_broadcast(P), before_lat))
    b_sp = sb("b_sp", P, 4)
    ws = ada_acc[:, 0, :].rearrange("p (g q) -> p g q", g=4)
    ws_t = ada_acc[:, 1, :].rearrange("p (g q) -> p g q", g=4)
    b_sp_landed = load(b_sp[:, :], a["b_spatial_2"][0])
    ws_landed = load(ws, a["w_spatial_2"][0].rearrange("g p q -> p g q"), before_lat)

    def run(e, i):
        for g in range(4):
            mm = e.transpose(bank[6][:, g * P:(g + 1) * P], ws[:, g, :], ident[:, :])
        return mm
    done = pe(run, bank_read[6], ws_landed)
    ws_ready = bank_read[6] = act(lambda e, i: e.activation(ws_t, bank[6][:, :].rearrange("p (g q) -> p g q", g=4),
                                                            ACT.Copy), done)
    cm_stat = small[:, 192:200]
    for t in range(NT):
        v, u = p2[:, 6, t, :], p2[:, 5, t, :]
        mean, var = cm_stat[:, 2 * t:2 * t + 1], cm_stat[:, 2 * t + 1:2 * t + 2]
        s1 = dve(lambda e, i, v=v, mean=mean: e.tensor_reduce(mean, v, AX_X, ALU.add), cm_ready)
        s2 = dve(lambda e, i, mean=mean: e.tensor_scalar(mean, mean, 1.0 / GW, None, ALU.mult), s1)
        s3 = dve(lambda e, i, v=v, mean=mean: e.tensor_scalar(v, v, mean, None, ALU.subtract), s2)
        s4 = sum_squares(v, var, GW ** -0.5, s3)
        s5 = rstd_of("cm", var, 1.0, 1, s4)
        s6 = dve(lambda e, i, v=v, var=var: e.scalar_tensor_tensor(v, v, var, ln_rows[:, 0, :], ALU.mult, ALU.mult),
                 s5, ln_landed)
        s7 = dve(lambda e, i, v=v: e.tensor_tensor(v, v, ln_rows[:, 1, :], ALU.add), s6)

        def run(e, i, t=t, v=v):
            for g in range(4):
                mm = e.matmul(bank[2 + t][:, g * P:(g + 1) * P], ws_t[:, g, :], v[:, g * P:(g + 1) * P], start=True,
                              stop=True)
            return mm
        done = pe(run, bank_read[2 + t], s7, ws_ready)
        for g in range(4):
            part = u[:, g * P:(g + 1) * P]
            gated = dve(lambda e, i, part=part, g=g, t=t: e.scalar_tensor_tensor(
                part, bank[2 + t][:, g * P:(g + 1) * P], b_sp[:, g:g + 1], part, ALU.add, ALU.mult), done, cm_ready, b_sp_landed)
        bank_read[2 + t] = gated
    gate_t = region(17408, GH, SEQ)
    gate_t_ready = transposed(lambda t, k: p2[:, 5, t, k * P:(k + 1) * P], GH, [6, 7],
                              gained(gate_t, None, factors_free, None), gated)

    merged = region(18432, NT, D)
    wide_slot = [s_[:, :, :].rearrange("p k n -> p (k n)").rearrange("p (k n) -> p k n", k=4) for s_ in slots]
    for s, (name, left, ready) in enumerate((("w_branch_a_2", rec_t, rec_t_ready), ("w_branch_b_2", gate_t, gate_t_ready))):
        landed = prog.dma("sync", lambda e, i, s=s, name=name: e.dma_start(
            wide_slot[s], a[name][0].rearrange("(k p) n -> p k n", p=P)), slot_count[s], slot_used[s])
        for t in range(NT):
            for half in range(2):
                b = 4 * s + 2 * t + half

                def run(e, i, s=s, t=t, half=half, b=b, left=left):
                    for k in range(4):
                        mm = e.matmul(bank[b][:, :], left[:, k, t * P:(t + 1) * P],
                                      wide_slot[s][:, k, half * UNIT:(half + 1) * UNIT], start=(k == 0), stop=(k == 3))
                    return mm
                done = pe(run, landed, bank_read[b], ready)
                dst = merged[:, t, half * UNIT:(half + 1) * UNIT]
                g = p2[:, 7 + 2 * s + half, t, :]
                if s == 0:
                    first_done = bank_read[b] = dve(lambda e, i, dst=dst, b=b, g=g: e.tensor_tensor(
                        dst, bank[b][:, :], g, ALU.mult), done, gates_out, factors_free)
                else:
                    m = bank_read[b] = dve(lambda e, i, b=b, g=g: e.tensor_tensor(g, bank[b][:, :], g, ALU.mult),
                                           done, gates_out)
                    merged_ready = dve(lambda e, i, dst=dst, g=g: e.tensor_tensor(dst, dst, g, ALU.add), m, first_done)
        slot_used[s] = done
    merged_t = transposed(lambda t, k: merged[:, t, k * P:(k + 1) * P], KD, [4, 5, 6, 7],
                          gained(act_t, None, pe_so_far(), None), merged_ready)
    y2 = region(0, NT, D)
    y2_free = pe_so_far()
    merge_over = everything()
    linear(2, columns(a["w_out_2"][0]), act_t, merged_t, copy_to(y2, "y2", y2_free))
    act_t_free = pe_so_far()

    for t in range(NT):
        total = small[:, 200 + t:201 + t]
        sq = sum_squares(y2[:, t, :], total, D ** -0.5, last["y2"])
        r = rstd_of("post", total, 1.0, 1, sq)
        m = dve(lambda e, i, t=t, total=total: e.scalar_tensor_tensor(
            y2[:, t, :], y2[:, t, :], total, mod_rows[:, 2, :], ALU.mult, ALU.mult), r, post1)
        x5_ready = dve(lambda e, i, t=t: e.tensor_tensor(x_res[:, t, :], x_res[:, t, :], y2[:, t, :], ALU.add), m)

    gain, gain_ready = modulated(2, mod_cols[:, 4, :], stack["g_pre_ffn_2"])
    h2_ready = norm_t(x_res, act_t, gain, Both(act_t_free, gain_ready), x5_ready, shift=mod_cols[:, 3, :], col=12)
    route = spare[:, 64:64 + NT * N_EXP].rearrange("p (t e) -> p t e", t=NT)
    lower = sb("lower", P, N_GROUPS, N_GROUPS)
    lo0 = pool(lambda e, i: e.memset(lower[:, :, :], 1.0))
    lower_ready = pool(lambda e, i: e.affine_select(out=lower[:, :, :], in_=lower[:, :, :],
                                                    pattern=[[1, N_GROUPS], [-1, N_GROUPS]], compare_op=ALU.is_gt,
                                                    fill=0.0, base=0, channel_multiplier=0), lo0)
    stage_9 = everything()
    chosen = spare[:, 192:192 + NT * N_EXP].rearrange("p (t e) -> p t e", t=NT)
    GE = N_EXP // N_GROUPS
    for t in range(NT):
        base = t * 600
        score, sel = region(base, N_EXP), region(base + 64, N_EXP)
        top = region(base + 128, N_GROUPS, 8)
        grp, gsel = region(base + 192, N_GROUPS), region(base + 200, N_GROUPS)
        cmp_, eq = region(base + 208, N_GROUPS, N_GROUPS), region(base + 272, N_GROUPS, N_GROUPS)
        best, left_ = region(base + 336, 8), region(base + 344, N_EXP)
        tot = region(base + 408, 2)
        b = t

        def run(e, i, t=t, b=b):
            for k in range(KD):
                mm = e.matmul(bank[b][:, 0:N_EXP], act_t[:, k, t * P:(t + 1) * P], w_router[:, k, :], start=(k == 0),
                              stop=(k == KD - 1))
            return mm
        done = pe(run, bank_read[b], h2_ready, router_landed)
        sc = bank_read[b] = act(lambda e, i, b=b, score=score: e.activation(score, bank[b][:, 0:N_EXP], ACT.Sigmoid), done,
                                stage_9)
        c = dve(lambda e, i, sel=sel, score=score: e.tensor_tensor(sel, score, r_bias, ALU.add), sc, bias_r_landed)
        for g in range(N_GROUPS):
            tp = dve(lambda e, i, g=g, top=top, sel=sel: e.max(top[:, g, :], sel[:, g * GE:(g + 1) * GE]), c)
        c = dve(lambda e, i, grp=grp, top=top: e.tensor_tensor(grp, top[:, :, 0], top[:, :, 1], ALU.add), tp)
        mine = grp.unsqueeze(2).to_broadcast([P, N_GROUPS, N_GROUPS])
        others = grp.unsqueeze(1).to_broadcast([P, N_GROUPS, N_GROUPS])
        c1 = dve(lambda e, i, cmp_=cmp_, mine=mine, others=others: e.tensor_tensor(cmp_, others, mine, ALU.is_gt), c)
        c2 = dve(lambda e, i, eq=eq, mine=mine, others=others: e.tensor_tensor(eq, others, mine, ALU.is_equal), c)
        c2 = dve(lambda e, i, eq=eq: e.tensor_tensor(eq, eq, lower[:, :, :], ALU.mult), c2, lower_ready)
        c1 = dve(lambda e, i, cmp_=cmp_, eq=eq: e.tensor_tensor(cmp_, cmp_, eq, ALU.add), c1, c2)
        c1 = dve(lambda e, i, gsel=gsel, cmp_=cmp_: e.tensor_reduce(gsel, cmp_, AX_X, ALU.add), c1)
        c1 = dve(lambda e, i, gsel=gsel: e.tensor_scalar(gsel, gsel, TOPK_GROUPS - 0.5, None, ALU.is_lt), c1)
        by_group = lambda v: v.rearrange("p (g e) -> p g e", g=N_GROUPS)
        gm = gsel.unsqueeze(2).to_broadcast([P, N_GROUPS, GE])
        c1 = dve(lambda e, i, sel=by_group(sel), gm=gm: e.tensor_tensor(sel, sel, gm, ALU.mult), c1)
        c2 = dve(lambda e, i, grp=grp, gsel=gsel: e.tensor_scalar(grp, gsel, -NEG_INF, NEG_INF, ALU.mult, ALU.add), c1)
        low = grp.unsqueeze(2).to_broadcast([P, N_GROUPS, GE])
        c1 = dve(lambda e, i, sel=by_group(sel), low=low: e.tensor_tensor(sel, sel, low, ALU.add), c2)
        c1 = dve(lambda e, i, best=best, sel=sel: e.max(best, sel), c1)
        c1 = dve(lambda e, i, left_=left_, best=best, sel=sel: e.match_replace(left_, best, sel, 2 * NEG_INF), c1)
        picked = c1 = dve(lambda e, i, left_=left_, sel=sel, t=t: e.tensor_tensor(chosen[:, t, :], left_, sel,
                                                                                 ALU.not_equal), c1)
        c1 = dve(lambda e, i, left_=left_, score=score, t=t: e.tensor_tensor(left_, chosen[:, t, :], score,
                                                                             ALU.mult), c1)
        c1 = dve(lambda e, i, left_=left_, tot=tot: e.tensor_reduce(tot[:, 0:1], left_, AX_X, ALU.add), c1)
        c1 = dve(lambda e, i, tot=tot: e.reciprocal(tot[:, 1:2], tot[:, 0:1]), c1)
        routed = dve(lambda e, i, left_=left_, tot=tot, t=t: e.tensor_scalar(
            route[:, t, :], left_, tot[:, 1:2], ROUTED_SCALE, ALU.mult, ALU.mult), c1)

    shared_gu = region(2048, KD, UNIT)
    shared_down = region(6144, 2, D)
    shared_landed = [load(shared_gu, a["w_shared_gu_2"][0].rearrange("(k p) n -> p k n", p=P), merge_over,
                          engine="sync"),
                     load(shared_down, a["w_shared_down_2"][0].rearrange("(k p) n -> p k n", p=P), merge_over,
                          engine="sync")]
    shared_act = region(24576, NT, D_EXP)
    shared_t = region(25088, 2, SEQ)
    for t in range(NT):
        b = 4 + t

        def run(e, i, t=t, b=b):
            for k in range(KD):
                mm = e.matmul(bank[b][:, :], act_t[:, k, t * P:(t + 1) * P], shared_gu[:, k, :],
                              start=(k == 0), stop=(k == KD - 1))
            return mm
        done = pe(run, shared_landed[0], bank_read[b], h2_ready)
        g = act(lambda e, i, t=t, b=b: e.activation(shared_act[:, t, :], bank[b][:, 0:D_EXP], ACT.Silu), done,
                stage_9)
        u = bank_read[b] = dve(lambda e, i, t=t, b=b: e.tensor_tensor(
            shared_act[:, t, :], shared_act[:, t, :], bank[b][:, D_EXP:2 * D_EXP], ALU.mult), g)

    expert_place = spare[:, 320:320 + NT * N_EXP].rearrange("p (t e) -> p t e", t=NT)
    most = sb("most", 1, N_EXP // 2, dtype=I32)

    def run(e, i):
        e.matmul(bank[2][:, 0:N_EXP], earlier, chosen[:, 0, :], start=True, stop=True)
        e.matmul(bank[2][:, N_EXP:2 * N_EXP], earlier, chosen[:, 1, :], start=True, stop=False)
        e.matmul(bank[2][:, N_EXP:2 * N_EXP], ones[:, :], chosen[:, 0, :], start=False, stop=True)
        e.matmul(bank[2][:, 2 * N_EXP:3 * N_EXP], ones[:, :], chosen[:, 0, :], start=True, stop=False)
        return e.matmul(bank[2][:, 2 * N_EXP:3 * N_EXP], ones[:, :], chosen[:, 1, :], start=False, stop=True)
    counted = pe(run, picked, bank_read[2], earlier_landed)
    p1 = dve(lambda e, i: e.tensor_scalar(expert_place, chosen, -2.0 * SEQ, 2.0 * SEQ, ALU.mult, ALU.add), picked)
    placed = dve(lambda e, i: e.tensor_tensor(expert_place, expert_place, bank[2][:, 0:NT * N_EXP].rearrange(
        "p (t e) -> p t e", t=NT), ALU.add), p1, counted)
    pair_counts = bank[2][0:1, 2 * N_EXP:3 * N_EXP].rearrange("p (n two) -> p n two", two=2)
    most_ready = bank_read[2] = dve(lambda e, i: e.tensor_reduce(most[:, :], pair_counts, AX_X, ALU.max), counted)
    token_rows = rounded("token_rows", normed_base, 0, NT, D)

    rows_low = rounded("rows_low", work_base, 0, NT, D)

    def evacuate(b, t, k0, width, done):
        return halved(token_rows[:, t, k0 * P:(k0 + width) * P], rows_low[:, t, k0 * P:(k0 + width) * P],
                      bank[b][:, 0:width * P], done, h2_ready, routed)
    rows_ready = transposed(lambda t, k: act_t[:, k, t * P:(t + 1) * P], KD, [4, 5, 6, 7], evacuate, h2_ready)

    gu = [region(8192, 2 * KD, UNIT), weights[:, :, :]]
    down = [region(16384, 4, D), side_slot[:, :, :].rearrange("p k n -> p (k n)").rearrange("p (k n) -> p k n", k=4)]
    gathered = [mem_t[:, :, s * P:(s + 1) * P] for s in range(2)]
    exp_hidden = [region(at, D_EXP) for at in (20992, 21248, 25856)]
    exp_hidden_t = [region(21504 + s * D_EXP, D_EXP) for s in range(2)]
    token_of = [rounded(f"token_of{s}", work_base, 23040 + s * SEQ, NT, P) for s in range(2)]
    pick_both = rounded("pick_both", work_base, 22528, NT, 4, SLOTS)
    pick_more = rounded("pick_more", work_base, 25600, NT, 2, SLOTS)
    pick = [pick_both[:, :, 0:2, :], pick_both[:, :, 2:4, :], pick_more[:, :, :, :]]
    slot_weight = [small[:, 208 + n:209 + n] for n in range(3)]
    result = [rounded(f"result{s}", work_base, 23552 + s * D, D) for s in range(2)]
    result_low = [rounded(f"result_low{s}", work_base, 2048 + s * D, D) for s in range(2)]
    gu_count = [prog.count(f"expert_gu{s}_landed") for s in range(2)]
    down_count = [prog.count(f"expert_down{s}_landed") for s in range(2)]
    exp_used, exp_ready = {}, {}
    prog.carried += [exp_used, exp_ready]
    stage_10 = Both(placed, most_ready, stage_9)
    for s in range(2):
        for name in ("gathered", "hidden", "hidden_t", "result", "pick", "weight"):
            exp_used[name, s] = exp_ready[name, s] = stage_10
        exp_ready["gu", s] = exp_ready["down", s] = None
        exp_used["token_of", s] = exp_ready["token_of", s] = stage_10
    for name in ("pick", "hidden", "weight"):
        exp_used[name, 2] = exp_ready[name, 2] = stage_10
    exp_used["gu", 0] = exp_used["down", 0] = merge_over
    exp_used["gu", 1] = slot_used[1]
    exp_used["down", 1] = merge_over

    def load_pair(s, pair):
        gu_v = a["w_expert_gu_2"][0].rearrange("(n two) (k p) c -> n p (two k) c", two=2, p=P)
        down_v = a["w_expert_down_2"][0].rearrange("(n two) (k p) c -> n p (two k) c", two=2, p=P)

        def of(v, i):
            return v[bass.ds(pair(i), 1)].rearrange("n p k c -> p (n k) c")
        exp_ready["gu", s] = prog.dma("sync", lambda e, i: e.dma_start(gu[s], of(gu_v, i)), gu_count[s], exp_used["gu", s])
        exp_ready["down", s] = prog.dma("sync", lambda e, i: e.dma_start(down[s], of(down_v, i)), down_count[s],
                                    exp_used["down", s])

    def select(n, pair, block):
        wanted = slot_index[:, block * SLOTS:(block + 1) * SLOTS].unsqueeze(1).unsqueeze(1).to_broadcast(
            [P, NT, 2, SLOTS])

        def over_slots(v, i):
            return v[:, :, bass.ds(2 * pair(i), 2)].unsqueeze(3).to_broadcast([P, NT, 2, SLOTS])
        exp_ready["pick", n] = dve(lambda e, i: e.tensor_tensor(pick[n][:, :, :, :], wanted, over_slots(expert_place, i), ALU.is_equal),
                               placed, index_landed, exp_used["pick", n])

    def select_both(pair):
        wanted = slot_index[:, 0:SLOTS].unsqueeze(1).unsqueeze(1).to_broadcast([P, NT, 4, SLOTS])
        exp_ready["pick", 0] = exp_ready["pick", 1] = dve(lambda e, i: e.tensor_tensor(
            pick_both[:, :, :, :], wanted,
            expert_place[:, :, bass.ds(2 * pair(i), 4)].unsqueeze(3).to_broadcast([P, NT, 4, SLOTS]), ALU.is_equal),
            placed, index_landed, exp_used["pick", 0], exp_used["pick", 1])

    def gather_both(banks):
        for part in range(4):
            b = banks[part % 2]

            def run(e, i, part=part, b=b):
                for k in range(2):
                    dst = bank[b][:, k * 2 * P:(k + 1) * 2 * P]
                    cs = slice((2 * part + k) * P, (2 * part + k + 1) * P)
                    for t in range(NT):
                        slots_of_t = pick_both[:, t, :, :].rearrange("p e s -> p (e s)")
                        e.matmul(dst, token_rows[:, t, cs], slots_of_t, start=(t == 0), stop=False)
                        mm = e.matmul(dst, rows_low[:, t, cs], slots_of_t, start=False, stop=(t == NT - 1))
                return mm
            done = pe(run, exp_ready["pick", 0], rows_ready, bank_read[b])
            dst = mem_t[:, 2 * part:2 * part + 2, :]
            src = bank[b][:, :].rearrange("p (k n) -> p k n", k=2)
            free = Both(exp_used["gathered", 0], exp_used["gathered", 1])
            if part % 2 == 0:
                by_act = bank_read[b] = act(lambda e, i, dst=dst, src=src: e.activation(dst, src, ACT.Copy), done, free)
            else:
                by_dve = bank_read[b] = dve(lambda e, i, dst=dst, src=src: e.tensor_copy(dst, src), done, free)
        exp_used["pick", 0] = exp_used["pick", 1] = done
        exp_ready["gathered", 0] = exp_ready["gathered", 1] = Both(by_act, by_dve)

    def gather(n, s, banks):
        halves = []
        for part in range(2):
            def run(e, i, part=part):
                for k in range(4):
                    cs = slice((4 * part + k) * P, (4 * part + k + 1) * P)
                    for t in range(NT):
                        chosen_slots = pick[n][:, t, :, :].rearrange("p e s -> p (e s)")
                        e.matmul(bank[banks[part]][:, k * P:(k + 1) * P], token_rows[:, t, cs],
                                 chosen_slots, start=(t == 0), stop=False)
                        mm = e.matmul(bank[banks[part]][:, k * P:(k + 1) * P], rows_low[:, t, cs],
                                      chosen_slots, start=False, stop=(t == NT - 1))
                return mm
            exp_used["pick", n] = pe(run, exp_ready["pick", n], rows_ready, bank_read[banks[part]])
            dst = gathered[s][:, 4 * part:4 * part + 4, :]
            src = bank[banks[part]][:, :].rearrange("p (k n) -> p k n", n=P)
            if part == 0:
                m = act(lambda e, i, dst=dst, src=src: e.activation(dst, src, ACT.Copy), exp_used["pick", n],
                        exp_used["gathered", s])
            else:
                m = dve(lambda e, i, dst=dst, src=src: e.tensor_copy(dst, src), exp_used["pick", n], exp_used["gathered", s])
            bank_read[banks[part]] = m
            halves.append(m)
        exp_ready["gathered", s] = Both(*halves)

    def prepare(m, n, o, pair, b):
        def run(e, i):
            for t in range(NT):
                e.transpose(bank[b][:, D_EXP + t * P:D_EXP + (t + 1) * P],
                            pick[m][:, t, :, :].rearrange("p e s -> p (e s)").bitcast(F32), ident[:, :])
            for t in range(NT):
                mm = e.matmul(bank[b][:, 0:2], pick[m][:, t, :, :].rearrange("p e s -> p (e s)").bitcast(F32),
                              route[:, t, bass.ds(2 * pair(i), 2)], start=(t == 0), stop=(t == NT - 1))
            return mm
        done = exp_used["pick", m] = pe(run, exp_ready["pick", m], routed, bank_read[b])
        parts = []
        for x in range(2):
            own = slice(x * SLOTS, (x + 1) * SLOTS)
            parts.append(dve(lambda e, i, own=own, x=x: e.tensor_copy(slot_weight[n][own, :], bank[b][own, x:x + 1]),
                             done, exp_used["weight", n]))
        exp_ready["weight", n] = Both(*parts)
        exp_ready["token_of", o] = act(lambda e, i: e.activation(
            token_of[o][:, :, :], bank[b][:, D_EXP:2 * D_EXP].rearrange("p (t q) -> p t q", t=NT), ACT.Copy),
            done, exp_used["token_of", o], *parts)
        bank_read[b] = Both(exp_ready["token_of", o], *parts)

    def expert_gate_up(s, n, banks):
        def run(e, i):
            for k in range(KD):
                for x in range(2):
                    mm = e.matmul(bank[banks[0]][x * SLOTS:(x + 1) * SLOTS, :],
                                  gathered[s][:, k, x * SLOTS:(x + 1) * SLOTS], gu[s][:, x * KD + k, :],
                                  start=(k == 0), stop=(k == KD - 1))
            return mm
        done = exp_used["gathered", s] = exp_used["gu", s] = pe(run, exp_ready["gathered", s], exp_ready["gu", s], bank_read[banks[0]])
        g = act(lambda e, i: e.activation(exp_hidden[n], bank[banks[0]][:, 0:D_EXP], ACT.Silu), done, exp_used["hidden", n])
        bank_read[banks[0]] = exp_ready["hidden", n] = exp_used["weight", n] = dve(
            lambda e, i: e.scalar_tensor_tensor(exp_hidden[n], exp_hidden[n], slot_weight[n],
                                                bank[banks[0]][:, D_EXP:2 * D_EXP], ALU.mult, ALU.mult),
            g, exp_ready["weight", n])

    def turn(h, n, b):
        def run(e, i):
            for k in range(2):
                mm = e.transpose(bank[b][:, k * P:(k + 1) * P], exp_hidden[h][:, k * P:(k + 1) * P], ident[:, :])
            return mm
        done = exp_used["hidden", h] = pe(run, exp_ready["hidden", h], bank_read[b])
        exp_ready["hidden_t", n] = bank_read[b] = act(lambda e, i: e.activation(
            exp_hidden_t[n], bank[b][:, 0:D_EXP], ACT.Copy), done, exp_used["hidden_t", n])

    def project_down(s, n, banks):
        halves = []
        for half in range(2):
            def run(e, i, half=half):
                for k in range(2):
                    for x in range(2):
                        mm = e.matmul(bank[banks[half]][x * SLOTS:(x + 1) * SLOTS, :],
                                      exp_hidden_t[n][:, k * P + x * SLOTS:k * P + (x + 1) * SLOTS],
                                      down[s][:, 2 * x + k, half * UNIT:(half + 1) * UNIT], start=(k == 0),
                                      stop=(k == 1))
                return mm
            done = pe(run, exp_ready["hidden_t", n], exp_ready["down", s], bank_read[banks[half]])
            cs = slice(half * UNIT, (half + 1) * UNIT)
            m = halved(result[n][:, cs], result_low[n][:, cs], bank[banks[half]][:, :], done, exp_used["result", n])
            bank_read[banks[half]] = m
            halves.append(m)
        exp_used["down", s] = exp_used["hidden_t", n] = done
        exp_ready["result", n] = Both(*halves)

    def scatter(n, last_one=False):
        def run(e, i):
            for t in range(NT):
                for half in range(2):
                    cs = slice(half * UNIT, (half + 1) * UNIT)
                    e.matmul(bank[2 * t + half][:, :], token_of[n][:, t, :], result[n][:, cs], start=False,
                             stop=False, skip_group_check=True)
                    mm = e.matmul(bank[2 * t + half][:, :], token_of[n][:, t, :], result_low[n][:, cs], start=False,
                                  stop=last_one, skip_group_check=True)
            return mm
        exp_used["token_of", n] = exp_used["result", n] = pe(run, exp_ready["result", n], exp_ready["token_of", n])
        return exp_used["result", n]

    def pair_steps(s, pair, first=False, final=False):
        o = 1 - s
        banks, others = ((6, 7), (4, 5)) if s == 0 else ((4, 5), (6, 7))
        following = lambda i: pair(i) + 1
        if not first and not final:
            load_pair(o, following)
        fuller = lambda i: most[0:1, bass.ds(pair(i), 1)]
        prepare(s, s, s, pair, banks[1])
        expert_gate_up(s, s, banks)
        if not first:
            scatter(o)
        prog.when(fuller, SLOTS)
        prog.when(fuller, 2 * SLOTS)
        for block in range(2, SEQ // SLOTS):
            select(2, pair, block)
            gather(2, s, others)
            prepare(2, 2, o, pair, others[1])
            expert_gate_up(s, 2, others)
            turn(2, o, others[1])
            project_down(s, o, others)
            scatter(o)
        prog.otherwise()
        select(2, pair, 1)
        gather(2, s, others)
        prepare(2, 2, o, pair, others[1])
        expert_gate_up(s, 2, others)
        prog.otherwise()
        if first:
            select(o, following, 0)
        elif not final and s == 1:
            select_both(following)
        turn(s, s, banks[1])
        if first:
            gather(o, o, others)
        elif not final and s == 1:
            gather_both(others)
        project_down(s, s, banks)
        prog.when(fuller, SLOTS, again=True)
        turn(2, o, banks[1])
        project_down(s, o, banks)
        scatter(o)
        prog.otherwise()

    load_pair(0, lambda i: 0)
    load_pair(1, lambda i: 1)

    def run(e, i):
        for k in range(2):
            for t in range(NT):
                mm = e.transpose(bank[6][:, k * SEQ + t * P:k * SEQ + (t + 1) * P],
                                 shared_act[:, t, k * P:(k + 1) * P], ident[:, :])
        return mm
    done = pe(run, u, bank_read[6])
    shared_turned = bank_read[6] = act(lambda e, i: e.activation(
        shared_t, bank[6][:, :].rearrange("p (k t) -> p k t", k=2), ACT.Copy), done, stage_9)
    select(0, lambda i: 0, 0)
    gather(0, 0, (6, 7))

    def run(e, i):
        for t in range(NT):
            for half in range(2):
                for k in range(2):
                    mm = e.matmul(bank[2 * t + half][:, :], shared_t[:, k, t * P:(t + 1) * P],
                                  shared_down[:, k, half * UNIT:(half + 1) * UNIT], start=(k == 0), stop=False,
                                  skip_group_check=True)
        return mm
    shared_done = pe(run, shared_turned, shared_landed[1], bank_read[0], bank_read[1], bank_read[2], bank_read[3])
    for s in range(2):
        exp_used["result", s] = Both(exp_used["result", s], shared_done)

    N_PAIRS = N_EXP // 2
    pair_steps(0, lambda i: 0, first=True)
    prog.begin((N_PAIRS - 2) // 2)
    for step in (1, 2):
        pair_steps(step % 2, lambda i, step=step: 2 * i + step)
    prog.end()
    pair_steps(1, lambda i: N_PAIRS - 1, final=True)
    experts_done = scatter(1, last_one=True)

    totals = small[:, 204:208].rearrange("p (t h) -> p t h", t=NT)
    y3 = normed
    for t in range(NT):
        for half in range(2):
            sq = sum_squares(bank[2 * t + half][:, :], totals[:, t, half:half + 1], D ** -0.5, experts_done)
        s1 = dve(lambda e, i, t=t: e.tensor_tensor(totals[:, t, 0:1], totals[:, t, 0:1], totals[:, t, 1:2], ALU.add), sq)
        r = rstd_of("post2", totals[:, t, 0:1], 1.0, 1, s1)
        for half in range(2):
            cs = slice(half * UNIT, (half + 1) * UNIT)
            m = dve(lambda e, i, t=t, half=half, cs=cs: e.scalar_tensor_tensor(
                y3[:, t, cs], bank[2 * t + half][:, :], totals[:, t, 0:1], mod_rows[:, 5, cs], ALU.mult, ALU.mult), r,
                post2)
            final = dve(lambda e, i, t=t, cs=cs: e.tensor_tensor(y3[:, t, cs], y3[:, t, cs], x_res[:, t, cs], ALU.add), m)
        stored = load(out[0, t * P:(t + 1) * P, :], y3[:, t, :], final, engine="sync", count=out_count)
    prog.put("sync", lambda e, i: e.nop(), [stored])
    with nc.Block() as block:
        prog.emit(block)


def kernel(**inputs):
    import concourse.bacc as bacc
    from concourse.bass_utils import run_bass_kernel_spmd

    arrays = {name: np.ascontiguousarray(value) for name, value in inputs.items()}
    seq = arrays["x"].shape[1]
    arrays["ident"] = np.eye(P, dtype=np.float32)
    arrays["mirror"] = np.eye(P, dtype=np.float32)[::-1].copy()
    arrays["bucket_rows"] = bucket_rows(seq)
    arrays["decay_masks"] = decay_masks()
    arrays["pair_masks"] = pair_masks()
    arrays["slot_index"] = np.arange(seq, dtype=np.float32)
    nc = bacc.Bacc("TRN2", target_bir_lowering=False, num_devices=1)
    views = {name: nc.dram_tensor(f"in_{name}", value.shape, F32, kind="ExternalInput").ap()
             for name, value in arrays.items()}
    out = nc.dram_tensor("out", list(arrays["x"].shape), F32, kind="ExternalOutput").ap()
    scratch_bias = nc.dram_tensor("scratch_bias", [12, 2 * seq], F32, kind="Internal").ap()
    build_program(nc, views, out, scratch_bias)
    results = run_bass_kernel_spmd(nc, [{f"in_{name}": value for name, value in arrays.items()}], core_ids=[0])
    return results.results[0]["out"]
```
